# Optimizing a Trainium2 kernel written in Bass

```python
import jax, jax.numpy as jnp
from jax import lax
import numpy as np

D_MODEL = 1024
BATCH = 1
SEQ = 256
DEPTH = 2
DEC_BATCH = 1
DEC_SEQ = 256
PAST_LEN = 128

EPS = 1e-6
N_MEM = 256
RET_HEADS = 4
RET_DK = 128
RET_DV = 128
RET_QK = RET_HEADS * RET_DK
RET_W = RET_HEADS * RET_DV
RET_CHUNK = 128
ROPE_BASE = 10000.0
GDN_HEADS = 4
GDN_DK = 128
GDN_DV = 128
GDN_QK = GDN_HEADS * GDN_DK
GDN_W = GDN_HEADS * GDN_DV
GDN_CHUNK = 64
CONV_W = 3
MIX_W = RET_W + GDN_W
IN_W = 3 * RET_QK - RET_QK + RET_W + RET_W + 2 * GDN_QK + 2 * GDN_W + 4 * GDN_HEADS
XA_HEADS = 4
XA_DH = D_MODEL // XA_HEADS
PEER_HEADS = 8
PEER_NKEYS = 128
PEER_EXPERTS = PEER_NKEYS * PEER_NKEYS
PEER_DKEY = 256
PEER_DHALF = PEER_DKEY // 2
PEER_TOPK = 16
PEER_TOKEN_BLOCK = 128

kernel_name = 'hybrid_retention_gdn_peer_encoder'

def rms_norm(x, w):
    xf = x.astype(jnp.float32)
    y = xf * lax.rsqrt(jnp.mean(xf * xf, axis=-1, keepdims=True) + EPS)
    return (y * w.astype(jnp.float32)).astype(x.dtype)

def l2_norm(x):
    return x * lax.rsqrt(jnp.sum(x * x, axis=-1, keepdims=True) + EPS)

def rotary(x):
    s, d = x.shape[1], x.shape[-1]
    inv = ROPE_BASE ** (-jnp.arange(0, d, 2, dtype=jnp.float32) / d)
    ang = jnp.arange(s, dtype=jnp.float32)[:, None] * inv[None, :]
    cos = jnp.cos(ang)[None, :, None, :]
    sin = jnp.sin(ang)[None, :, None, :]
    xf = x.astype(jnp.float32)
    x1, x2 = xf[..., 0::2], xf[..., 1::2]
    return jnp.stack([x1 * cos - x2 * sin, x1 * sin + x2 * cos], axis=-1).reshape(x.shape)

def retention_log_decays():
    h = jnp.arange(RET_HEADS, dtype=jnp.float32)
    fwd = jnp.log1p(-jnp.exp2(-5.0 - h))
    bwd = jnp.log1p(-jnp.exp2(-5.5 - h))
    return fwd, bwd

def retention_dir(q, k, v, log_gamma, strict):
    b, h, s, dk = q.shape
    dv = v.shape[-1]
    c = RET_CHUNK
    n = s // c
    qc = q.astype(jnp.float32).reshape(b, h, n, c, dk)
    kc = k.astype(jnp.float32).reshape(b, h, n, c, dk)
    vc = v.astype(jnp.float32).reshape(b, h, n, c, dv)
    pos = jnp.arange(c, dtype=jnp.float32)
    diff = pos[:, None] - pos[None, :]
    mask = diff > 0 if strict else diff >= 0
    lg = log_gamma[:, None, None]
    dmat = jnp.where(mask[None], jnp.exp(lg * jnp.where(mask, diff, 0.0)[None]), 0.0)
    scores = jnp.einsum('bhncd,bhnjd->bhncj', qc, kc) * dmat[None, :, None]
    o_intra = jnp.einsum('bhncj,bhnje->bhnce', scores, vc)
    k_dec = kc * jnp.exp(log_gamma[:, None] * (c - 1.0 - pos)[None])[None, :, None, :, None]
    chunk_kv = jnp.einsum('bhncd,bhnce->nbhde', k_dec, vc)
    chunk_decay = jnp.exp(log_gamma * c)[None, :, None, None]

    def step(state, kv):
        return state * chunk_decay + kv, state

    _, s_prev = lax.scan(step, jnp.zeros((b, h, dk, dv), jnp.float32), chunk_kv)
    q_dec = qc * jnp.exp(log_gamma[:, None] * (pos + 1.0)[None])[None, :, None, :, None]
    o_inter = jnp.einsum('bhncd,nbhde->bhnce', q_dec, s_prev)
    return (o_intra + o_inter).reshape(b, h, s, dv)

def gated_delta_dir(q, k, v, g, beta):
    b, h, s, dk = q.shape
    dv = v.shape[-1]
    c = GDN_CHUNK
    n = s // c
    f32 = jnp.float32
    qc = q.astype(f32).reshape(b, h, n, c, dk)
    kc = k.astype(f32).reshape(b, h, n, c, dk)
    vc = v.astype(f32).reshape(b, h, n, c, dv)
    gc = jnp.cumsum(g.astype(f32).reshape(b, h, n, c), axis=-1)
    bc = beta.astype(f32).reshape(b, h, n, c)
    idx = jnp.arange(c)
    lower = idx[:, None] >= idx[None, :]
    strict_lower = idx[:, None] > idx[None, :]
    decay = jnp.exp(jnp.where(lower, gc[..., :, None] - gc[..., None, :], -jnp.inf))
    kb = kc * bc[..., None]
    vb = vc * bc[..., None]
    m = jnp.where(strict_lower, jnp.einsum('bhnid,bhnjd->bhnij', kb, kc) * decay, 0.0)
    eye = jnp.broadcast_to(jnp.eye(c, dtype=f32), m.shape)
    t = lax.linalg.triangular_solve(eye + m, eye, left_side=True, lower=True)
    u = jnp.matmul(t, vb)
    w = jnp.matmul(t, kb * jnp.exp(gc)[..., None])
    qk = jnp.where(lower, jnp.einsum('bhnid,bhnjd->bhnij', qc, kc) * decay, 0.0)
    q_dec = qc * jnp.exp(gc)[..., None]
    g_last = gc[..., -1]
    k_tail = kc * jnp.exp(g_last[..., None] - gc)[..., None]
    xs = tuple(jnp.moveaxis(a, 2, 0) for a in (u, w, qk, q_dec, k_tail, g_last))

    def step(state, inp):
        u_n, w_n, qk_n, qd_n, kt_n, gl_n = inp
        v_new = u_n - jnp.matmul(w_n, state)
        o = jnp.matmul(qd_n, state) + jnp.matmul(qk_n, v_new)
        state = state * jnp.exp(gl_n)[..., None, None] + jnp.matmul(jnp.swapaxes(kt_n, -1, -2), v_new)
        return state, o

    _, o = lax.scan(step, jnp.zeros((b, h, dk, dv), f32), xs)
    return jnp.moveaxis(o, 0, 2).reshape(b, h, s, dv)

def token_mixer(h, w_in, ret_norm, gdn_conv, gdn_a_log, gdn_dt_bias, gdn_norm, w_out):
    b, s, _ = h.shape
    proj = h @ w_in
    sizes = [RET_QK, RET_QK, RET_W, RET_W, GDN_QK, GDN_QK, GDN_W, GDN_W, 2 * GDN_HEADS, 2 * GDN_HEADS]
    cuts, acc = [], 0
    for sz in sizes[:-1]:
        acc += sz
        cuts.append(acc)
    rq, rk, rv, rg, gq, gk, gv, gz, gb, ga = jnp.split(proj, cuts, axis=-1)

    flip = lambda a: jnp.flip(a, axis=2)
    q = rotary(rq.reshape(b, s, RET_HEADS, RET_DK)).transpose(0, 2, 1, 3)
    k = (rotary(rk.reshape(b, s, RET_HEADS, RET_DK)) * (RET_DK ** -0.5)).transpose(0, 2, 1, 3)
    v = rv.reshape(b, s, RET_HEADS, RET_DV).astype(jnp.float32).transpose(0, 2, 1, 3)
    lg_f, lg_b = retention_log_decays()
    o_r = retention_dir(q, k, v, lg_f, False) + flip(retention_dir(flip(q), flip(k), flip(v), lg_b, True))
    o_r = o_r.transpose(0, 2, 1, 3)
    mu = jnp.mean(o_r, axis=-1, keepdims=True)
    var = jnp.mean(jnp.square(o_r - mu), axis=-1, keepdims=True)
    o_r = ((o_r - mu) * lax.rsqrt(var + EPS)).reshape(b, s, RET_W)
    o_r = o_r * ret_norm.astype(jnp.float32) * jax.nn.silu(rg.astype(jnp.float32))

    qkv = jnp.concatenate([gq, gk, gv], axis=-1)
    pad = CONV_W // 2
    qkv_p = jnp.pad(qkv, ((0, 0), (pad, pad), (0, 0)))
    conv = sum(qkv_p[:, j:j + s] * gdn_conv[j] for j in range(CONV_W))
    conv = jax.nn.silu(conv.astype(jnp.float32))
    cq, ck, cv = jnp.split(conv, [GDN_QK, 2 * GDN_QK], axis=-1)
    q2 = (l2_norm(cq.reshape(b, s, GDN_HEADS, GDN_DK)) * (GDN_DK ** -0.5)).transpose(0, 2, 1, 3)
    k2 = l2_norm(ck.reshape(b, s, GDN_HEADS, GDN_DK)).transpose(0, 2, 1, 3)
    v2 = cv.reshape(b, s, GDN_HEADS, GDN_DV).transpose(0, 2, 1, 3)
    beta = jax.nn.sigmoid(gb.astype(jnp.float32).reshape(b, s, 2, GDN_HEADS))
    g = -jnp.exp(gdn_a_log.astype(jnp.float32)) * jax.nn.softplus(
        ga.astype(jnp.float32).reshape(b, s, 2, GDN_HEADS) + gdn_dt_bias.astype(jnp.float32))
    g_f, g_b = g[:, :, 0].transpose(0, 2, 1), g[:, :, 1].transpose(0, 2, 1)
    be_f, be_b = beta[:, :, 0].transpose(0, 2, 1), beta[:, :, 1].transpose(0, 2, 1)
    o_g = gated_delta_dir(q2, k2, v2, g_f, be_f) + flip(
        gated_delta_dir(flip(q2), flip(k2), flip(v2), flip(g_b), flip(be_b)))
    o_g = o_g.transpose(0, 2, 1, 3)
    o_g = o_g * lax.rsqrt(jnp.mean(o_g * o_g, axis=-1, keepdims=True) + EPS) * gdn_norm.astype(jnp.float32)
    o_g = o_g * jax.nn.silu(gz.astype(jnp.float32).reshape(b, s, GDN_HEADS, GDN_DV))
    o_g = o_g.reshape(b, s, GDN_W)

    merged = jnp.concatenate([o_r, o_g], axis=-1).astype(h.dtype)
    return merged @ w_out

def memory_cross_attention(h, mem_n, w_xq, w_xkv, w_xo):
    b, s, _ = h.shape
    m = mem_n.shape[1]
    q = (h @ w_xq).reshape(b, s, XA_HEADS, XA_DH)
    kv = (mem_n @ w_xkv).reshape(b, m, 2, XA_HEADS, XA_DH)
    k, v = kv[:, :, 0], kv[:, :, 1]
    scores = jnp.einsum('bshd,bmhd->bhsm', q, k).astype(jnp.float32) * (XA_DH ** -0.5)
    p = jax.nn.softmax(scores, axis=-1).astype(v.dtype)
    o = jnp.einsum('bhsm,bmhd->bshd', p, v).reshape(b, s, D_MODEL)
    return o @ w_xo

def peer_ffn(h, peer_wq, peer_keys, peer_u, peer_v):
    b, s, d = h.shape
    t = b * s
    x = h.reshape(t, d)
    q = (x @ peer_wq).reshape(t, PEER_HEADS, 2, PEER_DHALF)
    sc = jnp.einsum('thcd,hcnd->thcn', q, peer_keys).astype(jnp.float32)
    s1, i1 = lax.top_k(sc[:, :, 0], PEER_TOPK)
    s2, i2 = lax.top_k(sc[:, :, 1], PEER_TOPK)
    cand_s = (s1[..., :, None] + s2[..., None, :]).reshape(t, PEER_HEADS, PEER_TOPK * PEER_TOPK)
    cand_i = (i1[..., :, None] * PEER_NKEYS + i2[..., None, :]).reshape(t, PEER_HEADS, PEER_TOPK * PEER_TOPK)
    top_s, top_pos = lax.top_k(cand_s, PEER_TOPK)
    eidx = jnp.take_along_axis(cand_i, top_pos, axis=-1)
    gate = jax.nn.softmax(top_s, axis=-1)
    nb = t // PEER_TOKEN_BLOCK

    def block(args):
        xb, eb, gb = args
        u = peer_u[eb]
        a = jax.nn.gelu(jnp.einsum('thkd,td->thk', u, xb).astype(jnp.float32))
        wgt = (a * gb).astype(xb.dtype)
        return jnp.einsum('thk,thkd->td', wgt, peer_v[eb])

    out = lax.map(block, (x.reshape(nb, PEER_TOKEN_BLOCK, d),
                          eidx.reshape(nb, PEER_TOKEN_BLOCK, PEER_HEADS, PEER_TOPK),
                          gate.reshape(nb, PEER_TOKEN_BLOCK, PEER_HEADS, PEER_TOPK)))
    return out.reshape(b, s, d)

def encoder_trunk(x, mem, norm_mix, w_in, ret_norm, gdn_conv, gdn_a_log, gdn_dt_bias, gdn_norm, w_out,
                  norm_xa, norm_mem, w_xq, w_xkv, w_xo, norm_ffn, peer_wq, peer_keys, peer_u, peer_v,
                  norm_final):
    for l in range(DEPTH):
        hn = rms_norm(x, norm_mix[l])
        x = x + token_mixer(hn, w_in[l], ret_norm[l], gdn_conv[l], gdn_a_log[l], gdn_dt_bias[l],
                            gdn_norm[l], w_out[l]).astype(x.dtype)
        hn = rms_norm(x, norm_xa[l])
        mn = rms_norm(mem, norm_mem[l])
        x = x + memory_cross_attention(hn, mn, w_xq[l], w_xkv[l], w_xo[l]).astype(x.dtype)
        hn = rms_norm(x, norm_ffn[l])
        x = x + peer_ffn(hn, peer_wq[l], peer_keys[l], peer_u[l], peer_v[l]).astype(x.dtype)
    return rms_norm(x, norm_final)

def setup_inputs(seed: int = 0) -> dict:
    key = jax.random.key(seed)
    ks = jax.random.split(key, 26)
    f32 = jnp.float32
    nrm = lambda k, shape, scale: jax.random.normal(k, shape, f32) * scale
    gain = lambda k, shape: 1.0 + 0.02 * jax.random.normal(k, shape, f32)
    a_log = jnp.log(jax.random.uniform(ks[8], (DEPTH, 2, GDN_HEADS), f32, minval=1.0, maxval=16.0))
    dt = jnp.exp(jax.random.uniform(ks[9], (DEPTH, 2, GDN_HEADS), f32,
                                    minval=float(np.log(1e-3)), maxval=float(np.log(1e-1))))
    dt_bias = dt + jnp.log(-jnp.expm1(-dt))
    return {
        'x_prompt': nrm(ks[0], (BATCH, SEQ, D_MODEL), 1.0),
        'x_sample': nrm(ks[1], (DEC_BATCH, DEC_SEQ, D_MODEL), 1.0),
        'mem_prompt': nrm(ks[2], (BATCH, N_MEM, D_MODEL), 1.0),
        'mem_sample': nrm(ks[3], (DEC_BATCH, N_MEM, D_MODEL), 1.0),
        'norm_mix': gain(ks[4], (DEPTH, D_MODEL)),
        'w_in': nrm(ks[5], (DEPTH, D_MODEL, IN_W), D_MODEL ** -0.5),
        'ret_norm': gain(ks[6], (DEPTH, RET_W)),
        'gdn_conv': nrm(ks[7], (DEPTH, CONV_W, 2 * GDN_QK + GDN_W), CONV_W ** -0.5),
        'gdn_a_log': a_log,
        'gdn_dt_bias': dt_bias,
        'gdn_norm': gain(ks[10], (DEPTH, GDN_DV)),
        'w_out': nrm(ks[11], (DEPTH, MIX_W, D_MODEL), MIX_W ** -0.5),
        'norm_xa': gain(ks[12], (DEPTH, D_MODEL)),
        'norm_mem': gain(ks[13], (DEPTH, D_MODEL)),
        'w_xq': nrm(ks[14], (DEPTH, D_MODEL, D_MODEL), D_MODEL ** -0.5),
        'w_xkv': nrm(ks[15], (DEPTH, D_MODEL, 2 * D_MODEL), D_MODEL ** -0.5),
        'w_xo': nrm(ks[16], (DEPTH, D_MODEL, D_MODEL), D_MODEL ** -0.5),
        'norm_ffn': gain(ks[17], (DEPTH, D_MODEL)),
        'peer_wq': nrm(ks[18], (DEPTH, D_MODEL, PEER_HEADS * PEER_DKEY), D_MODEL ** -0.5),
        'peer_keys': nrm(ks[19], (DEPTH, PEER_HEADS, 2, PEER_NKEYS, PEER_DHALF), PEER_DHALF ** -0.5),
        'peer_u': nrm(ks[20], (DEPTH, PEER_EXPERTS, D_MODEL), D_MODEL ** -0.5),
        'peer_v': nrm(ks[21], (DEPTH, PEER_EXPERTS, D_MODEL), PEER_HEADS ** -0.5),
        'norm_final': gain(ks[22], (D_MODEL,)),
    }

def reference(x_prompt, x_sample, mem_prompt, mem_sample, norm_mix, w_in, ret_norm, gdn_conv, gdn_a_log,
              gdn_dt_bias, gdn_norm, w_out, norm_xa, norm_mem, w_xq, w_xkv, w_xo, norm_ffn, peer_wq,
              peer_keys, peer_u, peer_v, norm_final):
    y_prompt = encoder_trunk(x_prompt, mem_prompt, norm_mix, w_in, ret_norm, gdn_conv, gdn_a_log, gdn_dt_bias,
                             gdn_norm, w_out, norm_xa, norm_mem, w_xq, w_xkv, w_xo, norm_ffn, peer_wq,
                             peer_keys, peer_u, peer_v, norm_final)
    y_sample = encoder_trunk(x_sample, mem_sample, norm_mix, w_in, ret_norm, gdn_conv, gdn_a_log, gdn_dt_bias,
                             gdn_norm, w_out, norm_xa, norm_mem, w_xq, w_xkv, w_xo, norm_ffn, peer_wq,
                             peer_keys, peer_u, peer_v, norm_final)
    return (y_prompt, y_sample)


_drawn_inputs = setup_inputs


def setup_inputs(seed=0):
    import zlib

    import numpy as np

    out = dict(_drawn_inputs(seed))
    spreads = {}
    factors = {'norm_xa': 3.734, 'norm_mem': 3.144, 'norm_final': 2.823}
    for name, (base, spread) in spreads.items():
        noise = np.random.default_rng([zlib.crc32(name.encode()), seed]).standard_normal(out[name].shape)
        drawn = base * np.exp(spread * noise) if base else spread * noise
        out[name] = __import__('jax').numpy.asarray(drawn.astype(out[name].dtype))
    for name, factor in factors.items():
        out[name] = (out[name] * factor).astype(out[name].dtype)
    return out
```

```python
from contextlib import ExitStack

import numpy as np

import concourse.bass as bass
from concourse import mybir

ALU = mybir.AluOpType
ACT = mybir.ActivationFunctionType
AX = mybir.AxisListType
F32 = mybir.dt.float32
F32R = mybir.dt.float32r
U32 = mybir.dt.uint32

P = 128
EPS = 1e-6
SEQ = 256
N_SEQ = 2
TILES = N_SEQ * SEQ // P
TOK = N_SEQ * SEQ
D = 1024
KC = D // P
DEPTH = 2
HEADS = 4
LEVELS = 7
XA_DH = 256
PH = 8
TOPK = 16
SLOTS = PH * TOPK
NKEYS = 128
GROUP = 4
CHUNK = 512
NEG = -3.0e38
DIRS = 2


class Stage:

    before = []

    def __init__(self, nc, name):
        self.nc, self.name, self.ctx, self.sems = nc, name, ExitStack(), []

    def __enter__(self):
        return self

    def sb(self, name, shape, dtype=F32):
        return self.ctx.enter_context(self.nc.sbuf_tensor(f"{self.name}_{name}", shape, dtype))

    def sem(self, name):
        s = self.nc.alloc_semaphore(f"{self.name}_{name}")
        self.sems.append(s)
        return s

    def block(self):
        done, Stage.before = Stage.before, self.sems
        self.block_ctx = self.nc.Block()
        b = self.block_ctx.__enter__()

        @b.gpsimd
        def _(pool):
            for s in done:
                pool.sem_clear(s)

        self.done = done
        return b

    def __exit__(self, *e):
        self.block_ctx.__exit__(*e)
        for s in self.done:
            self.nc.release_semaphore(s)
        self.ctx.__exit__(*e)
        return False


class Inner(Stage):

    def __init__(self, nc, outer, name):
        super().__init__(nc, name)
        outer.block_ctx.__exit__(None, None, None)
        for s in outer.done:
            nc.release_semaphore(s)
        self.outer = outer

    def close(self):
        self.outer.block_ctx, self.outer.done = self.block_ctx, self.done
        self.outer.ctx.push(self.ctx.pop_all())


def mm3(pe, out, lhs, rhs, first, last):
    pe.matmul(out, lhs[0], rhs[0], start=first, stop=False)
    pe.matmul(out, lhs[1], rhs[0], start=False, stop=False)
    return pe.matmul(out, lhs[0], rhs[1], start=False, stop=last)


def norm_stage(nc, name, res, src, weight, src_dram=None):
    AH, AL, ident, PS = res.AH, res.AL, res.ident, res.PS
    with Stage(nc, name) as st:
        if src is None:
            src = st.sb("src", [P, TILES, D])
        sq = st.sb("sq", [P, D])
        ms = st.sb("ms", [P, TILES])
        mse = st.sb("mse", [P, TILES])
        rs = st.sb("rs", [P, TILES])
        wcol = st.sb("wcol", [P, KC])
        xn = st.sb("xn", [P, TILES, D])
        w_in_ = st.sem("weight_loaded")
        x_in = st.sem("rows_loaded")
        ssq = st.sem("squares_summed")
        m_ok = st.sem("mean_ready")
        r_ok = st.sem("rsqrt_ready")
        n_ok = st.sem("rows_scaled")
        t_ok = st.sem("chunk_transposed")
        h_ok = st.sem("hi_written")
        l_ok = st.sem("lo_written")
        b = st.block()

        @b.sync
        def _(sp):
            sp.dma_start(wcol[:], weight.rearrange("(k p) -> p k", p=P)).then_inc(w_in_, 16)
            if src_dram is not None:
                for t in range(TILES):
                    sp.dma_start(src[:, t, :], src_dram[t]).then_inc(x_in, 16)

        @b.scalar
        def _(act):
            if src_dram is not None:
                act.wait_ge(x_in, 16 * TILES)
            for t in range(TILES):
                act.activation(sq[:], src[:, t, :], ACT.Square, accum_out=ms[:, t:t + 1]).then_inc(ssq, 1)
                act.wait_ge(ssq, t + 1)
            act.wait_ge(w_in_, 16)
            for k in range(KC):
                act.wait_ge(t_ok, k + 1)
                act.activation(AH[:, k, :], PS[:, k % 4, :], ACT.Copy, scale=wcol[:, k:k + 1]).then_inc(h_ok, 1)

        @b.gpsimd
        def _(pool):
            pool.wait_ge(m_ok, 1)
            pool.tensor_tensor(rs[:], mse[:], res.mhalf[:, 0:TILES], ALU.pow).then_inc(r_ok, 1)

        @b.vector
        def _(dve):
            dve.wait_ge(ssq, TILES)
            dve.tensor_scalar(mse[:], ms[:], 1.0 / D, EPS, ALU.mult, ALU.add).then_inc(m_ok, 1)
            dve.wait_ge(r_ok, 1)
            for t in range(TILES):
                dve.tensor_scalar(xn[:, t, :], src[:, t, :], rs[:, t:t + 1], None, ALU.mult).then_inc(n_ok, 1)
            dve.wait_ge(w_in_, 16)
            for k in range(KC):
                dve.wait_ge(h_ok, k + 1)
                dve.scalar_tensor_tensor(out=AL[:, k, :], in0=PS[:, k % 4, :], scalar=wcol[:, k:k + 1],
                                         in1=AH[:, k, :].bitcast(F32), op0=ALU.mult,
                                         op1=ALU.subtract).then_inc(l_ok, 1)

        @b.tensor
        def _(pe):
            pe.wait_ge(n_ok, TILES)
            for k in range(KC):
                if k >= 4:
                    pe.wait_ge(l_ok, k - 3)
                for t in range(TILES):
                    i = pe.transpose(PS[:, k % 4, t * P:(t + 1) * P], xn[:, t, k * P:(k + 1) * P], ident[:])
                i.then_inc(t_ok, 1)


def project_stage(nc, name, res, w, parts, tail=None):
    AH, AL, PS, X = res.AH, res.AL, res.PS, res.X
    KH = KC // 2
    with Stage(nc, name) as st:
        raw = st.sb("raw", [P, 2, KH, CHUNK])
        hi = st.sb("hi", [P, 2, KH, CHUNK], F32R)
        lo = st.sb("lo", [P, 2, KH, CHUNK], F32R)
        w_in_ = [st.sem(f"half{i}_loaded") for i in range(2)]
        h_ok = st.sem("hi_written")
        l_ok = st.sem("lo_written")
        mm = st.sem("bank_accumulated")
        ev = st.sem("bank_evacuated")
        if tail is not None:
            tw, tcol, tout = tail
            NT = tout.shape[2]
            traw = st.sb("traw", [P, KC, NT])
            thi = st.sb("thi", [P, KC, NT], F32R)
            tlo = st.sb("tlo", [P, KC, NT], F32R)
            t_in = st.sem("tail_loaded")
            th_ok = st.sem("tail_hi")
            tl_ok = st.sem("tail_lo")
            t_mm = st.sem("tail_accumulated")
        b = st.block()
        base = [sum(p[0] for p in parts[:i]) for i in range(len(parts))]
        total = sum(p[0] for p in parts)

        def w_half(job, col0, kh):
            return w.rearrange("(k p) n -> p k n", p=P)[:, kh * KH:(kh + 1) * KH, bass.ds(job * CHUNK + col0, CHUNK)]

        @b.sync
        def _(sp):
            if tail is not None:
                sp.dma_start(traw[:], tw.rearrange("(k p) n -> p k n", p=P)[:, :, tcol:tcol + NT]).then_inc(t_in, 16)
            for (jobs, col0, _, _), j0 in zip(parts, base):
                def load(job, n):
                    for kh in range(2):
                        if n is not None:
                            sp.wait_ge(l_ok, 2 * n + kh - 1)
                        sp.dma_start(raw[:, kh], w_half(job, col0, kh)).then_inc(w_in_[kh], 16)
                first = 0
                if j0 == 0:
                    load(0, None)
                    first = 1
                if jobs > first:
                    with sp.Fori(first, jobs) as job:
                        load(job, job + j0)

        @b.scalar
        def _(act):
            if tail is not None:
                act.wait_ge(t_in, 16)
                act.copy(thi[:], traw[:]).then_inc(th_ok, 1)

            def split(n, again):
                for kh in range(2):
                    act.wait_ge(w_in_[kh], 16 * (n + 1))
                    if again:
                        act.wait_ge(mm, 8 * n - 4 + 4 * kh)
                    act.copy(hi[:, kh], raw[:, kh]).then_inc(h_ok, 1)

            split(0, False)
            with act.Fori(1, total) as n:
                split(n, True)

        @b.vector
        def _(dve):
            if tail is not None:
                dve.wait_ge(th_ok, 1)
                dve.tensor_tensor(tlo[:], traw[:], thi[:].bitcast(F32), ALU.subtract).then_inc(tl_ok, 1)

            def split(c, kh):
                dve.wait_ge(h_ok, c + 1)
                dve.tensor_tensor(lo[:, kh], raw[:, kh], hi[:, kh].bitcast(F32), ALU.subtract).then_inc(l_ok, 1)

            def evacuate(n, job, out):
                for k in range(4):
                    dve.wait_ge(mm, 8 * n + 5 + k)
                    if out is None:
                        dst = X[:, k, bass.ds(job * CHUNK, CHUNK)]
                        dve.tensor_tensor(dst, PS[:, k, :], dst, ALU.add).then_inc(ev, 1)
                    else:
                        dve.tensor_copy(out(job, k), PS[:, k, :]).then_inc(ev, 1)

            split(0, 0)
            split(1, 1)
            for i, ((jobs, _, _, out), j0) in enumerate(zip(parts, base)):
                inner = jobs if i < len(parts) - 1 else jobs - 1
                if inner:
                    with dve.Fori(0, inner) as job:
                        n = job + j0
                        split(2 * n + 2, 0)
                        evacuate(n, job, out)
                        split(2 * n + 3, 1)
                if inner < jobs:
                    evacuate(total - 1, jobs - 1, out)
            if tail is not None:
                dve.wait_ge(t_mm, 1)
                dve.tensor_copy(tout, PS[:, 4, 0:TILES * NT].rearrange("p (t n) -> p t n", n=NT)).then_inc(ev, 1)

        @b.tensor
        def _(pe):
            def product(n, token_major, again):
                for kh in range(2):
                    pe.wait_ge(l_ok, 2 * n + kh + 1)
                    for k in range(4):
                        if again and kh == 0:
                            pe.wait_ge(ev, 4 * n - 3 + k)
                        for i in range(KH):
                            kk = kh * KH + i
                            wide = slice(0, TOK)
                            tile = slice(k * P, (k + 1) * P)
                            if token_major:
                                lhs, rhs = (AH[:, kk, tile], AL[:, kk, tile]), (hi[:, kh, i, :], lo[:, kh, i, :])
                            else:
                                lhs, rhs = (hi[:, kh, i, tile], lo[:, kh, i, tile]), (AH[:, kk, wide], AL[:, kk, wide])
                            ins = mm3(pe, PS[:, k, :], lhs, rhs, kk == 0, kk == KC - 1)
                        ins.then_inc(mm, 1)

            for (jobs, _, token_major, _), j0 in zip(parts, base):
                first = 0
                if j0 == 0:
                    product(0, token_major, False)
                    first = 1
                if jobs > first:
                    with pe.Fori(first, jobs) as job:
                        product(job + j0, token_major, True)
            if tail is not None:
                pe.wait_ge(tl_ok, 1)
                for t in range(TILES):
                    for k in range(KC):
                        s = slice(t * P, (t + 1) * P)
                        ins = mm3(pe, PS[:, 4, t * NT:(t + 1) * NT], (AH[:, k, s], AL[:, k, s]),
                                  (thi[:, k, :], tlo[:, k, :]), k == 0, k == KC - 1)
                ins.then_inc(t_mm, 1)


def merge_stage(nc, name, res, O, center, gain, per_head, SG, sg, k0):
    AH, AL, ident, PS = res.AH, res.AL, res.ident, res.PS
    R = TILES * HEADS
    with Stage(nc, name) as st:
        tmp = st.sb("tmp", [P, R, P])
        cen = st.sb("cen", [P, R, P])
        s1 = st.sb("s1", [P, R])
        s2 = st.sb("s2", [P, R])
        rs = st.sb("rs", [P, R])
        gcol = st.sb("gcol", [P, HEADS])
        prod = st.sb("prod", [P, 2, TOK])
        g_in = st.sem("gain_loaded")
        step = st.sem("vector_step")
        sqd = st.sem("squared")
        sgd = st.sem("gate_ready")
        r_ok = st.sem("rsqrt_ready")
        t_ok = st.sem("head_transposed")
        p_ok = st.sem("product_ready")
        h_ok = st.sem("hi_written")
        l_ok = st.sem("lo_written")
        b = st.block()
        o = O[:].rearrange("p t h e -> p (t h) e")

        def lo(dve, h):
            dve.wait_ge(h_ok, h + 1)
            dve.tensor_tensor(AL[:, k0 + h, :], prod[:, h % 2, :], AH[:, k0 + h, :].bitcast(F32),
                              ALU.subtract).then_inc(l_ok, 1)

        @b.sync
        def _(sp):
            if per_head:
                sp.dma_start(gcol[:], gain.rearrange("(h p) -> p h", p=P)).then_inc(g_in, 16)
            else:
                for h in range(HEADS):
                    sp.dma_start(gcol[:, h:h + 1], gain.rearrange("(p o) -> p o", o=1)).then_inc(g_in, 16)

        @b.scalar
        def _(act):
            act.activation(SG[:, sg], SG[:, sg], ACT.Silu).then_inc(sgd, 1)
            if center:
                act.wait_ge(step, 3)
            act.activation(tmp[:], cen[:] if center else o, ACT.Square).then_inc(sqd, 1)
            for h in range(HEADS):
                act.wait_ge(p_ok, h + 1)
                act.copy(AH[:, k0 + h, :], prod[:, h % 2, :]).then_inc(h_ok, 1)

        @b.gpsimd
        def _(pool):
            pool.wait_ge(step, 5 if center else 2)
            pool.tensor_tensor(rs[:], s2[:], res.mhalf[:, 0:R], ALU.pow).then_inc(r_ok, 1)

        @b.vector
        def _(dve):
            n = 0
            if center:
                dve.tensor_reduce(s1[:], o, AX.X, ALU.add).then_inc(step, 1)
                dve.wait_ge(step, 1)
                dve.tensor_scalar(s1[:], s1[:], 1.0 / P, None, ALU.mult).then_inc(step, 1)
                dve.wait_ge(step, 2)
                dve.tensor_tensor(cen[:], o, s1[:, :, None].broadcast_to([P, R, P]), ALU.subtract).then_inc(step, 1)
                n = 3
            dve.wait_ge(sqd, 1)
            dve.tensor_reduce(s2[:], tmp[:], AX.X, ALU.add).then_inc(step, 1)
            dve.wait_ge(step, n + 1)
            dve.tensor_scalar(s2[:], s2[:], 1.0 / P, EPS, ALU.mult, ALU.add).then_inc(step, 1)
            dve.wait_ge(r_ok, 1)
            dve.wait_ge(sqd, 1)
            dve.tensor_tensor(tmp[:], cen[:] if center else o, rs[:, :, None].broadcast_to([P, R, P]),
                              ALU.mult).then_inc(step, 1)
            dve.wait_ge(g_in, 16 if per_head else 16 * HEADS)
            dve.wait_ge(sgd, 1)
            for h in range(HEADS):
                dve.wait_ge(t_ok, h + 1)
                if h >= 2:
                    dve.wait_ge(h_ok, h - 1)
                    dve.wait_ge(l_ok, h - 1)
                dve.scalar_tensor_tensor(out=prod[:, h % 2, :], in0=PS[:, h, :], scalar=gcol[:, h:h + 1],
                                         in1=SG[:, sg, h, :], op0=ALU.mult, op1=ALU.mult).then_inc(p_ok, 1)
                if h >= 1:
                    lo(dve, h - 1)
            lo(dve, HEADS - 1)

        @b.tensor
        def _(pe):
            pe.wait_ge(step, 6 if center else 3)
            for h in range(HEADS):
                for t in range(TILES):
                    ins = pe.transpose(PS[:, h, t * P:(t + 1) * P], tmp[:, t * HEADS + h, :], ident[:])
                ins.then_inc(t_ok, 1)


def retention_stage(nc, res, tok, Oret):
    ident, PS = res.ident, res.PS
    UNITS = [(s, h) for s in range(N_SEQ) for h in range(HEADS)]
    with Stage(nc, "ret") as st:
        cs = st.sb("cos_sin", [P, 2, 2, 64])
        dec = st.sb("decay", [P, HEADS, 2, SEQ])
        rot = st.sb("rotated", [P, 2, TILES, HEADS, 64, 2])
        ta = st.sb("ta", [P, 2, HEADS, 64])
        tb = st.sb("tb", [P, 2, HEADS, 64])
        tc = st.sb("tc", [P, 2, HEADS, 64])
        td = st.sb("td", [P, 2, HEADS, 64])
        qk = st.sb("qk_T", [P, len(UNITS), 2, SEQ])
        sc = st.sb("scores", [P, len(UNITS), 2, SEQ])
        c_in = st.sem("tables_loaded")
        mul = st.sem("rotary_products")
        rt = st.sem("tile_rotated")
        qt = st.sem("qk_transposed")
        qc = st.sem("qk_copied")
        sm = st.sem("scores_done")
        sd = st.sem("scores_decayed")
        om = st.sem("output_done")
        oc = st.sem("output_copied")
        b = st.block()

        @b.sync
        def _(sp):
            sp.dma_start(cs[:], res.c_rot).then_inc(c_in, 16)
            sp.dma_start(dec[:], res.c_dec).then_inc(c_in, 16)

        @b.vector
        def _(dve):
            dve.wait_ge(c_in, 32)
            for t in range(TILES):
                x = tok[:, 0:2, t, :].rearrange("p j (h d two) -> p j h d two", h=HEADS, two=2)
                shape = [P, 2, HEADS, 64]
                cos = cs[:, t % 2, 0, :][:, None, None, :].broadcast_to(shape)
                sin = cs[:, t % 2, 1, :][:, None, None, :].broadcast_to(shape)
                if t:
                    dve.wait_ge(rt, 2 * t)
                dve.tensor_tensor(ta[:], x[:, :, :, :, 0], cos, ALU.mult).then_inc(mul, 1)
                dve.tensor_tensor(tb[:], x[:, :, :, :, 1], sin, ALU.mult).then_inc(mul, 1)
                dve.tensor_tensor(tc[:], x[:, :, :, :, 0], sin, ALU.mult).then_inc(mul, 1)
                dve.tensor_tensor(td[:], x[:, :, :, :, 1], cos, ALU.mult).then_inc(mul, 1)
                dve.wait_ge(mul, 4 * t + 4)
                dve.tensor_tensor(rot[:, :, t, :, :, 0], ta[:], tb[:], ALU.subtract).then_inc(rt, 1)
                dve.tensor_tensor(rot[:, :, t, :, :, 1], tc[:], td[:], ALU.add).then_inc(rt, 1)
            for u, (s, h) in enumerate(UNITS):
                dve.wait_ge(sm, u + 1)
                dve.tensor_tensor(sc[:, u], PS[:, 2 + u % 2, :].rearrange("p (a i) -> p a i", a=2), dec[:, h],
                                  ALU.mult).then_inc(sd, 1)

        @b.scalar
        def _(act):
            n = len(UNITS)
            for i in range(n + 2):
                if i < n:
                    act.wait_ge(qt, i + 1)
                    act.copy(qk[:, i], PS[:, i % 2, :].rearrange("p (a i) -> p a i", a=2)).then_inc(qc, 1)
                if i >= 2:
                    u = i - 2
                    s, h = UNITS[u]
                    act.wait_ge(om, u + 1)
                    act.copy(Oret[:, 2 * s:2 * s + 2, h, :],
                             PS[:, 4 + u % 4, 0:2 * P].rearrange("p (c e) -> p c e", c=2)).then_inc(oc, 1)

        @b.tensor
        def _(pe):
            def turn(u):
                s, h = UNITS[u]
                if u >= 2:
                    pe.wait_ge(qc, u - 1)
                for j in range(2):
                    for c in range(2):
                        src = rot[:, j, 2 * s + c, h].rearrange("p d two -> p (d two)")
                        i = pe.transpose(PS[:, u % 2, (2 * j + c) * P:(2 * j + c + 1) * P], src, ident[:])
                i.then_inc(qt, 1)

            def scores(u):
                pe.wait_ge(qc, u + 1)
                if u >= 2:
                    pe.wait_ge(sd, u - 1)
                for jc in range(2):
                    i = pe.matmul(PS[:, 2 + u % 2, jc * SEQ:(jc + 1) * SEQ], qk[:, u, 1, jc * P:(jc + 1) * P],
                                  qk[:, u, 0, :], start=True, stop=True)
                i.then_inc(sm, 1)

            def output(u):
                s, h = UNITS[u]
                pe.wait_ge(sd, u + 1)
                if u >= 4:
                    pe.wait_ge(oc, u - 3)
                for ic in range(2):
                    for jc in range(2):
                        i = pe.matmul(PS[:, 4 + u % 4, ic * P:(ic + 1) * P], sc[:, u, jc, ic * P:(ic + 1) * P],
                                      tok[:, 2, 2 * s + jc, h * P:(h + 1) * P], start=jc == 0, stop=jc == 1)
                i.then_inc(om, 1)

            pe.wait_ge(rt, 2 * TILES)
            n = len(UNITS)
            for u in range(n + 2):
                if u < n:
                    turn(u)
                if 1 <= u <= n:
                    scores(u - 1)
                if u >= 2:
                    output(u - 2)


def conv_stage(nc, res, conv_w, raw, small, gates, a_log, dt_bias):
    G = HEADS * DIRS
    with Stage(nc, "conv") as st:
        wc = st.sb("taps", [P, 3, 12])
        y = st.sb("y", [P, 3, TOK])
        al = st.sb("a_log", [P, G])
        dtb = st.sb("dt_bias", [P, G])
        ea = st.sb("ea", [P, G])
        x = st.sb("x", [P, TILES, G])
        ax = st.sb("ax", [P, TILES, G])
        e = st.sb("e", [P, TILES, G])
        u = st.sb("u", [P, TILES, G])
        ln = st.sb("ln", [P, TILES, G])
        c = st.sb("c", [P, TILES, G])
        eb = st.sb("eb", [P, TILES, G])
        w_in_ = st.sem("taps_loaded")
        a_in = st.sem("gate_weights_loaded")
        mid = st.sem("middle_tap")
        side = st.sem("side_taps")
        done = st.sem("silu_done")
        gs = st.sem("gate_vector_step")
        ga = st.sem("gate_scalar_step")
        b = st.block()

        @b.sync
        def _(sp):
            for j in range(3):
                sp.dma_start(wc[:, j, :], conv_w[j].rearrange("(n p) -> p n", p=P)).then_inc(w_in_, 16)
            sp.dma_start(al[:], a_log.partition_broadcast(P)).then_inc(a_in, 16)
            sp.dma_start(dtb[:], dt_bias.partition_broadcast(P)).then_inc(a_in, 16)

        def silu(act, n):
            act.wait_ge(side, 2 * n + 2)
            act.activation(raw[:, n // 4, n % 4, :], y[:, n % 3, :], ACT.Silu).then_inc(done, 1)

        @b.scalar
        def _(act):
            act.wait_ge(a_in, 32)
            act.activation(ea[:], al[:], ACT.Exp).then_inc(ga, 1)
            act.activation(eb[:], small[:, :, 0:G], ACT.Exp, scale=-1.0).then_inc(ga, 1)
            act.wait_ge(gs, 2)
            act.activation(e[:], ax[:], ACT.Exp, scale=-1.0).then_inc(ga, 1)
            act.wait_ge(gs, 4)
            act.activation(ln[:], u[:], ACT.Ln).then_inc(ga, 1)
            act.wait_ge(w_in_, 48)
            for n in range(12):
                if n >= 3:
                    act.wait_ge(done, n - 2)
                act.activation(y[:, n % 3, :], raw[:, n // 4, n % 4, :], ACT.Copy, scale=wc[:, 1, n:n + 1]).then_inc(mid, 1)
                if n >= 1:
                    silu(act, n - 1)
            silu(act, 11)

        @b.vector
        def _(dve):
            step = 0

            def link(ins):
                nonlocal step
                step += 1
                ins.then_inc(gs, 1)
                dve.wait_ge(gs, step)

            dve.wait_ge(a_in, 32)
            link(dve.tensor_tensor(x[:], small[:, :, G:2 * G], dtb[:, None, :].broadcast_to([P, TILES, G]), ALU.add))
            link(dve.scalar_tensor_tensor(out=ax[:], in0=x[:], scalar=-1.0, in1=x[:], op0=ALU.mult, op1=ALU.max))
            dve.wait_ge(ga, 3)
            link(dve.tensor_scalar(x[:], x[:], 0.0, None, ALU.max))
            link(dve.tensor_scalar(u[:], e[:], 1.0, None, ALU.add))
            link(dve.tensor_scalar(c[:], u[:], -1.0, None, ALU.add))
            link(dve.tensor_tensor(c[:], e[:], c[:], ALU.subtract))
            dve.wait_ge(ga, 4)
            link(dve.reciprocal(u[:], u[:]))
            link(dve.tensor_tensor(c[:], c[:], u[:], ALU.mult))
            link(dve.tensor_tensor(c[:], c[:], ln[:], ALU.add))
            link(dve.tensor_tensor(c[:], c[:], x[:], ALU.add))
            link(dve.tensor_tensor(c[:], c[:], ea[:, None, :].broadcast_to([P, TILES, G]), ALU.mult))
            link(dve.tensor_scalar(gates[:, 1], c[:], -1.0, None, ALU.mult))
            link(dve.tensor_scalar(eb[:], eb[:], 1.0, None, ALU.add))
            link(dve.reciprocal(gates[:, 0], eb[:]))
            dve.wait_ge(w_in_, 48)
            for n in range(12):
                dve.wait_ge(mid, n + 1)
                yy = y[:, n % 3, :].rearrange("p (s t) -> p s t", s=N_SEQ)
                xx = raw[:, n // 4, n % 4, :].rearrange("p (s t) -> p s t", s=N_SEQ)
                dve.scalar_tensor_tensor(out=yy[:, :, 1:], in0=xx[:, :, :-1], scalar=wc[:, 0, n:n + 1],
                                         in1=yy[:, :, 1:], op0=ALU.mult, op1=ALU.add).then_inc(side, 1)
                dve.wait_ge(side, 2 * n + 1)
                dve.scalar_tensor_tensor(out=yy[:, :, :-1], in0=xx[:, :, 1:], scalar=wc[:, 2, n:n + 1],
                                         in1=yy[:, :, :-1], op0=ALU.mult, op1=ALU.add).then_inc(side, 1)


def unit_stage(nc, res, raw, tokm):
    ident, PS = res.ident, res.PS
    N = 2 * HEADS
    with Stage(nc, "unit") as st:
        sq = st.sb("sq", [P, TILES, N, P])
        ss = st.sb("ss", [P, TILES, N])
        rs = st.sb("rs", [P, TILES, N])
        t_ok = st.sem("tile_transposed")
        c_ok = st.sem("tile_copied")
        sqd = st.sem("squared")
        step = st.sem("vector_step")
        r_ok = st.sem("rsqrt_ready")
        b_ok = st.sem("head_transposed_back")
        bc = st.sem("head_copied")
        b = st.block()

        @b.tensor
        def _(pe):
            for t in range(TILES):
                for j in range(3):
                    n = 3 * t + j
                    if n >= 6:
                        pe.wait_ge(c_ok, n - 5)
                    for h in range(HEADS):
                        i = pe.transpose(PS[:, n % 6, h * P:(h + 1) * P], raw[:, j, h, t * P:(t + 1) * P], ident[:])
                    i.then_inc(t_ok, 1)
            pe.wait_ge(step, 4)
            for n in range(N):
                if n >= 2:
                    pe.wait_ge(bc, n - 1)
                for t in range(TILES):
                    i = pe.transpose(PS[:, 6 + n % 2, t * P:(t + 1) * P],
                                     tokm[:, t, n // HEADS, (n % HEADS) * P:(n % HEADS + 1) * P], ident[:])
                i.then_inc(b_ok, 1)

        @b.scalar
        def _(act):
            for n in range(3 * TILES):
                act.wait_ge(t_ok, n + 1)
                act.copy(tokm[:, n // 3, n % 3, :], PS[:, n % 6, :]).then_inc(c_ok, 1)
            act.wait_ge(c_ok, 3 * TILES)
            for t in range(TILES):
                act.activation(sq[:, t], tokm[:, t, 0:2].rearrange("p j (h e) -> p (j h) e", e=P),
                               ACT.Square).then_inc(sqd, 1)
            for n in range(N):
                act.wait_ge(b_ok, n + 1)
                act.copy(raw[:, n // HEADS, n % HEADS, :], PS[:, 6 + n % 2, :]).then_inc(bc, 1)

        @b.gpsimd
        def _(pool):
            pool.wait_ge(step, 2)
            pool.tensor_tensor(rs[:], ss[:], res.mhalf[:, 0:TILES * N].rearrange("p (t n) -> p t n", n=N),
                               ALU.pow).then_inc(r_ok, 1)

        @b.vector
        def _(dve):
            dve.wait_ge(sqd, TILES)
            dve.tensor_reduce(ss[:], sq[:], AX.X, ALU.add).then_inc(step, 1)
            dve.wait_ge(step, 1)
            dve.tensor_scalar(ss[:], ss[:], EPS, None, ALU.add).then_inc(step, 1)
            dve.wait_ge(r_ok, 1)
            dve.tensor_scalar(rs[:, :, 0:HEADS], rs[:, :, 0:HEADS], P ** -0.5, None, ALU.mult).then_inc(step, 1)
            dve.wait_ge(step, 3)
            v = tokm[:, :, 0:2, :].rearrange("p t j (h e) -> p t (j h) e", e=P)
            for t in range(TILES):
                i = dve.tensor_tensor(v[:, t], v[:, t], rs[:, t, :, None].broadcast_to([P, N, P]), ALU.mult)
            i.then_inc(step, 1)


def first_tile(s, d):
    return 2 * s + d


def second_tile(s, d):
    return 2 * s + 1 - d


def delta_stage(nc, res, raw, tokm, gates, Ogdn):
    ident, PS = res.ident, res.PS
    NB = TILES * DIRS
    H4 = [P, HEADS, P]
    qn, kn = raw[:, 0], raw[:, 1]

    def heads(ap):
        return ap.rearrange("p (h i) -> p h i", h=HEADS)

    def bank(n):
        return heads(PS[:, n, :])

    with Stage(nc, "dlta") as st:
        tri = st.sb("tri", [P, DIRS, P])
        lm = st.sb("level_masks", [P, DIRS, LEVELS, P])
        lmc = st.sb("level_mask", [P, DIRS, P])
        T = st.sb("T", [P, NB] + H4[1:])
        TT = st.sb("TT", [P, NB] + H4[1:])
        MT = st.sb("MT", [P, NB] + H4[1:])
        QK = st.sb("QK", [P, NB] + H4[1:])
        qd = st.sb("q_decayed", [P, 4] + H4[1:])
        ring = st.sb("ring", [P, 2] + H4[1:])
        gcc = st.sb("g_cumulative", [P, DIRS, TILES, HEADS])
        glast = st.sb("g_last", [P, TILES, DIRS, HEADS])
        kt = st.sb("tail_factor", [P, DIRS, TILES, HEADS])
        kg = st.sb("key_factor", [P, DIRS, TILES, HEADS])
        eg = st.sb("exp_g", [P, DIRS, TILES, HEADS])
        c_in = st.sem("masks_loaded")
        gm = st.sem("gate_sums_done")
        gcp = st.sem("gate_sums_copied")
        gst = st.sem("gate_factor_step")
        rows = st.sem("rows_ready")
        kk = st.sem("products_ready")
        df = st.sem("differences_ready")
        ex = st.sem("decay_ready")
        xg = st.sem("row_exponential_ready")
        br = st.sem("beta_row_copied")
        em = st.sem("decay_masked")
        ebm = st.sem("decay_times_beta")
        fin = st.sem("batch_matrices_ready")
        b = st.block()

        @b.sync
        def _(sp):
            sp.dma_start(tri[:], res.c_tri).then_inc(c_in, 16)
            sp.dma_start(lm[:], res.c_lm).then_inc(c_in, 16)

        def second(n):
            t, d = n // DIRS, n % DIRS
            return t == second_tile(t // 2, d)

        seconds = [n for n in range(NB) if second(n)]

        @b.tensor
        def _(pe):
            pe.wait_ge(c_in, 32)
            for d in range(DIRS):
                pe.matmul(PS[:, 0, d * 16:(d + 1) * 16], tri[:, d, :],
                          gates[:, 1].rearrange("p t (d h) -> p t d h", d=DIRS)[:, :, d, :], start=True, stop=True)
            pe.matmul(PS[:, 0, 32:64], res.ones[:], gates[:, 1], start=True, stop=True).then_inc(gm, 1)
            for n in range(NB):
                t, d = n // DIRS, n % DIRS
                if n >= 1:
                    pe.wait_ge(fin, n)
                for h in range(HEADS):
                    g = gates[:, 1, t, d * HEADS + h:d * HEADS + h + 1].broadcast_to([P, P])
                    be = gates[:, 0, t, d * HEADS + h:d * HEADS + h + 1].broadcast_to([P, P])
                    pe.matmul(PS[:, 1, h * P:(h + 1) * P], g, tri[:, d, :], start=True, stop=True)
                    i = pe.matmul(PS[:, 2, h * P:(h + 1) * P], be, ident[:], start=True, stop=True)
                i.then_inc(rows, 1)
                for h in range(HEADS):
                    s = slice(t * P, (t + 1) * P)
                    pe.matmul(PS[:, 3, h * P:(h + 1) * P], kn[:, h, s], kn[:, h, s], start=True, stop=True)
                    i = pe.matmul(PS[:, 4, h * P:(h + 1) * P], kn[:, h, s], qn[:, h, s], start=True, stop=True)
                i.then_inc(kk, 1)

        @b.scalar
        def _(act):
            act.wait_ge(gcp, 2)
            act.activation(eg[:], gcc[:], ACT.Exp).then_inc(gst, 1)
            act.wait_ge(gst, 2)
            act.activation(kt[:], kt[:], ACT.Exp).then_inc(gst, 1)
            for n in range(NB):
                act.wait_ge(rows, n + 1)
                if second(n):
                    if n > seconds[0]:
                        act.wait_ge(fin, n)
                    act.wait_ge(df, 2 * n + 1)
                    act.activation(ring[:, 0], bank(1), ACT.Exp).then_inc(xg, 1)
                act.copy(TT[:, n], bank(2)).then_inc(br, 1)
                act.wait_ge(df, 2 * n + 2)
                act.activation(T[:, n], T[:, n], ACT.Exp).then_inc(ex, 1)

        @b.gpsimd
        def _(pool):
            pool.wait_ge(c_in, 32)
            for n in range(NB):
                d = n % DIRS
                pool.wait_ge(ex, n + 1)
                pool.tensor_tensor(T[:, n], T[:, n], tri[:, d, None, :].broadcast_to(H4), ALU.mult).then_inc(em, 1)
                pool.wait_ge(br, n + 1)
                pool.wait_ge(em, n + 1)
                pool.tensor_tensor(TT[:, n], TT[:, n], T[:, n], ALU.mult).then_inc(ebm, 1)

        @b.vector
        def _(dve):
            dve.wait_ge(gm, 1)
            dve.tensor_copy(gcc[:].rearrange("p d t h -> p (d t h)"), PS[:, 0, 0:32]).then_inc(gcp, 1)
            dve.tensor_copy(glast[:].rearrange("p t d h -> p (t d h)"), PS[:, 0, 32:64]).then_inc(gcp, 1)
            dve.wait_ge(gcp, 2)
            dve.wait_ge(gst, 1)
            dve.tensor_tensor(kt[:], glast[:].rearrange("p t d h -> p d t h"), gcc[:], ALU.subtract).then_inc(gst, 1)
            dve.tensor_tensor(kg[:], gates[:, 0].rearrange("p t (d h) -> p d t h", d=DIRS), eg[:],
                              ALU.mult).then_inc(gcp, 1)
            for n in range(NB):
                t, d = n // DIRS, n % DIRS
                dve.wait_ge(rows, n + 1)
                dve.tensor_tensor(T[:, n], bank(1), gcc[:, d, t, :, None].broadcast_to(H4), ALU.subtract).then_inc(df, 1)
                dve.wait_ge(df, 2 * n + 1)
                dve.tensor_scalar(T[:, n], T[:, n], 0.0, None, ALU.min).then_inc(df, 1)
                if second(n):
                    dve.wait_ge(xg, seconds.index(n) + 1)
                    dve.tensor_tensor(qd[:, seconds.index(n)], qn[:, :, t * P:(t + 1) * P], ring[:, 0], ALU.mult)
                dve.wait_ge(kk, n + 1)
                dve.wait_ge(em, n + 1)
                dve.tensor_tensor(QK[:, n], bank(4), T[:, n], ALU.mult)
                dve.wait_ge(ebm, n + 1)
                dve.tensor_tensor(MT[:, n], bank(3), TT[:, n], ALU.mult).then_inc(fin, 1)

        inv = Inner(nc, st, "inv")
        mk = inv.sem("level_masked")
        xm = inv.sem("x_done")
        xc = inv.sem("x_copied")
        ym = inv.sem("y_done")
        up = inv.sem("inverse_updated")
        init = inv.sem("identity_set")
        lc = inv.sem("level_mask_copied")
        b = inv.block()

        @b.gpsimd
        def _(pool):
            pool.sem_inc(mk, 1)
            for n in range(NB):
                pool.tensor_copy(T[:, n], ident[:, None, :].broadcast_to(H4)).then_inc(init, 1)
                pool.tensor_copy(TT[:, n], ident[:, None, :].broadcast_to(H4)).then_inc(init, 1)
            with pool.Fori(0, LEVELS) as lev:
                pool.wait_ge(mk, lev * NB + 1)
                pool.wait_ge(init, 2 * NB)
                pool.tensor_copy(lmc[:], lm[:, :, bass.ds(lev, 1), :].squeeze(2)).then_inc(lc, 1)
                pool.wait_ge(lc, lev + 1)
                for n in range(NB):
                    if n < 2:
                        pool.wait_ge(xm, lev * NB + 1)
                    else:
                        pool.wait_ge(xm, lev * NB + n)
                    pool.tensor_tensor(ring[:, n % 2], MT[:, n],
                                       lmc[:, n % DIRS, None, :].broadcast_to(H4), ALU.mult).then_inc(mk, 1)

        xs = Ogdn[:, 0:2]

        @b.tensor
        def _(pe):
            pe.sem_inc(xm, 1)
            pe.sem_inc(ym, 1)
            with pe.Fori(0, LEVELS) as lev:
                def x(n):
                    pe.wait_ge(mk, lev * NB + n + 2)
                    if n < 2:
                        pe.wait_ge(xc, lev * NB + 1)
                    else:
                        pe.wait_ge(xc, lev * NB + n)
                    if n == 0:
                        pe.wait_ge(init, 2 * NB)
                        pe.wait_ge(up, 2 * NB * lev + 1)
                    for h in range(HEADS):
                        i = pe.matmul(PS[:, n % 2, h * P:(h + 1) * P], ring[:, n % 2, h, :], T[:, n, h, :],
                                      start=True, stop=True)
                    i.then_inc(xm, 1)

                def y(n):
                    pe.wait_ge(xc, lev * NB + n + 2)
                    if n >= 3:
                        pe.wait_ge(up, 2 * NB * lev + 2 * n - 3)
                    bk = 2 + 2 * (n % 3)
                    for h in range(HEADS):
                        pe.matmul(PS[:, bk, h * P:(h + 1) * P], TT[:, n, h, :], xs[:, n % 2, h, :],
                                  start=True, stop=True)
                        i = pe.matmul(PS[:, bk + 1, h * P:(h + 1) * P], xs[:, n % 2, h, :], TT[:, n, h, :],
                                      start=True, stop=True)
                    i.then_inc(ym, 1)

                x(0)
                for n in range(1, NB):
                    x(n)
                    y(n - 1)
                y(NB - 1)

        @b.scalar
        def _(act):
            act.sem_inc(xc, 1)
            with act.Fori(0, LEVELS) as lev:
                for n in range(NB):
                    act.wait_ge(xm, lev * NB + n + 2)
                    if n < 2:
                        act.wait_ge(ym, lev * NB + 1)
                    else:
                        act.wait_ge(ym, lev * NB + n)
                    act.copy(xs[:, n % 2], bank(n % 2)).then_inc(xc, 1)

        @b.vector
        def _(dve):
            dve.sem_inc(up, 1)
            dve.wait_ge(init, 2 * NB)
            with dve.Fori(0, LEVELS) as lev:
                for n in range(NB):
                    dve.wait_ge(ym, lev * NB + n + 2)
                    bk = 2 + 2 * (n % 3)
                    dve.tensor_tensor(T[:, n], T[:, n], bank(bk), ALU.subtract).then_inc(up, 1)
                    dve.tensor_tensor(TT[:, n], TT[:, n], bank(bk + 1), ALU.subtract).then_inc(up, 1)
        inv.close()

        out = Inner(nc, st, "dout")
        vb = MT
        kb = T
        NW = ring
        S = raw[:, 2].rearrange("p q (h e) -> p q h e", h=HEADS)
        SEQS = [(s, d) for s in range(N_SEQ) for d in range(DIRS)]
        scl = out.sem("operands_scaled")
        um = out.sem("first_values_done")
        uc = out.sem("first_values_copied")
        wm = out.sem("readers_done")
        wc = out.sem("readers_copied")
        sm = out.sem("state_done")
        scp = out.sem("state_copied")
        vm = out.sem("second_values_done")
        vc = out.sem("second_values_copied")
        om = out.sem("output_done")
        oc = out.sem("output_copied")
        b = out.block()

        def batch(t, d):
            return t * DIRS + d

        def tok(t, j):
            return heads(tokm[:, t, j, :])

        @b.vector
        def _(dve):
            for q, (s, d) in enumerate(SEQS):
                f, g = first_tile(s, d), second_tile(s, d)
                be = gates[:, 0, f, d * HEADS:(d + 1) * HEADS, None].broadcast_to(H4)
                dve.tensor_tensor(vb[:, batch(f, d)], tok(f, 2), be, ALU.mult).then_inc(scl, 1)
                dve.tensor_tensor(kb[:, 4 + q], tok(f, 1), kt[:, d, f, :, None].broadcast_to(H4), ALU.mult).then_inc(scl, 1)
                be = gates[:, 0, g, d * HEADS:(d + 1) * HEADS, None].broadcast_to(H4)
                dve.tensor_tensor(kb[:, q], tok(g, 1), kg[:, d, g, :, None].broadcast_to(H4), ALU.mult).then_inc(scl, 1)
                dve.tensor_tensor(vb[:, batch(g, d)], tok(g, 2), be, ALU.mult).then_inc(scl, 1)
            for q, (s, d) in enumerate(SEQS):
                dve.wait_ge(wm, q + 1)
                if q >= 2:
                    dve.wait_ge(vm, q - 1)
                dve.tensor_scalar(NW[:, q % 2], bank(1), -1.0, None, ALU.mult).then_inc(wc, 1)
                dve.wait_ge(vm, q + 1)
                dve.tensor_copy(vb[:, batch(second_tile(s, d), d)], bank(3)).then_inc(vc, 1)

        @b.scalar
        def _(act):
            for q, (s, d) in enumerate(SEQS):
                act.wait_ge(um, q + 1)
                act.copy(vb[:, batch(first_tile(s, d), d)], bank(0)).then_inc(uc, 1)
                act.wait_ge(sm, q + 1)
                act.copy(S[:, q], bank(2)).then_inc(scp, 1)
            for t in range(TILES):
                act.wait_ge(om, t + 1)
                act.copy(Ogdn[:, t], bank(4 + t)).then_inc(oc, 1)

        @b.tensor
        def _(pe):
            for q, (s, d) in enumerate(SEQS):
                f, g = first_tile(s, d), second_tile(s, d)
                pe.wait_ge(scl, 4 * q + 4)
                if q >= 1:
                    pe.wait_ge(uc, q)
                    pe.wait_ge(wc, q)
                    pe.wait_ge(scp, q)
                    pe.wait_ge(vc, q)
                for h in range(HEADS):
                    i = pe.matmul(PS[:, 0, h * P:(h + 1) * P], TT[:, batch(f, d), h, :], vb[:, batch(f, d), h, :],
                                  start=True, stop=True)
                i.then_inc(um, 1)
                for h in range(HEADS):
                    i = pe.matmul(PS[:, 1, h * P:(h + 1) * P], kb[:, q, h, :], TT[:, batch(g, d), h, :],
                                  start=True, stop=True)
                i.then_inc(wm, 1)
                pe.wait_ge(uc, q + 1)
                for h in range(HEADS):
                    i = pe.matmul(PS[:, 2, h * P:(h + 1) * P], kb[:, 4 + q, h, :], vb[:, batch(f, d), h, :],
                                  start=True, stop=True)
                i.then_inc(sm, 1)
                pe.wait_ge(wc, q + 1)
                pe.wait_ge(scp, q + 1)
                for h in range(HEADS):
                    o = PS[:, 3, h * P:(h + 1) * P]
                    pe.matmul(o, TT[:, batch(g, d), h, :], vb[:, batch(g, d), h, :], start=True, stop=False)
                    i = pe.matmul(o, NW[:, q % 2, h, :], S[:, q, h, :], start=False, stop=True)
                i.then_inc(vm, 1)
            pe.wait_ge(vc, len(SEQS))
            for t in range(TILES):
                s = t // 2
                d2 = [d for d in range(DIRS) if second_tile(s, d) == t][0]
                for h in range(HEADS):
                    o = PS[:, 4 + t, h * P:(h + 1) * P]
                    for d in range(DIRS):
                        pe.matmul(o, QK[:, batch(t, d), h, :], vb[:, batch(t, d), h, :], start=d == 0, stop=False)
                    i = pe.matmul(o, qd[:, seconds.index(batch(t, d2)), h, :], S[:, SEQS.index((s, d2)), h, :],
                                  start=False, stop=True)
                i.then_inc(om, 1)
        out.close()


def attention_stage(nc, res, qT, kT, v):
    AH, AL, ident, PS = res.AH, res.AL, res.ident, res.PS
    UNITS = [(s, h) for s in range(N_SEQ) for h in range(HEADS)]
    scale = XA_DH ** -0.5
    with Stage(nc, "att") as st:
        p = st.sb("probs", [P, 2, 2, SEQ])
        pT = st.sb("probs_T", [P, 2, 2, SEQ])
        mx = st.sb("max", [P, 2, 2])
        nm = st.sb("neg_max", [P, 2, 2])
        su = st.sb("sum", [P, 2, 2])
        ri = st.sb("inverse", [P, 2, 2])
        sm = st.sem("scores_done")
        ms = st.sem("max_step")
        ex = st.sem("exp_done")
        rs = st.sem("sum_inverted")
        nz = st.sem("probs_normalised")
        tm = st.sem("probs_turned")
        tcp = st.sem("probs_T_copied")
        om = st.sem("output_done")
        h_ok = st.sem("hi_written")
        l_ok = st.sem("lo_written")
        b = st.block()

        def dst(a, u):
            s, h = UNITS[u]
            return a[:, 2 * h:2 * h + 2, s * SEQ:(s + 1) * SEQ]

        def two(n):
            return PS[:, n, :].rearrange("p (a i) -> p a i", a=2)

        @b.tensor
        def _(pe):
            def scores(u):
                s, h = UNITS[u]
                if u >= 2:
                    pe.wait_ge(ex, 2 * (u - 1))
                for t in range(2):
                    for k in range(2):
                        i = pe.matmul(PS[:, u % 2, t * SEQ:(t + 1) * SEQ],
                                      qT[:, 2 * h + k, s * SEQ + t * P:s * SEQ + (t + 1) * P],
                                      kT[:, 2 * h + k, s * SEQ:(s + 1) * SEQ], start=k == 0, stop=k == 1)
                i.then_inc(sm, 1)

            def turn(u):
                pe.wait_ge(nz, 2 * u + 2)
                if u >= 2:
                    pe.wait_ge(tcp, u - 1)
                for m in range(2):
                    for t in range(2):
                        i = pe.transpose(PS[:, 2 + u % 2, m * SEQ + t * P:m * SEQ + (t + 1) * P],
                                         p[:, u % 2, t, m * P:(m + 1) * P], ident[:])
                i.then_inc(tm, 1)

            def output(u):
                s, h = UNITS[u]
                pe.wait_ge(tcp, u + 1)
                if u >= 2:
                    pe.wait_ge(l_ok, u - 1)
                for e in range(2):
                    for m in range(2):
                        i = pe.matmul(PS[:, 4 + u % 2, e * SEQ:(e + 1) * SEQ],
                                      v[:, 2 * s + m, h * XA_DH + e * P:h * XA_DH + (e + 1) * P],
                                      pT[:, u % 2, m, :], start=m == 0, stop=m == 1)
                i.then_inc(om, 1)

            n = len(UNITS)
            for u in range(n + 2):
                if u < n:
                    scores(u)
                if 1 <= u <= n:
                    turn(u - 1)
                if u >= 2:
                    output(u - 2)

        @b.vector
        def _(dve):
            def low(u):
                dve.wait_ge(h_ok, u + 1)
                dve.tensor_tensor(dst(AL, u), two(4 + u % 2), dst(AH, u).bitcast(F32), ALU.subtract).then_inc(l_ok, 1)

            for u in range(len(UNITS)):
                dve.wait_ge(sm, u + 1)
                if u >= 2:
                    dve.wait_ge(ex, 2 * (u - 1))
                dve.tensor_reduce(mx[:, u % 2], two(u % 2), AX.X, ALU.max).then_inc(ms, 1)
                dve.wait_ge(ms, 2 * u + 1)
                dve.tensor_scalar(nm[:, u % 2], mx[:, u % 2], -scale, None, ALU.mult).then_inc(ms, 1)
                dve.wait_ge(ex, 2 * u + 2)
                dve.reciprocal(ri[:, u % 2], su[:, u % 2]).then_inc(rs, 1)
                dve.wait_ge(rs, u + 1)
                for t in range(2):
                    dve.tensor_scalar(p[:, u % 2, t], p[:, u % 2, t], ri[:, u % 2, t:t + 1], None, ALU.mult).then_inc(nz, 1)
                dve.wait_ge(tm, u + 1)
                dve.tensor_copy(pT[:, u % 2], two(2 + u % 2)).then_inc(tcp, 1)
                if u >= 1:
                    low(u - 1)
            low(len(UNITS) - 1)

        @b.scalar
        def _(act):
            def high(u):
                act.wait_ge(om, u + 1)
                act.copy(dst(AH, u), two(4 + u % 2)).then_inc(h_ok, 1)

            for u in range(len(UNITS)):
                act.wait_ge(ms, 2 * u + 2)
                if u >= 2:
                    act.wait_ge(tm, u - 1)
                for t in range(2):
                    act.activation(p[:, u % 2, t], PS[:, u % 2, t * SEQ:(t + 1) * SEQ], ACT.Exp,
                                   bias=nm[:, u % 2, t:t + 1], scale=scale,
                                   accum_out=su[:, u % 2, t:t + 1]).then_inc(ex, 1)
                if u >= 1:
                    high(u - 1)
            high(len(UNITS) - 1)


def select_stage(nc, res, qT, keys, SL):
    ident, PS = res.ident, res.PS
    HC = 2 * PH
    STEPS = 20
    GATE_IN = 12
    with Stage(nc, "sel") as st:
        kraw = st.sb("keys", [P, HC, P])
        kTs = st.sb("keys_T", [P, HC, P])
        sc = st.sb("scores", [P, 2, HC, NKEYS])
        v1 = st.sb("top_values", [P, HC, TOPK])
        i1 = st.sb("top_indices", [P, HC, TOPK], U32)
        i1f = st.sb("top_indices_f", [P, HC, TOPK])
        ca = st.sb("candidates", [P, PH, TOPK * TOPK])
        tv = st.sb("best_values", [P, PH, TOPK])
        tp = st.sb("best_positions", [P, PH, TOPK], U32)
        ab = st.sb("position_halves", [P, 2, PH, TOPK], U32)
        abf = st.sb("position_halves_f", [P, 2, PH, TOPK])
        eq = st.sb("eq", [P, 2, SLOTS, TOPK])
        out = st.sb("slots", [P, 3, SLOTS])
        ez = st.sb("gate_exp", [P, PH, TOPK])
        zs = st.sb("gate_sum", [P, PH])
        zi = st.sb("gate_inverse", [P, PH])
        k_in = st.sem("keys_loaded")
        kt_ = st.sem("keys_turned")
        kc = st.sem("keys_copied")
        sm = st.sem("scores_done")
        scp = st.sem("scores_copied")
        step = st.sem("vector_step")
        ge = st.sem("gate_exp_done")
        pool_eq = st.sem("pool_matches")
        so = st.sem("slots_ready")
        tr = st.sem("slots_turned")
        tcp = st.sem("slots_copied")
        b = st.block()

        @b.sync
        def _(sp):
            for n in range(HC):
                sp.dma_start(kraw[:, n, :], keys[n // 2, n % 2]).then_inc(k_in, 16)

        @b.tensor
        def _(pe):
            pe.wait_ge(k_in, 16 * HC)
            for n in range(4):
                for m in range(4):
                    i = pe.transpose(PS[:, n, m * P:(m + 1) * P], kraw[:, 4 * n + m, :], ident[:])
                i.then_inc(kt_, 1)
            pe.wait_ge(kc, 4)

            def scores(t):
                for n in range(4):
                    if t >= 1:
                        pe.wait_ge(scp, 4 * (t - 1) + n + 1)
                    for m in range(4):
                        i = pe.matmul(PS[:, n, m * P:(m + 1) * P], qT[:, 4 * n + m, t * P:(t + 1) * P],
                                      kTs[:, 4 * n + m, :], start=True, stop=True)
                    i.then_inc(sm, 1)

            def turn(t):
                pe.wait_ge(so, 3 * t + 3)
                if t >= 1:
                    pe.wait_ge(tcp, 3 * t)
                for j in range(3):
                    i = pe.transpose(PS[:, 4, j * P:(j + 1) * P], out[:, j, :], ident[:])
                i.then_inc(tr, 1)

            scores(0)
            for t in range(TILES):
                if t + 1 < TILES:
                    scores(t + 1)
                turn(t)

        @b.scalar
        def _(act):
            for n in range(4):
                act.wait_ge(kt_, n + 1)
                act.copy(kTs[:, 4 * n:4 * n + 4, :].rearrange("p a n -> p (a n)"), PS[:, n, :]).then_inc(kc, 1)
            act.wait_ge(kc, 4)

            def scores(t):
                if t >= 2:
                    act.wait_ge(step, STEPS * (t - 2) + 5)
                for n in range(4):
                    act.wait_ge(sm, 4 * t + n + 1)
                    act.copy(sc[:, t % 2, 4 * n:4 * n + 4, :].rearrange("p a n -> p (a n)"), PS[:, n, :]).then_inc(scp, 1)

            scores(0)
            for t in range(TILES):
                if t + 1 < TILES:
                    scores(t + 1)
                act.wait_ge(step, STEPS * t + GATE_IN)
                act.activation(ez[:], ez[:], ACT.Exp).then_inc(ge, 1)

        @b.vector
        def _(dve):
            n = 0

            def mark(ins):
                nonlocal n
                n += 1
                ins.then_inc(step, 1)
                dve.wait_ge(step, n)

            for t in range(TILES):
                dve.wait_ge(scp, 4 * t + 4)
                s = sc[:, t % 2]

                def top16(values, count, top, index):
                    for j in range(count):
                        i = dve.max(top[:, j, 0:8], values[:, j, :])
                    mark(i)
                    for j in range(count):
                        i = dve.max_index(index[:, j, 0:8], top[:, j, 0:8], values[:, j, :])
                    mark(i)
                    for j in range(count):
                        i = dve.match_replace(values[:, j, :], top[:, j, 0:8], values[:, j, :], NEG)
                    mark(i)
                    for j in range(count):
                        i = dve.max(top[:, j, 8:16], values[:, j, :])
                    mark(i)
                    for j in range(count):
                        i = dve.max_index(index[:, j, 8:16], top[:, j, 8:16], values[:, j, :])
                    mark(i)

                top16(s, HC, v1, i1)
                vv = v1[:].rearrange("p (h c) k -> p h c k", c=2)
                shape = [P, PH, TOPK, TOPK]
                mark(dve.tensor_tensor(ca[:].rearrange("p h (a b) -> p h a b", a=TOPK),
                                       vv[:, :, 0, :, None].broadcast_to(shape),
                                       vv[:, :, 1, None, :].broadcast_to(shape), ALU.add))
                top16(ca, PH, tv, tp)
                mark(dve.tensor_tensor(ez[:], tv[:], tv[:, :, 0:1].broadcast_to([P, PH, TOPK]), ALU.subtract))
                dve.tensor_scalar(ab[:, 0], tp[:], 4, None, ALU.logical_shift_right)
                mark(dve.tensor_scalar(ab[:, 1], tp[:], TOPK - 1, None, ALU.bitwise_and))
                dve.tensor_copy(i1f[:], i1[:])
                mark(dve.tensor_copy(abf[:], ab[:]))
                if t:
                    dve.wait_ge(tr, t)
                for c in range(2):
                    e = eq[:, c]
                    mark(dve.tensor_tensor(
                        e, abf[:, c].rearrange("p h k -> p (h k)")[:, :, None].broadcast_to([P, SLOTS, TOPK]),
                        res.iota[:, None, 0:TOPK].broadcast_to([P, SLOTS, TOPK]), ALU.is_equal))
                    e4 = e.rearrange("p (h k) a -> p h k a", h=PH)
                    ix = i1f[:].rearrange("p (h c) k -> p h c k", c=2)[:, :, c, None, :].broadcast_to([P, PH, TOPK, TOPK])
                    mark(dve.tensor_tensor(e4, e4, ix, ALU.mult))
                for c in range(2):
                    dve.tensor_reduce(out[:, c, :], eq[:, c], AX.X, ALU.add).then_inc(so, 1)
                dve.wait_ge(ge, t + 1)
                mark(dve.tensor_reduce(zs[:], ez[:], AX.X, ALU.add))
                mark(dve.reciprocal(zi[:], zs[:]))
                dve.tensor_tensor(out[:, 2, :].rearrange("p (h k) -> p h k", h=PH), ez[:],
                                  zi[:, :, None].broadcast_to([P, PH, TOPK]), ALU.mult).then_inc(so, 1)
                dve.wait_ge(tr, t + 1)
                ts = slice(t * P, (t + 1) * P)
                dve.tensor_copy(SL.idx[:, :, ts], PS[:, 4, 0:2 * P].rearrange("p (a t) -> p a t", a=2)).then_inc(tcp, 1)
                dve.tensor_copy(SL.hi[:, ts], PS[:, 4, 2 * P:3 * P]).then_inc(tcp, 1)
                dve.wait_ge(tcp, 3 * t + 2)
                dve.tensor_tensor(SL.lo[:, ts], PS[:, 4, 2 * P:3 * P], SL.hi[:, ts].bitcast(F32), ALU.subtract).then_inc(tcp, 1)
            assert n == STEPS * TILES, n


BLK = 64


def gate_stage(nc, res, SL):
    PS = res.PS
    SUB = 4
    NR = 4
    BATCH = SUB * NR
    NBLK = TOK // BLK
    with Stage(nc, "gate") as st:
        oh = st.sb("one_hot_1", [P, BATCH, P], F32R)
        gh = st.sb("gated_one_hot_2", [P, BATCH, 2, P], F32R)
        gb = st.sb("block", [P, 2, P, BLK])
        ok = st.sem("one_hots_ready")
        mm = st.sem("four_tokens_done")
        cp = st.sem("bank_free")
        so = [st.sem(f"block{i}_stored") for i in range(2)]
        b = st.block()

        @b.vector
        def _(dve):
            with dve.Fori(0, TOK // BATCH) as it:
                for q in range(NR):
                    dve.wait_ge(mm, it * NR + q + 1)
                    for k in range(SUB):
                        j = q * SUB + k
                        col = bass.ds(it * BATCH + j, 1)
                        dve.tensor_scalar(oh[:, j, :], res.iota[:], SL.idx[:, 0, col], None, ALU.is_equal)
                        dve.tensor_scalar(gh[:, j, 0, :], res.iota[:], SL.idx[:, 1, col],
                                          SL.hi[:, col].bitcast(F32), ALU.is_equal, ALU.mult)
                        i = dve.tensor_scalar(gh[:, j, 1, :], res.iota[:], SL.idx[:, 1, col],
                                              SL.lo[:, col].bitcast(F32), ALU.is_equal, ALU.mult)
                    i.then_inc(ok, 1)

        @b.tensor
        def _(pe):
            pe.sem_inc(mm, NR)
            with pe.Fori(0, TOK // BATCH) as it:
                for q in range(NR):
                    pe.wait_ge(ok, it * NR + q + 1)
                    pe.wait_ge(cp, it * NR + q + 1)
                    for k in range(SUB):
                        j = q * SUB + k
                        o = PS[:, q, k * P:(k + 1) * P]
                        pe.matmul(o, gh[:, j, 0, :], oh[:, j, :], start=True, stop=False)
                        i = pe.matmul(o, gh[:, j, 1, :], oh[:, j, :], start=False, stop=True)
                    i.then_inc(mm, 1)

        @b.scalar
        def _(act):
            act.sem_inc(cp, NR)
            PER = BLK // BATCH
            with act.Fori(0, NBLK // 2) as pair:
                for half in range(2):
                    act.wait_ge(so[half], 16 * pair + 16)
                    with act.Fori(0, PER) as r:
                        for q in range(NR):
                            act.wait_ge(mm, ((pair * 2 + half) * PER + r) * NR + NR + q + 1)
                            act.copy(gb[:, half, :, bass.ds(r * BATCH + q * SUB, SUB)].rearrange("p i t -> p t i"),
                                     PS[:, q, :].rearrange("p (t i) -> p t i", t=SUB)).then_inc(cp, 1)

        @b.sync
        def _(sp):
            for half in range(2):
                sp.sem_inc(so[half], 16)
            with sp.Fori(0, NBLK // 2) as pair:
                for half in range(2):
                    sp.wait_ge(cp, NR + (pair * 2 + half + 1) * (BLK // SUB))
                    sp.dma_start(res.gates[:, :, bass.ds((pair * 2 + half) * BLK, BLK)].rearrange("a b t -> b a t"),
                                 gb[:, half]).then_inc(so[half], 16)
            for half in range(2):
                sp.wait_ge(so[half], 16 * (NBLK // 2 + 1))


def expert_stage(nc, res, U, V):
    AH, AL, ident, PS, X = res.AH, res.AL, res.ident, res.PS, res.X
    NT = NKEYS
    NG = NT // GROUP
    with Stage(nc, "exp") as st:
        ur = st.sb("u_raw", [P, 2, D])
        uh = st.sb("uT_hi", [P, 2, KC, P], F32R)
        ul = st.sb("uT_lo", [P, 2, KC, P], F32R)
        vr = st.sb("v_raw", [P, 2, D])
        vh = st.sb("v_hi", [P, GROUP, D], F32R)
        vl = st.sb("v_lo", [P, GROUP, D], F32R)
        gt = st.sb("gates", [P, GROUP, TOK])
        ag = st.sb("gelu", [P, 2, TOK])
        w = st.sb("w", [P, 2, TOK])
        wh = st.sb("w_hi", [P, GROUP, TOK], F32R)
        wl = st.sb("w_lo", [P, GROUP, TOK], F32R)
        u_in = [st.sem(f"u{i}_loaded") for i in range(2)]
        v_in = [st.sem(f"v{i}_loaded") for i in range(2)]
        g_in = [st.sem(f"gates{i}_loaded") for i in range(GROUP)]
        ut = st.sem("u_turned")
        uho = st.sem("uT_hi_written")
        ulo = st.sem("uT_lo_written")
        vho = st.sem("v_hi_written")
        vlo = st.sem("v_lo_written")
        am = st.sem("a_done")
        ge = st.sem("gelu_done")
        wo = st.sem("w_ready")
        who = st.sem("w_hi_written")
        wlo = st.sem("w_lo_written")
        om = st.sem("output_bank_done")
        ad = st.sem("output_bank_added")
        b = st.block()

        @b.sync
        def _(sp):
            def load_u(n, slot):
                sp.dma_start(ur[:, slot], U[bass.ds(n * P, P), :]).then_inc(u_in[slot], 16)

            def load_v(n, slot):
                sp.dma_start(vr[:, slot], V[bass.ds(n * P, P), :]).then_inc(v_in[slot], 16)

            def load_g(n, slot):
                sp.dma_start(gt[:, slot], res.gates[bass.ds(n, 1), :, :].rearrange("a b t -> (a b) t")).then_inc(g_in[slot], 16)

            for n in range(2):
                load_u(n, n)
                load_v(n, n)
            for n in range(GROUP):
                load_g(n, n)

            def ahead(g, e, last):
                n = g * GROUP + e
                sp.wait_ge(ut, n + 1)
                load_u(0 if last and e >= GROUP - 2 else n + 2, e % 2)
                if not (last and e >= GROUP - 2):
                    sp.wait_ge(vlo, n + 1)
                    load_v(n + 2, e % 2)
                if not last:
                    sp.wait_ge(wo, n + 3)
                    load_g(n + GROUP, e)

            with sp.Fori(0, NG - 1) as g:
                for e in range(GROUP):
                    ahead(g, e, False)
            for e in range(GROUP - 1):
                ahead(NG - 1, e, True)
            sp.wait_ge(u_in[0], 16 * (NT // 2 + 1))

        @b.tensor
        def _(pe):
            def turn(n, slot):
                pe.wait_ge(u_in[slot], (n - slot) * 8 + 16)
                for k in range(KC):
                    i = pe.transpose(PS[:, k // 4, (k % 4) * P:(k % 4 + 1) * P], ur[:, slot, k * P:(k + 1) * P], ident[:])
                i.then_inc(ut, 1)

            pe.sem_inc(am, 1)
            pe.sem_inc(om, 1)
            turn(0, 0)
            with pe.Fori(0, NG) as g:
                for e in range(GROUP):
                    n = g * GROUP + e
                    pe.wait_ge(ulo, n + 1)
                    turn(n + 1, (e + 1) % 2)
                    pe.wait_ge(ge, n + 1)
                    for k in range(KC):
                        i = mm3(pe, PS[:, 2 + e % 2, :], (uh[:, e % 2, k, :], ul[:, e % 2, k, :]),
                                (AH[:, k, :], AL[:, k, :]), k == 0, k == KC - 1)
                    i.then_inc(am, 1)
                for half in range(2):
                    cols = slice(half * CHUNK, (half + 1) * CHUNK)
                    for e in range(GROUP):
                        if half == 0:
                            pe.wait_ge(wlo, g * GROUP + e + 1)
                            pe.wait_ge(vlo, g * GROUP + e + 1)
                        for t in range(TILES):
                            if e == 0:
                                pe.wait_ge(ad, g * 8 + 4 * half + t + 1)
                            s = slice(t * P, (t + 1) * P)
                            i = mm3(pe, PS[:, 4 + t, :], (wh[:, e, s], wl[:, e, s]),
                                    (vh[:, e, cols], vl[:, e, cols]), e == 0, e == GROUP - 1)
                            if e == GROUP - 1:
                                i.then_inc(om, 1)

        def turned(n=None):
            return PS[:, 0:2, :].rearrange("p b (k e) -> p (b k) e", k=4)

        @b.scalar
        def _(act):
            act.sem_inc(ge, 2)

            def u_hi(n, slot):
                act.wait_ge(ut, n + 1)
                act.copy(uh[:, slot], turned()).then_inc(uho, 1)

            u_hi(0, 0)
            with act.Fori(0, NG) as g:
                for e in range(GROUP):
                    n = g * GROUP + e
                    act.wait_ge(v_in[e % 2], g * 32 + (e // 2) * 16 + 16)
                    if e == 0:
                        act.wait_ge(om, g * 8 + 1)
                    act.copy(vh[:, e], vr[:, e % 2]).then_inc(vho, 1)
                    act.wait_ge(am, n + 1)
                    u_hi(n + 1, (e + 1) % 2)
                    act.wait_ge(am, n + 2)
                    act.wait_ge(wo, n + 1)
                    act.activation(ag[:, e % 2], PS[:, 2 + e % 2, :], ACT.Gelu_apprx_tanh).then_inc(ge, 1)
                    act.wait_ge(wo, n + 3)
                    act.copy(wh[:, e], w[:, e % 2]).then_inc(who, 1)

        @b.vector
        def _(dve):
            dve.sem_inc(wo, 2)
            dve.sem_inc(ad, 4)

            def u_lo(n, slot):
                dve.wait_ge(uho, n + 1)
                dve.tensor_tensor(ul[:, slot], turned(), uh[:, slot].bitcast(F32), ALU.subtract).then_inc(ulo, 1)

            u_lo(0, 0)
            with dve.Fori(0, NG) as g:
                for e in range(GROUP):
                    n = g * GROUP + e
                    dve.wait_ge(vho, n + 1)
                    dve.tensor_tensor(vl[:, e], vr[:, e % 2], vh[:, e].bitcast(F32), ALU.subtract).then_inc(vlo, 1)
                    u_lo(n + 1, (e + 1) % 2)
                    dve.wait_ge(ge, n + 3)
                    dve.wait_ge(g_in[e], g * 16 + 16)
                    dve.tensor_tensor(w[:, e % 2], ag[:, e % 2], gt[:, e], ALU.mult).then_inc(wo, 1)
                    dve.wait_ge(who, n + 1)
                    dve.tensor_tensor(wl[:, e], w[:, e % 2], wh[:, e].bitcast(F32), ALU.subtract).then_inc(wlo, 1)
                for half in range(2):
                    for t in range(TILES):
                        dve.wait_ge(om, g * 8 + 4 * half + t + 2)
                        x = X[:, t, half * CHUNK:(half + 1) * CHUNK]
                        dve.tensor_tensor(x, PS[:, 4 + t, :], x, ALU.add).then_inc(ad, 1)


def final_stage(nc, res, weight, outs):
    X = res.X
    with Stage(nc, "final") as st:
        wb = st.sb("weight", [P, D])
        sq = st.sb("sq", [P, D])
        y = st.sb("y", [P, TILES, D])
        ms = st.sb("ms", [P, TILES])
        mse = st.sb("mse", [P, TILES])
        rs = st.sb("rs", [P, TILES])
        w_in_ = st.sem("weight_loaded")
        ssq = st.sem("squares_summed")
        m_ok = st.sem("mean_ready")
        r_ok = st.sem("rsqrt_ready")
        y_ok = st.sem("row_ready")
        stored = st.sem("stored")
        b = st.block()

        @b.sync
        def _(sp):
            sp.dma_start(wb[:], weight.partition_broadcast(P)).then_inc(w_in_, 16)
            for t in range(TILES):
                sp.wait_ge(y_ok, t + 1)
                sp.dma_start(outs[t // 2][0, (t % 2) * P:(t % 2 + 1) * P, :], y[:, t, :]).then_inc(stored, 16)
            sp.wait_ge(stored, 16 * TILES)

        @b.scalar
        def _(act):
            for t in range(TILES):
                act.activation(sq[:], X[:, t, :], ACT.Square, accum_out=ms[:, t:t + 1]).then_inc(ssq, 1)
                act.wait_ge(ssq, t + 1)

        @b.gpsimd
        def _(pool):
            pool.wait_ge(m_ok, 1)
            pool.tensor_tensor(rs[:], mse[:], res.mhalf[:, 0:TILES], ALU.pow).then_inc(r_ok, 1)

        @b.vector
        def _(dve):
            dve.wait_ge(ssq, TILES)
            dve.tensor_scalar(mse[:], ms[:], 1.0 / D, EPS, ALU.mult, ALU.add).then_inc(m_ok, 1)
            dve.wait_ge(r_ok, 1)
            dve.wait_ge(w_in_, 16)
            for t in range(TILES):
                dve.scalar_tensor_tensor(out=y[:, t, :], in0=X[:, t, :], scalar=rs[:, t:t + 1], in1=wb[:],
                                         op0=ALU.mult, op1=ALU.mult).then_inc(y_ok, 1)


class Resident:
    pass


class Slots:
    pass


def build(nc, a, outs, stop=None, depth=DEPTH):
    Stage.before = []
    res = Resident()
    with ExitStack() as ctx:
        ctx.enter_context(nc.allow_non_contiguous_dma(reason="per-partition vectors of a few values"))

        def sb(name, shape, dtype=F32):
            return ctx.enter_context(nc.sbuf_tensor(name, shape, dtype))

        res.X = sb("residual", [P, TILES, D])
        res.AH = sb("act_hi", [P, KC, TOK], F32R)
        res.AL = sb("act_lo", [P, KC, TOK], F32R)
        res.ident = sb("identity", [P, P])
        res.ones = sb("ones", [P, P])
        res.iota = sb("iota", [P, P])
        res.mhalf = sb("minus_half", [P, 32])
        res.PS = ctx.enter_context(nc.psum_tensor("banks", [P, 8, 512], F32))
        res.c_rot, res.c_dec, res.c_tri, res.c_lm = a["c_rot"], a["c_dec"], a["c_tri"], a["c_lm"]
        res.gates = nc.dram_tensor("dense_gates", [NKEYS, NKEYS, TOK], F32, kind="Internal").ap()

        with Stage(nc, "load") as st:
            x_in = st.sem("loaded")
            b = st.block()

            @b.sync
            def _(sp):
                for t in range(TILES):
                    src = a["x_prompt"] if t < 2 else a["x_sample"]
                    sp.dma_start(res.X[:, t, :], src[0, (t % 2) * P:(t % 2 + 1) * P, :]).then_inc(x_in, 16)
                sp.dma_start(res.ident[:], a["c_ident"]).then_inc(x_in, 16)
                sp.dma_start(res.iota[:], a["c_iota"].partition_broadcast(P)).then_inc(x_in, 16)
                sp.wait_ge(x_in, 16 * (TILES + 2))

            @b.gpsimd
            def _(pool):
                pool.memset(res.mhalf[:], -0.5)
                pool.memset(res.ones[:], 1.0)

        mems = [(a["mem_prompt"] if t < 2 else a["mem_sample"])[0, (t % 2) * P:(t % 2 + 1) * P, :] for t in range(TILES)]

        def layers(l):
            def of(name):
                return a[name][l]

            with ExitStack() as mix:
                SG = mix.enter_context(nc.sbuf_tensor("gate_rows", [P, 2, HEADS, TOK], F32))
                raw = mix.enter_context(nc.sbuf_tensor("delta_rows", [P, 3, HEADS, TOK], F32))
                small = mix.enter_context(nc.sbuf_tensor("small", [P, TILES, 16], F32))
                gates = mix.enter_context(nc.sbuf_tensor("delta_gates", [P, 2, TILES, 8], F32))
                O = mix.enter_context(nc.sbuf_tensor("mixer_out", [P, TILES, HEADS, P], F32))
                w_in = of("w_in")
                with ExitStack() as rt:
                    tok = rt.enter_context(nc.sbuf_tensor("ret_rows", [P, 3, TILES, CHUNK], F32))
                    norm_stage(nc, "nmix", res, res.X, of("norm_mix"))
                    project_stage(nc, "win", res, w_in, [
                        (3, 0, True, lambda j, t: one(tok[:, bass.ds(j, 1), t, :])),
                        (1, 3 * CHUNK, False, lambda j, c: SG[:, 0, c, :]),
                        (3, 4 * CHUNK, False, lambda j, c: one(raw[:, bass.ds(j, 1), c, :])),
                        (1, 7 * CHUNK, False, lambda j, c: SG[:, 1, c, :]),
                    ], tail=(w_in, 8 * CHUNK, small[:]))
                    retention_stage(nc, res, tok, O)
                merge_stage(nc, "mret", res, O, True, of("ret_norm"), True, SG, 0, 0)
                conv_stage(nc, res, of("gdn_conv"), raw, small, gates, of("gdn_a_log").rearrange("d h -> (d h)"),
                           of("gdn_dt_bias").rearrange("d h -> (d h)"))
                with ExitStack() as dl:
                    tokm = dl.enter_context(nc.sbuf_tensor("delta_tokens", [P, TILES, 3, CHUNK], F32))
                    unit_stage(nc, res, raw, tokm)
                    delta_stage(nc, res, raw, tokm, gates, O)
                merge_stage(nc, "mgdn", res, O, False, of("gdn_norm"), False, SG, 1, HEADS)
            project_stage(nc, "wout", res, of("w_out"), [(2, 0, True, None)])
            if stop == "mix":
                return
            with ExitStack() as xa:
                kT = xa.enter_context(nc.sbuf_tensor("mem_keys", [P, KC, TOK], F32))
                v = xa.enter_context(nc.sbuf_tensor("mem_values", [P, TILES, D], F32))
                qT = xa.enter_context(nc.sbuf_tensor("xa_queries", [P, KC, TOK], F32))
                norm_stage(nc, "nmem", res, None, of("norm_mem"), mems)
                project_stage(nc, "wkv", res, of("w_xkv"), [
                    (2, 0, False, lambda j, c: one(kT[:, bass.ds(j * 4 + c, 1), :])),
                    (2, 2 * CHUNK, True, lambda j, t: v[:, t, bass.ds(j * CHUNK, CHUNK)]),
                ])
                norm_stage(nc, "nxa", res, res.X, of("norm_xa"))
                project_stage(nc, "wxq", res, of("w_xq"), [(2, 0, False, lambda j, c: one(qT[:, bass.ds(j * 4 + c, 1), :]))])
                attention_stage(nc, res, qT, kT, v)
            project_stage(nc, "wxo", res, of("w_xo"), [(2, 0, True, None)])
            if stop == "xa":
                return
            norm_stage(nc, "nffn", res, res.X, of("norm_ffn"))
            with ExitStack() as pf:
                SL = Slots()
                SL.idx = pf.enter_context(nc.sbuf_tensor("slot_keys", [P, 2, TOK], F32))
                SL.hi = pf.enter_context(nc.sbuf_tensor("slot_gate_hi", [P, TOK], F32R))
                SL.lo = pf.enter_context(nc.sbuf_tensor("slot_gate_lo", [P, TOK], F32R))
                with ExitStack() as pq:
                    qT = pq.enter_context(nc.sbuf_tensor("peer_queries", [P, 2 * PH, TOK], F32))
                    project_stage(nc, "wpq", res, of("peer_wq"), [(4, 0, False, lambda j, c: one(qT[:, bass.ds(j * 4 + c, 1), :]))])
                    select_stage(nc, res, qT, of("peer_keys"), SL)
                gate_stage(nc, res, SL)
            expert_stage(nc, res, of("peer_u"), of("peer_v"))

        with nc.Fori(0, depth) as l:
            layers(l)
            with Stage(nc, "turn") as st:
                st.block()
        final_stage(nc, res, a["norm_final"], outs)
        with Stage(nc, "end") as st:
            st.block()


def one(ap):
    return ap.squeeze(1) if len(ap.shape) == 3 else ap


def tables():
    f = np.float32
    inv = (np.float32(10000.0) ** (-np.arange(0, P, 2, dtype=f) / f(P))).astype(f)
    ang = (np.arange(SEQ, dtype=f)[:, None] * inv[None, :]).astype(f).astype(np.float64)
    rot = np.stack([np.cos(ang), np.sin(ang)], 1).astype(f).reshape(2, P, 2, 64).transpose(1, 0, 2, 3)
    i = np.arange(SEQ)
    diff = (i[None, :] - i[:, None]).astype(np.float64)
    dec = np.zeros((HEADS, SEQ, SEQ))
    for h in range(HEADS):
        fwd, bwd = np.log1p(-2.0 ** (-5.0 - h)), np.log1p(-2.0 ** (-5.5 - h))
        dec[h] = np.where(diff >= 0, np.exp(fwd * np.abs(diff)), np.exp(bwd * np.abs(diff))) * P ** -0.5
    dec = dec.reshape(HEADS, 2, P, SEQ).transpose(2, 0, 1, 3).astype(f)
    j, k = np.arange(P)[:, None], np.arange(P)[None, :]
    tri = np.stack([j <= k, j >= k], 1).astype(f)
    lm = np.zeros((P, DIRS, LEVELS, P), f)
    for lev in range(LEVELS):
        s = 1 << lev
        pair = (j // (2 * s)) == (k // (2 * s))
        lm[:, 0, lev] = pair & (j // s % 2 == 0) & (k // s % 2 == 1)
        lm[:, 1, lev] = pair & (j // s % 2 == 1) & (k // s % 2 == 0)
    return {"c_rot": np.ascontiguousarray(rot), "c_dec": np.ascontiguousarray(dec), "c_tri": tri, "c_lm": lm,
            "c_ident": np.eye(P, dtype=f), "c_iota": np.arange(P, dtype=f)}


_INS = ["x_prompt", "x_sample", "mem_prompt", "mem_sample", "norm_mix", "w_in", "ret_norm", "gdn_conv", "gdn_a_log",
        "gdn_dt_bias", "gdn_norm", "w_out", "norm_xa", "norm_mem", "w_xq", "w_xkv", "w_xo", "norm_ffn", "peer_wq",
        "peer_keys", "peer_u", "peer_v", "norm_final"]


def kernel(**inputs):
    import concourse.bacc as _bacc
    from concourse.bass_utils import run_bass_kernel_spmd as _run

    nc = _bacc.Bacc("TRN2", target_bir_lowering=False, num_devices=1)
    arrays, args = {}, {}
    for name, x in [(n, np.ascontiguousarray(inputs[n])) for n in _INS] + list(tables().items()):
        arrays[f"in_{name}"] = x
        args[name] = nc.dram_tensor(f"in_{name}", x.shape, F32, kind="ExternalInput").ap()
    outs = [nc.dram_tensor(f"out_{i}", [1, SEQ, D], F32, kind="ExternalOutput").ap() for i in range(N_SEQ)]
    build(nc, args, outs)
    r = _run(nc, [arrays], core_ids=[0])
    return tuple(r.results[0][f"out_{i}"] for i in range(N_SEQ))
```

```python
from contextlib import ExitStack

import numpy as np

import concourse.bass as bass
from concourse import mybir

ALU = mybir.AluOpType
ACT = mybir.ActivationFunctionType
AX = mybir.AxisListType
F32 = mybir.dt.float32
F32R = mybir.dt.float32r
U32 = mybir.dt.uint32

P = 128
EPS = 1e-6
SEQ = 256
N_SEQ = 2
TILES = N_SEQ * SEQ // P
TOK = N_SEQ * SEQ
D = 1024
KC = D // P
DEPTH = 2
HEADS = 4
LEVELS = 7
XA_DH = 256
PH = 8
TOPK = 16
SLOTS = PH * TOPK
NKEYS = 128
GROUP = 4
CHUNK = 512
NEG = -3.0e38
DIRS = 2


class Stage:

    before = []

    def __init__(self, nc, name):
        self.nc, self.name, self.ctx, self.sems = nc, name, ExitStack(), []

    def __enter__(self):
        return self

    def sb(self, name, shape, dtype=F32):
        return self.ctx.enter_context(self.nc.sbuf_tensor(f"{self.name}_{name}", shape, dtype))

    def sem(self, name):
        s = self.nc.alloc_semaphore(f"{self.name}_{name}")
        self.sems.append(s)
        return s

    def block(self):
        done, Stage.before = Stage.before, self.sems
        self.block_ctx = self.nc.Block()
        b = self.block_ctx.__enter__()

        @b.gpsimd
        def _(pool):
            for s in done:
                pool.sem_clear(s)

        self.done = done
        return b

    def __exit__(self, *e):
        self.block_ctx.__exit__(*e)
        for s in self.done:
            self.nc.release_semaphore(s)
        self.ctx.__exit__(*e)
        return False


class Part:

    def __init__(self, stage, name):
        self.stage, self.name = stage, name

    def sb(self, name, shape, dtype=F32):
        return self.stage.sb(f"{self.name}_{name}", shape, dtype)

    def sem(self, name):
        return self.stage.sem(f"{self.name}_{name}")


class Inner(Stage):

    def __init__(self, nc, outer, name):
        super().__init__(nc, name)
        outer.block_ctx.__exit__(None, None, None)
        for s in outer.done:
            nc.release_semaphore(s)
        self.outer = outer

    def close(self):
        self.outer.block_ctx, self.outer.done = self.block_ctx, self.done
        self.outer.ctx.push(self.ctx.pop_all())


def mm3(pe, out, lhs, rhs, first, last):
    pe.matmul(out, lhs[0], rhs[0], start=first, stop=False)
    pe.matmul(out, lhs[1], rhs[0], start=False, stop=False)
    return pe.matmul(out, lhs[0], rhs[1], start=False, stop=last)


def norm_part(st, b, res, src, weight, src_dram=None):
    AH, AL, ident, PS = res.AH, res.AL, res.ident, res.PS
    if src is None:
        src = st.sb("src", [P, TILES, D])
    sq = st.sb("sq", [P, D])
    ms = st.sb("ms", [P, TILES])
    mse = st.sb("mse", [P, TILES])
    rs = st.sb("rs", [P, TILES])
    wcol = st.sb("wcol", [P, KC])
    xn = st.sb("xn", [P, TILES, D])
    w_in_ = st.sem("weight_loaded")
    x_in = st.sem("rows_loaded")
    ssq = st.sem("squares_summed")
    m_ok = st.sem("mean_ready")
    r_ok = st.sem("rsqrt_ready")
    n_ok = st.sem("rows_scaled")
    t_ok = st.sem("chunk_transposed")
    h_ok = st.sem("hi_written")
    l_ok = st.sem("lo_written")

    @b.sync
    def _(sp):
        sp.dma_start(wcol[:], weight.rearrange("(k p) -> p k", p=P)).then_inc(w_in_, 16)
        if src_dram is not None:
            for t in range(TILES):
                sp.dma_start(src[:, t, :], src_dram[t]).then_inc(x_in, 16)

    @b.scalar
    def _(act):
        if src_dram is not None:
            act.wait_ge(x_in, 16 * TILES)
        for t in range(TILES):
            act.activation(sq[:], src[:, t, :], ACT.Square, accum_out=ms[:, t:t + 1]).then_inc(ssq, 1)
            act.wait_ge(ssq, t + 1)
        act.wait_ge(w_in_, 16)
        for k in range(KC):
            act.wait_ge(t_ok, k + 1)
            act.activation(AH[:, k, :], PS[:, k % 4, :], ACT.Copy, scale=wcol[:, k:k + 1]).then_inc(h_ok, 1)

    @b.gpsimd
    def _(pool):
        pool.wait_ge(m_ok, 1)
        pool.tensor_tensor(rs[:], mse[:], res.mhalf[:, 0:TILES], ALU.pow).then_inc(r_ok, 1)

    @b.vector
    def _(dve):
        dve.wait_ge(ssq, TILES)
        dve.tensor_scalar(mse[:], ms[:], 1.0 / D, EPS, ALU.mult, ALU.add).then_inc(m_ok, 1)
        dve.wait_ge(r_ok, 1)
        for t in range(TILES):
            dve.tensor_scalar(xn[:, t, :], src[:, t, :], rs[:, t:t + 1], None, ALU.mult).then_inc(n_ok, 1)
        dve.wait_ge(w_in_, 16)
        for k in range(KC):
            dve.wait_ge(h_ok, k + 1)
            dve.scalar_tensor_tensor(out=AL[:, k, :], in0=PS[:, k % 4, :], scalar=wcol[:, k:k + 1],
                                     in1=AH[:, k, :].bitcast(F32), op0=ALU.mult,
                                     op1=ALU.subtract).then_inc(l_ok, 1)

    @b.tensor
    def _(pe):
        pe.wait_ge(n_ok, TILES)
        for k in range(KC):
            if k >= 4:
                pe.wait_ge(l_ok, k - 3)
            for t in range(TILES):
                i = pe.transpose(PS[:, k % 4, t * P:(t + 1) * P], xn[:, t, k * P:(k + 1) * P], ident[:])
            i.then_inc(t_ok, 1)


def project_part(st, b, res, w, parts, tail=None):
    AH, AL, PS, X = res.AH, res.AL, res.PS, res.X
    KH = KC // 2
    raw = st.sb("raw", [P, 2, KH, CHUNK])
    hi = st.sb("hi", [P, 2, KH, CHUNK], F32R)
    lo = st.sb("lo", [P, 2, KH, CHUNK], F32R)
    w_in_ = [st.sem(f"half{i}_loaded") for i in range(2)]
    h_ok = st.sem("hi_written")
    l_ok = st.sem("lo_written")
    mm = st.sem("bank_accumulated")
    ev = st.sem("bank_evacuated")
    if tail is not None:
        tw, tcol, tout = tail
        NT = tout.shape[2]
        traw = st.sb("traw", [P, KC, NT])
        thi = st.sb("thi", [P, KC, NT], F32R)
        tlo = st.sb("tlo", [P, KC, NT], F32R)
        t_in = st.sem("tail_loaded")
        th_ok = st.sem("tail_hi")
        tl_ok = st.sem("tail_lo")
        t_mm = st.sem("tail_accumulated")
    base = [sum(p[0] for p in parts[:i]) for i in range(len(parts))]
    total = sum(p[0] for p in parts)

    def w_half(job, col0, kh):
        return w.rearrange("(k p) n -> p k n", p=P)[:, kh * KH:(kh + 1) * KH, bass.ds(job * CHUNK + col0, CHUNK)]

    @b.sync
    def _(sp):
        if tail is not None:
            sp.dma_start(traw[:], tw.rearrange("(k p) n -> p k n", p=P)[:, :, tcol:tcol + NT]).then_inc(t_in, 16)
        for (jobs, col0, _, _), j0 in zip(parts, base):
            def load(job, n):
                for kh in range(2):
                    if n is not None:
                        sp.wait_ge(l_ok, 2 * n + kh - 1)
                    sp.dma_start(raw[:, kh], w_half(job, col0, kh)).then_inc(w_in_[kh], 16)
            first = 0
            if j0 == 0:
                load(0, None)
                first = 1
            if jobs > first:
                with sp.Fori(first, jobs) as job:
                    load(job, job + j0)

    @b.scalar
    def _(act):
        if tail is not None:
            act.wait_ge(t_in, 16)
            act.copy(thi[:], traw[:]).then_inc(th_ok, 1)

        def split(n, again):
            for kh in range(2):
                act.wait_ge(w_in_[kh], 16 * (n + 1))
                if again:
                    act.wait_ge(mm, 8 * n - 4 + 4 * kh)
                act.copy(hi[:, kh], raw[:, kh]).then_inc(h_ok, 1)

        split(0, False)
        with act.Fori(1, total) as n:
            split(n, True)

    @b.vector
    def _(dve):
        if tail is not None:
            dve.wait_ge(th_ok, 1)
            dve.tensor_tensor(tlo[:], traw[:], thi[:].bitcast(F32), ALU.subtract).then_inc(tl_ok, 1)

        def split(c, kh):
            dve.wait_ge(h_ok, c + 1)
            dve.tensor_tensor(lo[:, kh], raw[:, kh], hi[:, kh].bitcast(F32), ALU.subtract).then_inc(l_ok, 1)

        def evacuate(n, job, out):
            for k in range(4):
                dve.wait_ge(mm, 8 * n + 5 + k)
                if out is None:
                    dst = X[:, k, bass.ds(job * CHUNK, CHUNK)]
                    dve.tensor_tensor(dst, PS[:, k, :], dst, ALU.add).then_inc(ev, 1)
                else:
                    dve.tensor_copy(out(job, k), PS[:, k, :]).then_inc(ev, 1)

        split(0, 0)
        split(1, 1)
        for i, ((jobs, _, _, out), j0) in enumerate(zip(parts, base)):
            inner = jobs if i < len(parts) - 1 else jobs - 1
            if inner:
                with dve.Fori(0, inner) as job:
                    n = job + j0
                    split(2 * n + 2, 0)
                    evacuate(n, job, out)
                    split(2 * n + 3, 1)
            if inner < jobs:
                evacuate(total - 1, jobs - 1, out)
        if tail is not None:
            dve.wait_ge(t_mm, 1)
            dve.tensor_copy(tout, PS[:, 4, 0:TILES * NT].rearrange("p (t n) -> p t n", n=NT)).then_inc(ev, 1)

    @b.tensor
    def _(pe):
        def product(n, token_major, again):
            for kh in range(2):
                pe.wait_ge(l_ok, 2 * n + kh + 1)
                for k in range(4):
                    if again and kh == 0:
                        pe.wait_ge(ev, 4 * n - 3 + k)
                    for i in range(KH):
                        kk = kh * KH + i
                        wide = slice(0, TOK)
                        tile = slice(k * P, (k + 1) * P)
                        if token_major:
                            lhs, rhs = (AH[:, kk, tile], AL[:, kk, tile]), (hi[:, kh, i, :], lo[:, kh, i, :])
                        else:
                            lhs, rhs = (hi[:, kh, i, tile], lo[:, kh, i, tile]), (AH[:, kk, wide], AL[:, kk, wide])
                        ins = mm3(pe, PS[:, k, :], lhs, rhs, kk == 0, kk == KC - 1)
                    ins.then_inc(mm, 1)

        for (jobs, _, token_major, _), j0 in zip(parts, base):
            first = 0
            if j0 == 0:
                product(0, token_major, False)
                first = 1
            if jobs > first:
                with pe.Fori(first, jobs) as job:
                    product(job + j0, token_major, True)
        if tail is not None:
            pe.wait_ge(tl_ok, 1)
            for t in range(TILES):
                for k in range(KC):
                    s = slice(t * P, (t + 1) * P)
                    ins = mm3(pe, PS[:, 4, t * NT:(t + 1) * NT], (AH[:, k, s], AL[:, k, s]),
                              (thi[:, k, :], tlo[:, k, :]), k == 0, k == KC - 1)
            ins.then_inc(t_mm, 1)


def merge_part(st, b, res, O, center, gain, per_head, SG, sg, k0):
    AH, AL, ident, PS = res.AH, res.AL, res.ident, res.PS
    R = TILES * HEADS
    tmp = st.sb("tmp", [P, R, P])
    cen = st.sb("cen", [P, R, P])
    s1 = st.sb("s1", [P, R])
    s2 = st.sb("s2", [P, R])
    rs = st.sb("rs", [P, R])
    gcol = st.sb("gcol", [P, HEADS])
    prod = st.sb("prod", [P, 2, TOK])
    g_in = st.sem("gain_loaded")
    step = st.sem("vector_step")
    sqd = st.sem("squared")
    sgd = st.sem("gate_ready")
    r_ok = st.sem("rsqrt_ready")
    t_ok = st.sem("head_transposed")
    p_ok = st.sem("product_ready")
    h_ok = st.sem("hi_written")
    l_ok = st.sem("lo_written")
    o = O[:].rearrange("p t h e -> p (t h) e")

    def lo(dve, h):
        dve.wait_ge(h_ok, h + 1)
        dve.tensor_tensor(AL[:, k0 + h, :], prod[:, h % 2, :], AH[:, k0 + h, :].bitcast(F32),
                          ALU.subtract).then_inc(l_ok, 1)

    @b.sync
    def _(sp):
        if per_head:
            sp.dma_start(gcol[:], gain.rearrange("(h p) -> p h", p=P)).then_inc(g_in, 16)
        else:
            for h in range(HEADS):
                sp.dma_start(gcol[:, h:h + 1], gain.rearrange("(p o) -> p o", o=1)).then_inc(g_in, 16)

    @b.scalar
    def _(act):
        act.activation(SG[:, sg], SG[:, sg], ACT.Silu).then_inc(sgd, 1)
        if center:
            act.wait_ge(step, 3)
        act.activation(tmp[:], cen[:] if center else o, ACT.Square).then_inc(sqd, 1)
        for h in range(HEADS):
            act.wait_ge(p_ok, h + 1)
            act.copy(AH[:, k0 + h, :], prod[:, h % 2, :]).then_inc(h_ok, 1)

    @b.gpsimd
    def _(pool):
        pool.wait_ge(step, 5 if center else 2)
        pool.tensor_tensor(rs[:], s2[:], res.mhalf[:, 0:R], ALU.pow).then_inc(r_ok, 1)

    @b.vector
    def _(dve):
        n = 0
        if center:
            dve.tensor_reduce(s1[:], o, AX.X, ALU.add).then_inc(step, 1)
            dve.wait_ge(step, 1)
            dve.tensor_scalar(s1[:], s1[:], 1.0 / P, None, ALU.mult).then_inc(step, 1)
            dve.wait_ge(step, 2)
            dve.tensor_tensor(cen[:], o, s1[:, :, None].broadcast_to([P, R, P]), ALU.subtract).then_inc(step, 1)
            n = 3
        dve.wait_ge(sqd, 1)
        dve.tensor_reduce(s2[:], tmp[:], AX.X, ALU.add).then_inc(step, 1)
        dve.wait_ge(step, n + 1)
        dve.tensor_scalar(s2[:], s2[:], 1.0 / P, EPS, ALU.mult, ALU.add).then_inc(step, 1)
        dve.wait_ge(r_ok, 1)
        dve.wait_ge(sqd, 1)
        dve.tensor_tensor(tmp[:], cen[:] if center else o, rs[:, :, None].broadcast_to([P, R, P]),
                          ALU.mult).then_inc(step, 1)
        dve.wait_ge(g_in, 16 if per_head else 16 * HEADS)
        dve.wait_ge(sgd, 1)
        for h in range(HEADS):
            dve.wait_ge(t_ok, h + 1)
            if h >= 2:
                dve.wait_ge(h_ok, h - 1)
                dve.wait_ge(l_ok, h - 1)
            dve.scalar_tensor_tensor(out=prod[:, h % 2, :], in0=PS[:, h, :], scalar=gcol[:, h:h + 1],
                                     in1=SG[:, sg, h, :], op0=ALU.mult, op1=ALU.mult).then_inc(p_ok, 1)
            if h >= 1:
                lo(dve, h - 1)
        lo(dve, HEADS - 1)

    @b.tensor
    def _(pe):
        pe.wait_ge(step, 6 if center else 3)
        for h in range(HEADS):
            for t in range(TILES):
                ins = pe.transpose(PS[:, h, t * P:(t + 1) * P], tmp[:, t * HEADS + h, :], ident[:])
            ins.then_inc(t_ok, 1)


def retention_stage(nc, res, tok, Oret):
    ident, PS = res.ident, res.PS
    UNITS = [(s, h) for s in range(N_SEQ) for h in range(HEADS)]
    with Stage(nc, "ret") as st:
        cs = st.sb("cos_sin", [P, 2, 2, 64])
        dec = st.sb("decay", [P, HEADS, 2, SEQ])
        rot = st.sb("rotated", [P, 2, TILES, HEADS, 64, 2])
        ta = st.sb("ta", [P, 2, HEADS, 64])
        tb = st.sb("tb", [P, 2, HEADS, 64])
        tc = st.sb("tc", [P, 2, HEADS, 64])
        td = st.sb("td", [P, 2, HEADS, 64])
        qk = st.sb("qk_T", [P, len(UNITS), 2, SEQ])
        sc = st.sb("scores", [P, len(UNITS), 2, SEQ])
        c_in = st.sem("tables_loaded")
        mul = st.sem("rotary_products")
        rt = st.sem("tile_rotated")
        qt = st.sem("qk_transposed")
        qc = st.sem("qk_copied")
        sm = st.sem("scores_done")
        sd = st.sem("scores_decayed")
        om = st.sem("output_done")
        oc = st.sem("output_copied")
        b = st.block()

        @b.sync
        def _(sp):
            sp.dma_start(cs[:], res.c_rot).then_inc(c_in, 16)
            sp.dma_start(dec[:], res.c_dec).then_inc(c_in, 16)

        @b.vector
        def _(dve):
            dve.wait_ge(c_in, 32)
            for t in range(TILES):
                x = tok[:, 0:2, t, :].rearrange("p j (h d two) -> p j h d two", h=HEADS, two=2)
                shape = [P, 2, HEADS, 64]
                cos = cs[:, t % 2, 0, :][:, None, None, :].broadcast_to(shape)
                sin = cs[:, t % 2, 1, :][:, None, None, :].broadcast_to(shape)
                if t:
                    dve.wait_ge(rt, 2 * t)
                dve.tensor_tensor(ta[:], x[:, :, :, :, 0], cos, ALU.mult).then_inc(mul, 1)
                dve.tensor_tensor(tb[:], x[:, :, :, :, 1], sin, ALU.mult).then_inc(mul, 1)
                dve.tensor_tensor(tc[:], x[:, :, :, :, 0], sin, ALU.mult).then_inc(mul, 1)
                dve.tensor_tensor(td[:], x[:, :, :, :, 1], cos, ALU.mult).then_inc(mul, 1)
                dve.wait_ge(mul, 4 * t + 4)
                dve.tensor_tensor(rot[:, :, t, :, :, 0], ta[:], tb[:], ALU.subtract).then_inc(rt, 1)
                dve.tensor_tensor(rot[:, :, t, :, :, 1], tc[:], td[:], ALU.add).then_inc(rt, 1)
            for u, (s, h) in enumerate(UNITS):
                dve.wait_ge(sm, u + 1)
                dve.tensor_tensor(sc[:, u], PS[:, 2 + u % 2, :].rearrange("p (a i) -> p a i", a=2), dec[:, h],
                                  ALU.mult).then_inc(sd, 1)

        @b.scalar
        def _(act):
            n = len(UNITS)
            for i in range(n + 2):
                if i < n:
                    act.wait_ge(qt, i + 1)
                    act.copy(qk[:, i], PS[:, i % 2, :].rearrange("p (a i) -> p a i", a=2)).then_inc(qc, 1)
                if i >= 2:
                    u = i - 2
                    s, h = UNITS[u]
                    act.wait_ge(om, u + 1)
                    act.copy(Oret[:, 2 * s:2 * s + 2, h, :],
                             PS[:, 4 + u % 4, 0:2 * P].rearrange("p (c e) -> p c e", c=2)).then_inc(oc, 1)

        @b.tensor
        def _(pe):
            def turn(u):
                s, h = UNITS[u]
                if u >= 2:
                    pe.wait_ge(qc, u - 1)
                for j in range(2):
                    for c in range(2):
                        src = rot[:, j, 2 * s + c, h].rearrange("p d two -> p (d two)")
                        i = pe.transpose(PS[:, u % 2, (2 * j + c) * P:(2 * j + c + 1) * P], src, ident[:])
                i.then_inc(qt, 1)

            def scores(u):
                pe.wait_ge(qc, u + 1)
                if u >= 2:
                    pe.wait_ge(sd, u - 1)
                for jc in range(2):
                    i = pe.matmul(PS[:, 2 + u % 2, jc * SEQ:(jc + 1) * SEQ], qk[:, u, 1, jc * P:(jc + 1) * P],
                                  qk[:, u, 0, :], start=True, stop=True)
                i.then_inc(sm, 1)

            def output(u):
                s, h = UNITS[u]
                pe.wait_ge(sd, u + 1)
                if u >= 4:
                    pe.wait_ge(oc, u - 3)
                for ic in range(2):
                    for jc in range(2):
                        i = pe.matmul(PS[:, 4 + u % 4, ic * P:(ic + 1) * P], sc[:, u, jc, ic * P:(ic + 1) * P],
                                      tok[:, 2, 2 * s + jc, h * P:(h + 1) * P], start=jc == 0, stop=jc == 1)
                i.then_inc(om, 1)

            pe.wait_ge(rt, 2 * TILES)
            n = len(UNITS)
            for u in range(n + 2):
                if u < n:
                    turn(u)
                if 1 <= u <= n:
                    scores(u - 1)
                if u >= 2:
                    output(u - 2)


def conv_stage(nc, res, conv_w, raw, small, gates, a_log, dt_bias):
    G = HEADS * DIRS
    with Stage(nc, "conv") as st:
        wc = st.sb("taps", [P, 3, 12])
        y = st.sb("y", [P, 3, TOK])
        al = st.sb("a_log", [P, G])
        dtb = st.sb("dt_bias", [P, G])
        ea = st.sb("ea", [P, G])
        x = st.sb("x", [P, TILES, G])
        ax = st.sb("ax", [P, TILES, G])
        e = st.sb("e", [P, TILES, G])
        u = st.sb("u", [P, TILES, G])
        ln = st.sb("ln", [P, TILES, G])
        c = st.sb("c", [P, TILES, G])
        eb = st.sb("eb", [P, TILES, G])
        w_in_ = st.sem("taps_loaded")
        a_in = st.sem("gate_weights_loaded")
        mid = st.sem("middle_tap")
        side = st.sem("side_taps")
        done = st.sem("silu_done")
        gs = st.sem("gate_vector_step")
        ga = st.sem("gate_scalar_step")
        b = st.block()

        @b.sync
        def _(sp):
            for j in range(3):
                sp.dma_start(wc[:, j, :], conv_w[j].rearrange("(n p) -> p n", p=P)).then_inc(w_in_, 16)
            sp.dma_start(al[:], a_log.partition_broadcast(P)).then_inc(a_in, 16)
            sp.dma_start(dtb[:], dt_bias.partition_broadcast(P)).then_inc(a_in, 16)

        def silu(act, n):
            act.wait_ge(side, 2 * n + 2)
            act.activation(raw[:, n // 4, n % 4, :], y[:, n % 3, :], ACT.Silu).then_inc(done, 1)

        @b.scalar
        def _(act):
            act.wait_ge(a_in, 32)
            act.activation(ea[:], al[:], ACT.Exp).then_inc(ga, 1)
            act.activation(eb[:], small[:, :, 0:G], ACT.Exp, scale=-1.0).then_inc(ga, 1)
            act.wait_ge(gs, 2)
            act.activation(e[:], ax[:], ACT.Exp, scale=-1.0).then_inc(ga, 1)
            act.wait_ge(gs, 4)
            act.activation(ln[:], u[:], ACT.Ln).then_inc(ga, 1)
            act.wait_ge(w_in_, 48)
            for n in range(12):
                if n >= 3:
                    act.wait_ge(done, n - 2)
                act.activation(y[:, n % 3, :], raw[:, n // 4, n % 4, :], ACT.Copy, scale=wc[:, 1, n:n + 1]).then_inc(mid, 1)
                if n >= 1:
                    silu(act, n - 1)
            silu(act, 11)

        @b.vector
        def _(dve):
            step = 0

            def link(ins):
                nonlocal step
                step += 1
                ins.then_inc(gs, 1)
                dve.wait_ge(gs, step)

            dve.wait_ge(a_in, 32)
            link(dve.tensor_tensor(x[:], small[:, :, G:2 * G], dtb[:, None, :].broadcast_to([P, TILES, G]), ALU.add))
            link(dve.scalar_tensor_tensor(out=ax[:], in0=x[:], scalar=-1.0, in1=x[:], op0=ALU.mult, op1=ALU.max))
            dve.wait_ge(ga, 3)
            link(dve.tensor_scalar(x[:], x[:], 0.0, None, ALU.max))
            link(dve.tensor_scalar(u[:], e[:], 1.0, None, ALU.add))
            link(dve.tensor_scalar(c[:], u[:], -1.0, None, ALU.add))
            link(dve.tensor_tensor(c[:], e[:], c[:], ALU.subtract))
            dve.wait_ge(ga, 4)
            link(dve.reciprocal(u[:], u[:]))
            link(dve.tensor_tensor(c[:], c[:], u[:], ALU.mult))
            link(dve.tensor_tensor(c[:], c[:], ln[:], ALU.add))
            link(dve.tensor_tensor(c[:], c[:], x[:], ALU.add))
            link(dve.tensor_tensor(c[:], c[:], ea[:, None, :].broadcast_to([P, TILES, G]), ALU.mult))
            link(dve.tensor_scalar(gates[:, 1], c[:], -1.0, None, ALU.mult))
            link(dve.tensor_scalar(eb[:], eb[:], 1.0, None, ALU.add))
            link(dve.reciprocal(gates[:, 0], eb[:]))
            dve.wait_ge(w_in_, 48)
            for n in range(12):
                dve.wait_ge(mid, n + 1)
                yy = y[:, n % 3, :].rearrange("p (s t) -> p s t", s=N_SEQ)
                xx = raw[:, n // 4, n % 4, :].rearrange("p (s t) -> p s t", s=N_SEQ)
                dve.scalar_tensor_tensor(out=yy[:, :, 1:], in0=xx[:, :, :-1], scalar=wc[:, 0, n:n + 1],
                                         in1=yy[:, :, 1:], op0=ALU.mult, op1=ALU.add).then_inc(side, 1)
                dve.wait_ge(side, 2 * n + 1)
                dve.scalar_tensor_tensor(out=yy[:, :, :-1], in0=xx[:, :, 1:], scalar=wc[:, 2, n:n + 1],
                                         in1=yy[:, :, :-1], op0=ALU.mult, op1=ALU.add).then_inc(side, 1)


def unit_stage(nc, res, raw, tokm):
    ident, PS = res.ident, res.PS
    N = 2 * HEADS
    with Stage(nc, "unit") as st:
        sq = st.sb("sq", [P, TILES, N, P])
        ss = st.sb("ss", [P, TILES, N])
        rs = st.sb("rs", [P, TILES, N])
        t_ok = st.sem("tile_transposed")
        c_ok = st.sem("tile_copied")
        sqd = st.sem("squared")
        step = st.sem("vector_step")
        r_ok = st.sem("rsqrt_ready")
        b_ok = st.sem("head_transposed_back")
        bc = st.sem("head_copied")
        b = st.block()

        @b.tensor
        def _(pe):
            for t in range(TILES):
                for j in range(3):
                    n = 3 * t + j
                    if n >= 6:
                        pe.wait_ge(c_ok, n - 5)
                    for h in range(HEADS):
                        i = pe.transpose(PS[:, n % 6, h * P:(h + 1) * P], raw[:, j, h, t * P:(t + 1) * P], ident[:])
                    i.then_inc(t_ok, 1)
            pe.wait_ge(step, 4)
            for n in range(N):
                if n >= 2:
                    pe.wait_ge(bc, n - 1)
                for t in range(TILES):
                    i = pe.transpose(PS[:, 6 + n % 2, t * P:(t + 1) * P],
                                     tokm[:, t, n // HEADS, (n % HEADS) * P:(n % HEADS + 1) * P], ident[:])
                i.then_inc(b_ok, 1)

        @b.scalar
        def _(act):
            for n in range(3 * TILES):
                act.wait_ge(t_ok, n + 1)
                act.copy(tokm[:, n // 3, n % 3, :], PS[:, n % 6, :]).then_inc(c_ok, 1)
            act.wait_ge(c_ok, 3 * TILES)
            for t in range(TILES):
                act.activation(sq[:, t], tokm[:, t, 0:2].rearrange("p j (h e) -> p (j h) e", e=P),
                               ACT.Square).then_inc(sqd, 1)
            for n in range(N):
                act.wait_ge(b_ok, n + 1)
                act.copy(raw[:, n // HEADS, n % HEADS, :], PS[:, 6 + n % 2, :]).then_inc(bc, 1)

        @b.gpsimd
        def _(pool):
            pool.wait_ge(step, 2)
            pool.tensor_tensor(rs[:], ss[:], res.mhalf[:, 0:TILES * N].rearrange("p (t n) -> p t n", n=N),
                               ALU.pow).then_inc(r_ok, 1)

        @b.vector
        def _(dve):
            dve.wait_ge(sqd, TILES)
            dve.tensor_reduce(ss[:], sq[:], AX.X, ALU.add).then_inc(step, 1)
            dve.wait_ge(step, 1)
            dve.tensor_scalar(ss[:], ss[:], EPS, None, ALU.add).then_inc(step, 1)
            dve.wait_ge(r_ok, 1)
            dve.tensor_scalar(rs[:, :, 0:HEADS], rs[:, :, 0:HEADS], P ** -0.5, None, ALU.mult).then_inc(step, 1)
            dve.wait_ge(step, 3)
            v = tokm[:, :, 0:2, :].rearrange("p t j (h e) -> p t (j h) e", e=P)
            for t in range(TILES):
                i = dve.tensor_tensor(v[:, t], v[:, t], rs[:, t, :, None].broadcast_to([P, N, P]), ALU.mult)
            i.then_inc(step, 1)


def first_tile(s, d):
    return 2 * s + d


def second_tile(s, d):
    return 2 * s + 1 - d


def delta_stage(nc, res, raw, tokm, gates, Ogdn):
    ident, PS = res.ident, res.PS
    NB = TILES * DIRS
    H4 = [P, HEADS, P]
    qn, kn = raw[:, 0], raw[:, 1]

    def heads(ap):
        return ap.rearrange("p (h i) -> p h i", h=HEADS)

    def bank(n):
        return heads(PS[:, n, :])

    with Stage(nc, "dlta") as st:
        tri = st.sb("tri", [P, DIRS, P])
        lm = st.sb("level_masks", [P, DIRS, LEVELS, P])
        lmc = st.sb("level_mask", [P, DIRS, P])
        T = st.sb("T", [P, NB] + H4[1:])
        TT = st.sb("TT", [P, NB] + H4[1:])
        MT = st.sb("MT", [P, NB] + H4[1:])
        QK = st.sb("QK", [P, NB] + H4[1:])
        qd = st.sb("q_decayed", [P, 4] + H4[1:])
        ring = st.sb("ring", [P, 2] + H4[1:])
        gcc = st.sb("g_cumulative", [P, DIRS, TILES, HEADS])
        glast = st.sb("g_last", [P, TILES, DIRS, HEADS])
        kt = st.sb("tail_factor", [P, DIRS, TILES, HEADS])
        kg = st.sb("key_factor", [P, DIRS, TILES, HEADS])
        eg = st.sb("exp_g", [P, DIRS, TILES, HEADS])
        c_in = st.sem("masks_loaded")
        gm = st.sem("gate_sums_done")
        gcp = st.sem("gate_sums_copied")
        gst = st.sem("gate_factor_step")
        rows = st.sem("rows_ready")
        kk = st.sem("products_ready")
        df = st.sem("differences_ready")
        ex = st.sem("decay_ready")
        xg = st.sem("row_exponential_ready")
        br = st.sem("beta_row_copied")
        em = st.sem("decay_masked")
        ebm = st.sem("decay_times_beta")
        fin = st.sem("batch_matrices_ready")
        m0 = st.sem("first_level_masked")
        t0 = st.sem("first_inverse_ready")
        b = st.block()

        @b.sync
        def _(sp):
            sp.dma_start(tri[:], res.c_tri).then_inc(c_in, 16)
            sp.dma_start(lm[:], res.c_lm).then_inc(c_in, 16)

        def second(n):
            t, d = n // DIRS, n % DIRS
            return t == second_tile(t // 2, d)

        seconds = [n for n in range(NB) if second(n)]

        def banks(n):
            return (1, 2, 3, 4) if n % 2 == 0 else (5, 6, 7, 0)

        @b.tensor
        def _(pe):
            pe.wait_ge(c_in, 32)
            for d in range(DIRS):
                pe.matmul(PS[:, 0, d * 16:(d + 1) * 16], tri[:, d, :],
                          gates[:, 1].rearrange("p t (d h) -> p t d h", d=DIRS)[:, :, d, :], start=True, stop=True)
            pe.matmul(PS[:, 0, 32:64], res.ones[:], gates[:, 1], start=True, stop=True).then_inc(gm, 1)
            for n in range(NB):
                t, d = n // DIRS, n % DIRS
                b1, b2, b3, b4 = banks(n)
                if n == 1:
                    pe.wait_ge(gcp, 2)
                if n >= 2:
                    pe.wait_ge(fin, n - 1)
                for h in range(HEADS):
                    g = gates[:, 1, t, d * HEADS + h:d * HEADS + h + 1].broadcast_to([P, P])
                    be = gates[:, 0, t, d * HEADS + h:d * HEADS + h + 1].broadcast_to([P, P])
                    pe.matmul(PS[:, b1, h * P:(h + 1) * P], g, tri[:, d, :], start=True, stop=True)
                    i = pe.matmul(PS[:, b2, h * P:(h + 1) * P], be, ident[:], start=True, stop=True)
                i.then_inc(rows, 1)
                for h in range(HEADS):
                    s = slice(t * P, (t + 1) * P)
                    pe.matmul(PS[:, b3, h * P:(h + 1) * P], kn[:, h, s], kn[:, h, s], start=True, stop=True)
                    i = pe.matmul(PS[:, b4, h * P:(h + 1) * P], kn[:, h, s], qn[:, h, s], start=True, stop=True)
                i.then_inc(kk, 1)

        @b.scalar
        def _(act):
            act.wait_ge(gcp, 2)
            act.activation(eg[:], gcc[:], ACT.Exp).then_inc(gst, 1)
            act.wait_ge(gst, 2)
            act.activation(kt[:], kt[:], ACT.Exp).then_inc(gst, 1)
            for n in range(NB):
                act.wait_ge(rows, n + 1)
                if second(n):
                    if n > seconds[0]:
                        act.wait_ge(fin, n)
                    act.wait_ge(df, 2 * n + 1)
                    act.activation(ring[:, 0], bank(banks(n)[0]), ACT.Exp).then_inc(xg, 1)
                act.copy(TT[:, n], bank(banks(n)[1])).then_inc(br, 1)
                act.wait_ge(df, 2 * n + 2)
                act.activation(T[:, n], T[:, n], ACT.Exp).then_inc(ex, 1)

        @b.gpsimd
        def _(pool):
            def first_level(n):
                pool.wait_ge(fin, n + 1)
                pool.tensor_tensor(T[:, n], MT[:, n], lm[:, n % DIRS, 0, None, :].broadcast_to(H4), ALU.mult).then_inc(m0, 1)

            pool.wait_ge(c_in, 32)
            for n in range(NB):
                d = n % DIRS
                if n:
                    first_level(n - 1)
                pool.wait_ge(ex, n + 1)
                pool.tensor_tensor(T[:, n], T[:, n], tri[:, d, None, :].broadcast_to(H4), ALU.mult).then_inc(em, 1)
                pool.wait_ge(br, n + 1)
                pool.wait_ge(em, n + 1)
                pool.tensor_tensor(TT[:, n], TT[:, n], T[:, n], ALU.mult).then_inc(ebm, 1)
            first_level(NB - 1)

        @b.vector
        def _(dve):
            dve.wait_ge(gm, 1)
            dve.tensor_copy(gcc[:].rearrange("p d t h -> p (d t h)"), PS[:, 0, 0:32]).then_inc(gcp, 1)
            dve.tensor_copy(glast[:].rearrange("p t d h -> p (t d h)"), PS[:, 0, 32:64]).then_inc(gcp, 1)
            dve.wait_ge(gcp, 2)
            dve.wait_ge(gst, 1)
            dve.tensor_tensor(kt[:], glast[:].rearrange("p t d h -> p d t h"), gcc[:], ALU.subtract).then_inc(gst, 1)
            dve.tensor_tensor(kg[:], gates[:, 0].rearrange("p t (d h) -> p d t h", d=DIRS), eg[:],
                              ALU.mult).then_inc(gcp, 1)

            def first_inverse(n):
                dve.wait_ge(m0, n + 1)
                dve.tensor_tensor(TT[:, n], ident[:, None, :].broadcast_to(H4), T[:, n], ALU.subtract).then_inc(t0, 1)

            for n in range(NB):
                t, d = n // DIRS, n % DIRS
                b1, _, b3, b4 = banks(n)
                dve.wait_ge(rows, n + 1)
                dve.tensor_tensor(T[:, n], bank(b1), gcc[:, d, t, :, None].broadcast_to(H4), ALU.subtract).then_inc(df, 1)
                dve.wait_ge(df, 2 * n + 1)
                dve.tensor_scalar(T[:, n], T[:, n], 0.0, None, ALU.min).then_inc(df, 1)
                if second(n):
                    dve.wait_ge(xg, seconds.index(n) + 1)
                    dve.tensor_tensor(qd[:, seconds.index(n)], qn[:, :, t * P:(t + 1) * P], ring[:, 0], ALU.mult)
                dve.wait_ge(kk, n + 1)
                dve.wait_ge(em, n + 1)
                dve.tensor_tensor(QK[:, n], bank(b4), T[:, n], ALU.mult)
                dve.wait_ge(ebm, n + 1)
                dve.tensor_tensor(MT[:, n], bank(b3), TT[:, n], ALU.mult).then_inc(fin, 1)
                if n:
                    first_inverse(n - 1)
            dve.wait_ge(fin, NB)
            first_inverse(NB - 1)

        inv = Inner(nc, st, "inv")
        RINGS = 2
        mk = inv.sem("level_masked")
        xm = inv.sem("x_done")
        xc = inv.sem("x_copied")
        ym = inv.sem("y_done")
        up = inv.sem("inverse_updated")
        lc = inv.sem("level_mask_copied")
        tt = inv.sem("first_inverse_turned")
        tc = inv.sem("first_inverse_copied")
        b = inv.block()
        LAST = LEVELS - 2

        def each_level(eng, level):
            with eng.Fori(0, LAST) as r:
                level(r, False)
            level(LAST, True)

        @b.gpsimd
        def _(pool):
            pool.sem_inc(mk, 1)

            def level(r, last):
                pool.wait_ge(mk, r * NB + 1)
                mask = lm[:, :, LAST + 1, :] if last else lm[:, :, bass.ds(r + 1, 1), :].squeeze(2)
                pool.tensor_copy(lmc[:], mask).then_inc(lc, 1)
                pool.wait_ge(lc, r + 1)
                for n in range(NB):
                    pool.wait_ge(xm, r * NB + n + 1)
                    pool.tensor_tensor(ring[:, n % RINGS], MT[:, n],
                                       lmc[:, n % DIRS, None, :].broadcast_to(H4), ALU.mult).then_inc(mk, 1)

            each_level(pool, level)

        xs = Ogdn[:, 0:2]

        @b.tensor
        def _(pe):
            pe.sem_inc(xm, RINGS)
            pe.sem_inc(ym, RINGS)
            for n in range(NB):
                for h in range(HEADS):
                    i = pe.transpose(PS[:, n, h * P:(h + 1) * P], TT[:, n, h, :], ident[:])
                i.then_inc(tt, 1)

            def level(r, last):
                def x(n):
                    pe.wait_ge(mk, r * NB + n + 2)
                    pe.wait_ge(xc, r * NB + n + 1)
                    pe.wait_ge(tc, NB)
                    pe.wait_ge(up, 2 * NB * r + 2 * n + 1)
                    for h in range(HEADS):
                        i = pe.matmul(PS[:, n % 2, h * P:(h + 1) * P], ring[:, n % RINGS, h, :], T[:, n, h, :],
                                      start=True, stop=True)
                    i.then_inc(xm, 1)

                def y(n):
                    pe.wait_ge(xc, r * NB + n + RINGS + 1)
                    if n < 3:
                        pe.wait_ge(up, 2 * NB * r + 2 * (NB - 1 - (NB - 1 - n) % 3) + 2)
                    else:
                        pe.wait_ge(up, 2 * NB * (r + 1) + (n - 2) * (1 if last else 2))
                    bk = 2 + 2 * (n % 3)
                    for h in range(HEADS):
                        if not last:
                            pe.matmul(PS[:, bk, h * P:(h + 1) * P], TT[:, n, h, :], xs[:, n % RINGS, h, :],
                                      start=True, stop=True)
                        i = pe.matmul(PS[:, bk + 1, h * P:(h + 1) * P], xs[:, n % RINGS, h, :], TT[:, n, h, :],
                                      start=True, stop=True)
                    i.then_inc(ym, 1)

                x(0)
                for n in range(1, NB):
                    x(n)
                    y(n - 1)
                y(NB - 1)

            each_level(pe, level)

        @b.scalar
        def _(act):
            act.sem_inc(xc, RINGS)
            for n in range(NB):
                act.wait_ge(tt, n + 1)
                act.copy(T[:, n], bank(n)).then_inc(tc, 1)

            def level(r, last):
                for n in range(NB):
                    act.wait_ge(xm, r * NB + n + RINGS + 1)
                    act.wait_ge(ym, r * NB + n + 1)
                    act.copy(xs[:, n % RINGS], bank(n % 2)).then_inc(xc, 1)

            each_level(act, level)

        @b.vector
        def _(dve):
            dve.sem_inc(up, 2 * NB)

            def level(r, last):
                for n in range(NB):
                    dve.wait_ge(ym, r * NB + n + RINGS + 1)
                    bk = 2 + 2 * (n % 3)
                    if not last:
                        dve.tensor_tensor(T[:, n], T[:, n], bank(bk), ALU.subtract).then_inc(up, 1)
                    dve.tensor_tensor(TT[:, n], TT[:, n], bank(bk + 1), ALU.subtract).then_inc(up, 1)

            each_level(dve, level)
        inv.close()

        out = Inner(nc, st, "dout")
        vb = MT
        kb = T
        NW = ring
        S = raw[:, 2].rearrange("p q (h e) -> p q h e", h=HEADS)
        SEQS = [(s, d) for s in range(N_SEQ) for d in range(DIRS)]
        scl = out.sem("operands_scaled")
        um = out.sem("first_values_done")
        uc = out.sem("first_values_copied")
        wm = out.sem("readers_done")
        wc = out.sem("readers_copied")
        sm = out.sem("state_done")
        scp = out.sem("state_copied")
        vm = out.sem("second_values_done")
        vc = out.sem("second_values_copied")
        om = out.sem("output_done")
        oc = out.sem("output_copied")
        b = out.block()

        def batch(t, d):
            return t * DIRS + d

        def tok(t, j):
            return heads(tokm[:, t, j, :])

        @b.vector
        def _(dve):
            for q, (s, d) in enumerate(SEQS):
                f, g = first_tile(s, d), second_tile(s, d)
                be = gates[:, 0, f, d * HEADS:(d + 1) * HEADS, None].broadcast_to(H4)
                dve.tensor_tensor(vb[:, batch(f, d)], tok(f, 2), be, ALU.mult).then_inc(scl, 1)
                dve.tensor_tensor(kb[:, 4 + q], tok(f, 1), kt[:, d, f, :, None].broadcast_to(H4), ALU.mult).then_inc(scl, 1)
                be = gates[:, 0, g, d * HEADS:(d + 1) * HEADS, None].broadcast_to(H4)
                dve.tensor_tensor(kb[:, q], tok(g, 1), kg[:, d, g, :, None].broadcast_to(H4), ALU.mult).then_inc(scl, 1)
                dve.tensor_tensor(vb[:, batch(g, d)], tok(g, 2), be, ALU.mult).then_inc(scl, 1)
            for q, (s, d) in enumerate(SEQS):
                dve.wait_ge(wm, q + 1)
                if q >= 2:
                    dve.wait_ge(vm, q - 1)
                dve.tensor_scalar(NW[:, q % 2], bank(1), -1.0, None, ALU.mult).then_inc(wc, 1)
                dve.wait_ge(vm, q + 1)
                dve.tensor_copy(vb[:, batch(second_tile(s, d), d)], bank(3)).then_inc(vc, 1)

        @b.scalar
        def _(act):
            for q, (s, d) in enumerate(SEQS):
                act.wait_ge(um, q + 1)
                act.copy(vb[:, batch(first_tile(s, d), d)], bank(0)).then_inc(uc, 1)
                act.wait_ge(sm, q + 1)
                act.copy(S[:, q], bank(2)).then_inc(scp, 1)
            for t in range(TILES):
                act.wait_ge(om, t + 1)
                act.copy(Ogdn[:, t], bank(4 + t)).then_inc(oc, 1)

        @b.tensor
        def _(pe):
            for q, (s, d) in enumerate(SEQS):
                f, g = first_tile(s, d), second_tile(s, d)
                pe.wait_ge(scl, 4 * q + 4)
                if q >= 1:
                    pe.wait_ge(uc, q)
                    pe.wait_ge(wc, q)
                    pe.wait_ge(scp, q)
                    pe.wait_ge(vc, q)
                for h in range(HEADS):
                    i = pe.matmul(PS[:, 0, h * P:(h + 1) * P], TT[:, batch(f, d), h, :], vb[:, batch(f, d), h, :],
                                  start=True, stop=True)
                i.then_inc(um, 1)
                for h in range(HEADS):
                    i = pe.matmul(PS[:, 1, h * P:(h + 1) * P], kb[:, q, h, :], TT[:, batch(g, d), h, :],
                                  start=True, stop=True)
                i.then_inc(wm, 1)
                pe.wait_ge(uc, q + 1)
                for h in range(HEADS):
                    i = pe.matmul(PS[:, 2, h * P:(h + 1) * P], kb[:, 4 + q, h, :], vb[:, batch(f, d), h, :],
                                  start=True, stop=True)
                i.then_inc(sm, 1)
                pe.wait_ge(wc, q + 1)
                pe.wait_ge(scp, q + 1)
                for h in range(HEADS):
                    o = PS[:, 3, h * P:(h + 1) * P]
                    pe.matmul(o, TT[:, batch(g, d), h, :], vb[:, batch(g, d), h, :], start=True, stop=False)
                    i = pe.matmul(o, NW[:, q % 2, h, :], S[:, q, h, :], start=False, stop=True)
                i.then_inc(vm, 1)
            pe.wait_ge(vc, len(SEQS))
            for t in range(TILES):
                s = t // 2
                d2 = [d for d in range(DIRS) if second_tile(s, d) == t][0]
                for h in range(HEADS):
                    o = PS[:, 4 + t, h * P:(h + 1) * P]
                    for d in range(DIRS):
                        pe.matmul(o, QK[:, batch(t, d), h, :], vb[:, batch(t, d), h, :], start=d == 0, stop=False)
                    i = pe.matmul(o, qd[:, seconds.index(batch(t, d2)), h, :], S[:, SEQS.index((s, d2)), h, :],
                                  start=False, stop=True)
                i.then_inc(om, 1)
        out.close()


def attention_part(st, b, res, qT, kT, v):
    AH, AL, ident, PS = res.AH, res.AL, res.ident, res.PS
    UNITS = [(s, h) for s in range(N_SEQ) for h in range(HEADS)]
    scale = XA_DH ** -0.5
    p = st.sb("probs", [P, 2, 2, SEQ])
    pT = st.sb("probs_T", [P, 2, 2, SEQ])
    mx = st.sb("max", [P, 2, 2])
    nm = st.sb("neg_max", [P, 2, 2])
    su = st.sb("sum", [P, 2, 2])
    ri = st.sb("inverse", [P, 2, 2])
    sm = st.sem("scores_done")
    ms = st.sem("max_step")
    ex = st.sem("exp_done")
    rs = st.sem("sum_inverted")
    nz = st.sem("probs_normalised")
    tm = st.sem("probs_turned")
    tcp = st.sem("probs_T_copied")
    om = st.sem("output_done")
    h_ok = st.sem("hi_written")
    l_ok = st.sem("lo_written")

    def dst(a, u):
        s, h = UNITS[u]
        return a[:, 2 * h:2 * h + 2, s * SEQ:(s + 1) * SEQ]

    def two(n):
        return PS[:, n, :].rearrange("p (a i) -> p a i", a=2)

    @b.tensor
    def _(pe):
        def scores(u):
            s, h = UNITS[u]
            if u >= 2:
                pe.wait_ge(ex, 2 * (u - 1))
            for t in range(2):
                for k in range(2):
                    i = pe.matmul(PS[:, u % 2, t * SEQ:(t + 1) * SEQ],
                                  qT[:, 2 * h + k, s * SEQ + t * P:s * SEQ + (t + 1) * P],
                                  kT[:, 2 * h + k, s * SEQ:(s + 1) * SEQ], start=k == 0, stop=k == 1)
            i.then_inc(sm, 1)

        def turn(u):
            pe.wait_ge(nz, 2 * u + 2)
            if u >= 2:
                pe.wait_ge(tcp, u - 1)
            for m in range(2):
                for t in range(2):
                    i = pe.transpose(PS[:, 2 + u % 2, m * SEQ + t * P:m * SEQ + (t + 1) * P],
                                     p[:, u % 2, t, m * P:(m + 1) * P], ident[:])
            i.then_inc(tm, 1)

        def output(u):
            s, h = UNITS[u]
            pe.wait_ge(tcp, u + 1)
            if u >= 2:
                pe.wait_ge(l_ok, u - 1)
            for e in range(2):
                for m in range(2):
                    i = pe.matmul(PS[:, 4 + u % 2, e * SEQ:(e + 1) * SEQ],
                                  v[:, 2 * s + m, h * XA_DH + e * P:h * XA_DH + (e + 1) * P],
                                  pT[:, u % 2, m, :], start=m == 0, stop=m == 1)
            i.then_inc(om, 1)

        n = len(UNITS)
        for u in range(n + 2):
            if u < n:
                scores(u)
            if 1 <= u <= n:
                turn(u - 1)
            if u >= 2:
                output(u - 2)

    @b.vector
    def _(dve):
        def low(u):
            dve.wait_ge(h_ok, u + 1)
            dve.tensor_tensor(dst(AL, u), two(4 + u % 2), dst(AH, u).bitcast(F32), ALU.subtract).then_inc(l_ok, 1)

        for u in range(len(UNITS)):
            dve.wait_ge(sm, u + 1)
            if u >= 2:
                dve.wait_ge(ex, 2 * (u - 1))
            dve.tensor_reduce(mx[:, u % 2], two(u % 2), AX.X, ALU.max).then_inc(ms, 1)
            dve.wait_ge(ms, 2 * u + 1)
            dve.tensor_scalar(nm[:, u % 2], mx[:, u % 2], -scale, None, ALU.mult).then_inc(ms, 1)
            dve.wait_ge(ex, 2 * u + 2)
            dve.reciprocal(ri[:, u % 2], su[:, u % 2]).then_inc(rs, 1)
            dve.wait_ge(rs, u + 1)
            for t in range(2):
                dve.tensor_scalar(p[:, u % 2, t], p[:, u % 2, t], ri[:, u % 2, t:t + 1], None, ALU.mult).then_inc(nz, 1)
            dve.wait_ge(tm, u + 1)
            dve.tensor_copy(pT[:, u % 2], two(2 + u % 2)).then_inc(tcp, 1)
            if u >= 1:
                low(u - 1)
        low(len(UNITS) - 1)

    @b.scalar
    def _(act):
        def high(u):
            act.wait_ge(om, u + 1)
            act.copy(dst(AH, u), two(4 + u % 2)).then_inc(h_ok, 1)

        for u in range(len(UNITS)):
            act.wait_ge(ms, 2 * u + 2)
            if u >= 2:
                act.wait_ge(tm, u - 1)
            for t in range(2):
                act.activation(p[:, u % 2, t], PS[:, u % 2, t * SEQ:(t + 1) * SEQ], ACT.Exp,
                               bias=nm[:, u % 2, t:t + 1], scale=scale,
                               accum_out=su[:, u % 2, t:t + 1]).then_inc(ex, 1)
            if u >= 1:
                high(u - 1)
        high(len(UNITS) - 1)


def select_stage(nc, res, qT, keys, SL):
    ident, PS = res.ident, res.PS
    HC = 2 * PH
    BLOCKS = [(a, max(a, 1), TOPK // (a + 1)) for a in (0, 1, 2, 4, 8)]
    ROW = [nb for _, na, nb in BLOCKS for _ in range(na)]
    START = [sum(ROW[:a]) for a in range(TOPK + 1)]
    NCAND = START[TOPK]
    SINGLE = BLOCKS[-1][0]
    with Stage(nc, "sel") as st:
        kraw = st.sb("keys", [P, HC, P])
        kTs = st.sb("keys_T", [P, HC, P])
        sc = st.sb("scores", [P, 2, HC, NKEYS])
        v1 = st.sb("top_values", [P, HC, TOPK])
        i1 = st.sb("top_indices", [P, HC, TOPK], U32)
        i1f = st.sb("top_indices_f", [P, 2, HC, TOPK])
        ca = st.sb("candidates", [P, PH, NCAND])
        tv = st.sb("best_values", [P, PH, TOPK])
        tp = st.sb("best_positions", [P, PH, TOPK], U32)
        pf = st.sb("best_positions_f", [P, SLOTS])
        past = st.sb("past_row_start", [P, 2, SINGLE, SLOTS])
        tail = st.sb("past_last_start", [P, SLOTS])
        abf = st.sb("position_ranks", [P, 2, SLOTS])
        eq = st.sb("eq", [P, 2, SLOTS, TOPK])
        out = st.sb("slots", [P, 3, SLOTS])
        ez = st.sb("gate_exp", [P, PH, TOPK])
        zs = st.sb("gate_sum", [P, PH])
        zi = st.sb("gate_inverse", [P, PH])
        k_in = [st.sem(f"keys{n}_loaded") for n in range(4)]
        kt_ = st.sem("keys_turned")
        kc = st.sem("keys_copied")
        sm = st.sem("scores_done")
        scp = st.sem("scores_copied")
        used = st.sem("scores_used")
        step = st.sem("vector_step")
        pos = st.sem("positions_ready")
        zr = st.sem("gate_exponents_ready")
        ge = st.sem("gate_exp_done")
        dec = st.sem("pool_step")
        rk = st.sem("ranks_ready")
        ma = st.sem("matches_ready")
        px = st.sem("matches_times_index")
        so = st.sem("slots_ready")
        tr = st.sem("slots_turned")
        tcp = st.sem("slots_copied")
        b = st.block()

        @b.sync
        def _(sp):
            for n in range(4):
                sp.dma_start(kraw[:, 4 * n:4 * n + 4, :],
                             keys[2 * n:2 * n + 2].rearrange("h c n d -> n (h c) d")).then_inc(k_in[n], 16)

        @b.tensor
        def _(pe):
            for n in range(4):
                pe.wait_ge(k_in[n], 16)
                for m in range(4):
                    i = pe.transpose(PS[:, n, m * P:(m + 1) * P], kraw[:, 4 * n + m, :], ident[:])
                i.then_inc(kt_, 1)

            def scores(t):
                for n in range(4):
                    if t == 0:
                        pe.wait_ge(kc, n + 1)
                    else:
                        pe.wait_ge(scp, 4 * (t - 1) + n + 1)
                    for m in range(4):
                        i = pe.matmul(PS[:, n, m * P:(m + 1) * P], qT[:, 4 * n + m, t * P:(t + 1) * P],
                                      kTs[:, 4 * n + m, :], start=True, stop=True)
                    i.then_inc(sm, 1)

            scores(0)
            scores(1)
            for t in range(TILES):
                if t + 2 < TILES:
                    scores(t + 2)
                pe.wait_ge(so, 3 * t + 3)
                if t >= 1:
                    pe.wait_ge(tcp, 2 * t)
                for j in range(3):
                    i = pe.transpose(PS[:, 4, j * P:(j + 1) * P], out[:, j, :], ident[:])
                i.then_inc(tr, 1)

        @b.scalar
        def _(act):
            for n in range(4):
                act.wait_ge(kt_, n + 1)
                act.copy(kTs[:, 4 * n:4 * n + 4, :].rearrange("p a n -> p (a n)"), PS[:, n, :]).then_inc(kc, 1)

            def scores(t):
                if t >= 2:
                    act.wait_ge(used, t - 1)
                for n in range(4):
                    act.wait_ge(sm, 4 * t + n + 1)
                    act.copy(sc[:, t % 2, 4 * n:4 * n + 4, :].rearrange("p a n -> p (a n)"), PS[:, n, :]).then_inc(scp, 1)

            scores(0)
            scores(1)
            for t in range(TILES):
                act.wait_ge(zr, t + 1)
                act.activation(ez[:], ez[:], ACT.Exp).then_inc(ge, 1)
                if t + 2 < TILES:
                    scores(t + 2)
                act.wait_ge(tr, t + 1)
                ts = slice(t * P, (t + 1) * P)
                act.copy(SL.idx[:, :, ts], PS[:, 4, 0:2 * P].rearrange("p (a t) -> p a t", a=2)).then_inc(tcp, 1)
                act.copy(SL.g[:, ts], PS[:, 4, 2 * P:3 * P]).then_inc(tcp, 1)

        @b.gpsimd
        def _(pool):
            n = 0

            def mark(ins):
                nonlocal n
                n += 1
                ins.then_inc(dec, 1)
                pool.wait_ge(dec, n)

            for t in range(TILES):
                pool.wait_ge(pos, t + 1)
                for r in range(SINGLE):
                    pool.tensor_scalar(past[:, 0, r, :], pf[:], float(START[r + 1]), None, ALU.is_ge)
                    pool.tensor_scalar(past[:, 1, r, :], pf[:], float(START[r + 1]), float(ROW[r]), ALU.is_ge, ALU.mult)
                mark(pool.tensor_scalar(tail[:], pf[:], -float(START[SINGLE]), 0.0, ALU.add, ALU.max))
                half = SINGLE // 2
                while half:
                    mark(pool.tensor_tensor(past[:, :, 0:half], past[:, :, 0:half], past[:, :, half:2 * half], ALU.add))
                    half //= 2
                if t >= 1:
                    pool.wait_ge(ma, 2 * t)
                mark(pool.tensor_tensor(past[:, :, 0], past[:, :, 0], tail[:, None, :].broadcast_to([P, 2, SLOTS]), ALU.add))
                pool.tensor_copy(abf[:, 0], past[:, 0, 0]).then_inc(rk, 1)
                pool.tensor_tensor(abf[:, 1], pf[:], past[:, 1, 0], ALU.subtract).then_inc(rk, 1)
                for c in range(2):
                    pool.wait_ge(ma, 2 * t + c + 1)
                    e4 = eq[:, c].rearrange("p (h k) a -> p h k a", h=PH)
                    ix = i1f[:, t % 2].rearrange("p (h c) k -> p h c k", c=2)[:, :, c, None, :]
                    pool.tensor_tensor(e4, e4, ix.broadcast_to([P, PH, TOPK, TOPK]), ALU.mult).then_inc(px, 1)

        @b.vector
        def _(dve):
            n = 0

            def mark(ins):
                nonlocal n
                n += 1
                ins.then_inc(step, 1)
                dve.wait_ge(step, n)

            def top16(values, count, top, index):
                for half in (slice(0, 8), slice(8, 16)):
                    for j in range(count):
                        i = dve.max(top[:, j, half], values[:, j, :])
                    mark(i)
                    for j in range(count):
                        i = dve.max_index(index[:, j, half], top[:, j, half], values[:, j, :])
                    mark(i)
                    if half.start == 0:
                        for j in range(count):
                            i = dve.match_replace(values[:, j, :], top[:, j, half], values[:, j, :], NEG)
                        mark(i)

            def rank_keys(t):
                dve.wait_ge(scp, 4 * t + 4)
                top16(sc[:, t % 2], HC, v1, i1)
                dve.tensor_copy(i1f[:, t % 2], i1[:]).then_inc(used, 1)

            def match(t):
                if t:
                    dve.wait_ge(so, 3 * t)
                for c in range(2):
                    dve.wait_ge(rk, 2 * t + c + 1)
                    dve.tensor_tensor(eq[:, c], abf[:, c, :, None].broadcast_to([P, SLOTS, TOPK]),
                                      res.iota[:, None, 0:TOPK].broadcast_to([P, SLOTS, TOPK]), ALU.is_equal).then_inc(ma, 1)
                dve.wait_ge(ge, t + 1)
                mark(dve.tensor_reduce(zs[:], ez[:], AX.X, ALU.add))
                mark(dve.reciprocal(zi[:], zs[:]))
                if t:
                    dve.wait_ge(tr, t)
                dve.tensor_tensor(out[:, 2, :].rearrange("p (h k) -> p h k", h=PH), ez[:],
                                  zi[:, :, None].broadcast_to([P, PH, TOPK]), ALU.mult).then_inc(so, 1)
                dve.wait_ge(so, 3 * t + 1)

            def rank_sums(t):
                vv = v1[:].rearrange("p (h c) k -> p h c k", c=2)
                for a0, na, nb in BLOCKS:
                    shape = [P, PH, na, nb]
                    i = dve.tensor_tensor(ca[:, :, START[a0]:START[a0 + na]].rearrange("p h (a b) -> p h a b", a=na),
                                          vv[:, :, 0, a0:a0 + na, None].broadcast_to(shape),
                                          vv[:, :, 1, None, 0:nb].broadcast_to(shape), ALU.add)
                mark(i)
                top16(ca, PH, tv, tp)
                dve.tensor_copy(pf[:], tp[:].rearrange("p h k -> p (h k)")).then_inc(pos, 1)
                dve.tensor_tensor(ez[:], tv[:], tv[:, :, 0:1].broadcast_to([P, PH, TOPK]), ALU.subtract).then_inc(zr, 1)

            def slots(t):
                for c in range(2):
                    dve.wait_ge(px, 2 * t + c + 1)
                    dve.tensor_reduce(out[:, c, :], eq[:, c], AX.X, ALU.add).then_inc(so, 1)

            rank_keys(0)
            rank_sums(0)
            for t in range(1, TILES):
                rank_keys(t)
                match(t - 1)
                rank_sums(t)
                slots(t - 1)
            match(TILES - 1)
            slots(TILES - 1)


BLK = 128


def gate_stage(nc, res, SL):
    PS = res.PS
    SUB = 4
    NR = 4
    BATCH = SUB * NR
    NBLK = TOK // BLK
    with Stage(nc, "gate") as st:
        oh = st.sb("one_hots", [P, NR, 2, SUB, P])
        gh = st.sb("gated_one_hots", [P, NR, SUB, P])
        gb = st.sb("block", [P, 2, P, BLK])
        ok = st.sem("one_hots_ready")
        gp = st.sem("gated_by_pool")
        ga = st.sem("gated_by_scalar")
        mm = st.sem("four_tokens_done")
        cp = st.sem("bank_free")
        so = [st.sem(f"block{i}_stored") for i in range(2)]
        b = st.block()

        def first(it, q):
            return it * BATCH + q * SUB

        @b.vector
        def _(dve):
            with dve.Fori(0, TOK // BATCH) as it:
                for q in range(NR):
                    dve.wait_ge(mm, it * NR + q + 1)
                    shape = [P, 2, SUB, P]
                    dve.tensor_tensor(oh[:, q], SL.idx[:, :, bass.ds(first(it, q), SUB)][:, :, :, None].broadcast_to(shape),
                                      res.iota[:, None, None, :].broadcast_to(shape), ALU.is_equal).then_inc(ok, 1)

        @b.gpsimd
        def _(pool):
            with pool.Fori(0, TOK // BATCH) as it:
                for q in range(0, NR, 2):
                    g = SL.g[:, bass.ds(first(it, q), SUB)][:, :, None].broadcast_to([P, SUB, P])
                    pool.wait_ge(ok, it * NR + q + 1)
                    pool.tensor_tensor(gh[:, q], oh[:, q, 1], g, ALU.mult).then_inc(gp, 1)

        @b.tensor
        def _(pe):
            pe.sem_inc(mm, NR)
            with pe.Fori(0, TOK // BATCH) as it:
                for q in range(NR):
                    if q % 2 == 0:
                        pe.wait_ge(gp, it * (NR // 2) + q // 2 + 1)
                    else:
                        pe.wait_ge(ga, it * (NR // 2) + q // 2 + 1)
                    pe.wait_ge(cp, it * NR + q + 1)
                    for k in range(SUB):
                        i = pe.matmul(PS[:, q, k * P:(k + 1) * P], gh[:, q, k, :], oh[:, q, 0, k, :],
                                      start=True, stop=True)
                    i.then_inc(mm, 1)

        @b.scalar
        def _(act):
            act.sem_inc(cp, NR)
            PER = BLK // BATCH

            def gate(it, q):
                act.wait_ge(ok, it * NR + q + 1)
                for k in range(SUB):
                    i = act.activation(gh[:, q, k, :], oh[:, q, 1, k, :], ACT.Copy,
                                       scale=SL.g[:, bass.ds(first(it, q) + k, 1)])
                i.then_inc(ga, 1)

            with act.Fori(0, NBLK // 2) as pair:
                for half in range(2):
                    act.wait_ge(so[half], 16 * pair + 16)
                    with act.Fori(0, PER) as r:
                        it = (pair * 2 + half) * PER + r
                        gate(it, 1)
                        for q in range(NR):
                            if q == 1:
                                gate(it, 3)
                            act.wait_ge(mm, it * NR + NR + q + 1)
                            act.copy(gb[:, half, :, bass.ds(r * BATCH + q * SUB, SUB)].rearrange("p i t -> p t i"),
                                     PS[:, q, :].rearrange("p (t i) -> p t i", t=SUB)).then_inc(cp, 1)

        @b.sync
        def _(sp):
            for half in range(2):
                sp.sem_inc(so[half], 16)
            with sp.Fori(0, NBLK // 2) as pair:
                for half in range(2):
                    sp.wait_ge(cp, NR + (pair * 2 + half + 1) * (BLK // SUB))
                    sp.dma_start(res.gates[:, :, bass.ds((pair * 2 + half) * BLK, BLK)].rearrange("a b t -> b a t"),
                                 gb[:, half]).then_inc(so[half], 16)
            for half in range(2):
                sp.wait_ge(so[half], 16 * (NBLK // 2 + 1))


def expert_stage(nc, res, U, V):
    AH, AL, ident, PS, X = res.AH, res.AL, res.ident, res.PS, res.X
    NT = NKEYS
    NG = NT // GROUP
    with Stage(nc, "exp") as st:
        ur = st.sb("u_raw", [P, 2, D])
        uh = st.sb("uT_hi", [P, 2, KC, P], F32R)
        ul = st.sb("uT_lo", [P, 2, KC, P], F32R)
        vr = st.sb("v_raw", [P, 2, D])
        vh = st.sb("v_hi", [P, GROUP, D], F32R)
        vl = st.sb("v_lo", [P, GROUP, D], F32R)
        gt = st.sb("gates", [P, GROUP, TOK])
        ag = st.sb("gelu", [P, 2, TOK])
        w = st.sb("w", [P, 2, TOK])
        wh = st.sb("w_hi", [P, GROUP, TOK], F32R)
        wl = st.sb("w_lo", [P, GROUP, TOK], F32R)
        u_in = [st.sem(f"u{i}_loaded") for i in range(2)]
        v_in = [st.sem(f"v{i}_loaded") for i in range(2)]
        g_in = [st.sem(f"gates{i}_loaded") for i in range(GROUP)]
        ut = st.sem("u_turned")
        uho = st.sem("uT_hi_written")
        ulo = st.sem("uT_lo_written")
        vho = st.sem("v_hi_written")
        vlo = st.sem("v_lo_written")
        am = st.sem("a_done")
        ge = st.sem("gelu_done")
        wo = st.sem("w_ready")
        who = st.sem("w_hi_written")
        wlo = st.sem("w_lo_written")
        om = st.sem("output_bank_done")
        ad = st.sem("output_bank_added")
        b = st.block()

        @b.sync
        def _(sp):
            def load_u(n, slot):
                sp.dma_start(ur[:, slot], U[bass.ds(n * P, P), :]).then_inc(u_in[slot], 16)

            def load_v(n, slot):
                sp.dma_start(vr[:, slot], V[bass.ds(n * P, P), :]).then_inc(v_in[slot], 16)

            def load_g(n, slot):
                sp.dma_start(gt[:, slot], res.gates[bass.ds(n, 1), :, :].rearrange("a b t -> (a b) t")).then_inc(g_in[slot], 16)

            for n in range(2):
                load_u(n, n)
                load_v(n, n)
            for n in range(GROUP):
                load_g(n, n)

            def ahead(g, e, last):
                n = g * GROUP + e
                sp.wait_ge(ut, n + 1)
                load_u(0 if last and e >= GROUP - 2 else n + 2, e % 2)
                if not (last and e >= GROUP - 2):
                    sp.wait_ge(vlo, n + 1)
                    load_v(n + 2, e % 2)
                if not last:
                    sp.wait_ge(wo, n + 3)
                    load_g(n + GROUP, e)

            with sp.Fori(0, NG - 1) as g:
                for e in range(GROUP):
                    ahead(g, e, False)
            for e in range(GROUP - 1):
                ahead(NG - 1, e, True)
            sp.wait_ge(u_in[0], 16 * (NT // 2 + 1))

        @b.tensor
        def _(pe):
            def turn(n, slot):
                pe.wait_ge(u_in[slot], (n - slot) * 8 + 16)
                for k in range(KC):
                    i = pe.transpose(PS[:, k // 4, (k % 4) * P:(k % 4 + 1) * P], ur[:, slot, k * P:(k + 1) * P], ident[:])
                i.then_inc(ut, 1)

            pe.sem_inc(am, 1)
            pe.sem_inc(om, 1)
            turn(0, 0)
            with pe.Fori(0, NG) as g:
                for e in range(GROUP):
                    n = g * GROUP + e
                    pe.wait_ge(ulo, n + 1)
                    turn(n + 1, (e + 1) % 2)
                    pe.wait_ge(ge, n + 1)
                    for k in range(KC):
                        i = mm3(pe, PS[:, 2 + e % 2, :], (uh[:, e % 2, k, :], ul[:, e % 2, k, :]),
                                (AH[:, k, :], AL[:, k, :]), k == 0, k == KC - 1)
                    i.then_inc(am, 1)
                for half in range(2):
                    cols = slice(half * CHUNK, (half + 1) * CHUNK)
                    for e in range(GROUP):
                        if half == 0:
                            pe.wait_ge(wlo, g * GROUP + e + 1)
                            pe.wait_ge(vlo, g * GROUP + e + 1)
                        for t in range(TILES):
                            if e == 0:
                                pe.wait_ge(ad, g * 8 + 4 * half + t + 1)
                            s = slice(t * P, (t + 1) * P)
                            i = mm3(pe, PS[:, 4 + t, :], (wh[:, e, s], wl[:, e, s]),
                                    (vh[:, e, cols], vl[:, e, cols]), e == 0, e == GROUP - 1)
                            if e == GROUP - 1:
                                i.then_inc(om, 1)

        def turned(n=None):
            return PS[:, 0:2, :].rearrange("p b (k e) -> p (b k) e", k=4)

        @b.scalar
        def _(act):
            act.sem_inc(ge, 2)

            def u_hi(n, slot):
                act.wait_ge(ut, n + 1)
                act.copy(uh[:, slot], turned()).then_inc(uho, 1)

            u_hi(0, 0)
            with act.Fori(0, NG) as g:
                for e in range(GROUP):
                    n = g * GROUP + e
                    act.wait_ge(v_in[e % 2], g * 32 + (e // 2) * 16 + 16)
                    if e == 0:
                        act.wait_ge(om, g * 8 + 1)
                    act.copy(vh[:, e], vr[:, e % 2]).then_inc(vho, 1)
                    act.wait_ge(am, n + 1)
                    u_hi(n + 1, (e + 1) % 2)
                    act.wait_ge(am, n + 2)
                    act.wait_ge(wo, n + 1)
                    act.activation(ag[:, e % 2], PS[:, 2 + e % 2, :], ACT.Gelu_apprx_tanh).then_inc(ge, 1)
                    act.wait_ge(wo, n + 3)
                    act.copy(wh[:, e], w[:, e % 2]).then_inc(who, 1)

        @b.vector
        def _(dve):
            dve.sem_inc(wo, 2)
            dve.sem_inc(ad, 4)

            def u_lo(n, slot):
                dve.wait_ge(uho, n + 1)
                dve.tensor_tensor(ul[:, slot], turned(), uh[:, slot].bitcast(F32), ALU.subtract).then_inc(ulo, 1)

            u_lo(0, 0)
            with dve.Fori(0, NG) as g:
                for e in range(GROUP):
                    n = g * GROUP + e
                    dve.wait_ge(vho, n + 1)
                    dve.tensor_tensor(vl[:, e], vr[:, e % 2], vh[:, e].bitcast(F32), ALU.subtract).then_inc(vlo, 1)
                    u_lo(n + 1, (e + 1) % 2)
                    dve.wait_ge(ge, n + 3)
                    dve.wait_ge(g_in[e], g * 16 + 16)
                    dve.tensor_tensor(w[:, e % 2], ag[:, e % 2], gt[:, e], ALU.mult).then_inc(wo, 1)
                    dve.wait_ge(who, n + 1)
                    dve.tensor_tensor(wl[:, e], w[:, e % 2], wh[:, e].bitcast(F32), ALU.subtract).then_inc(wlo, 1)
                for half in range(2):
                    for t in range(TILES):
                        dve.wait_ge(om, g * 8 + 4 * half + t + 2)
                        x = X[:, t, half * CHUNK:(half + 1) * CHUNK]
                        dve.tensor_tensor(x, PS[:, 4 + t, :], x, ALU.add).then_inc(ad, 1)


def final_stage(nc, res, weight, outs):
    X = res.X
    with Stage(nc, "final") as st:
        wb = st.sb("weight", [P, D])
        sq = st.sb("sq", [P, D])
        y = st.sb("y", [P, TILES, D])
        ms = st.sb("ms", [P, TILES])
        mse = st.sb("mse", [P, TILES])
        rs = st.sb("rs", [P, TILES])
        w_in_ = st.sem("weight_loaded")
        ssq = st.sem("squares_summed")
        m_ok = st.sem("mean_ready")
        r_ok = st.sem("rsqrt_ready")
        y_ok = st.sem("row_ready")
        stored = st.sem("stored")
        b = st.block()

        @b.sync
        def _(sp):
            sp.dma_start(wb[:], weight.partition_broadcast(P)).then_inc(w_in_, 16)
            for t in range(TILES):
                sp.wait_ge(y_ok, t + 1)
                sp.dma_start(outs[t // 2][0, (t % 2) * P:(t % 2 + 1) * P, :], y[:, t, :]).then_inc(stored, 16)
            sp.wait_ge(stored, 16 * TILES)

        @b.scalar
        def _(act):
            for t in range(TILES):
                act.activation(sq[:], X[:, t, :], ACT.Square, accum_out=ms[:, t:t + 1]).then_inc(ssq, 1)
                act.wait_ge(ssq, t + 1)

        @b.gpsimd
        def _(pool):
            pool.wait_ge(m_ok, 1)
            pool.tensor_tensor(rs[:], mse[:], res.mhalf[:, 0:TILES], ALU.pow).then_inc(r_ok, 1)

        @b.vector
        def _(dve):
            dve.wait_ge(ssq, TILES)
            dve.tensor_scalar(mse[:], ms[:], 1.0 / D, EPS, ALU.mult, ALU.add).then_inc(m_ok, 1)
            dve.wait_ge(r_ok, 1)
            dve.wait_ge(w_in_, 16)
            for t in range(TILES):
                dve.scalar_tensor_tensor(out=y[:, t, :], in0=X[:, t, :], scalar=rs[:, t:t + 1], in1=wb[:],
                                         op0=ALU.mult, op1=ALU.mult).then_inc(y_ok, 1)


class Resident:
    pass


class Slots:
    pass


def build(nc, a, outs, stop=None, depth=DEPTH):
    Stage.before = []
    res = Resident()
    with ExitStack() as ctx:
        ctx.enter_context(nc.allow_non_contiguous_dma(reason="per-partition vectors of a few values"))

        def sb(name, shape, dtype=F32):
            return ctx.enter_context(nc.sbuf_tensor(name, shape, dtype))

        res.X = sb("residual", [P, TILES, D])
        res.AH = sb("act_hi", [P, KC, TOK], F32R)
        res.AL = sb("act_lo", [P, KC, TOK], F32R)
        res.ident = sb("identity", [P, P])
        res.ones = sb("ones", [P, P])
        res.iota = sb("iota", [P, P])
        res.mhalf = sb("minus_half", [P, 32])
        res.PS = ctx.enter_context(nc.psum_tensor("banks", [P, 8, 512], F32))
        res.c_rot, res.c_dec, res.c_tri, res.c_lm = a["c_rot"], a["c_dec"], a["c_tri"], a["c_lm"]
        res.gates = nc.dram_tensor("dense_gates", [NKEYS, NKEYS, TOK], F32, kind="Internal").ap()

        with Stage(nc, "load") as st:
            x_in = st.sem("loaded")
            b = st.block()

            @b.sync
            def _(sp):
                for t in range(TILES):
                    src = a["x_prompt"] if t < 2 else a["x_sample"]
                    sp.dma_start(res.X[:, t, :], src[0, (t % 2) * P:(t % 2 + 1) * P, :]).then_inc(x_in, 16)
                sp.dma_start(res.ident[:], a["c_ident"]).then_inc(x_in, 16)
                sp.dma_start(res.iota[:], a["c_iota"].partition_broadcast(P)).then_inc(x_in, 16)
                sp.wait_ge(x_in, 16 * (TILES + 2))

            @b.gpsimd
            def _(pool):
                pool.memset(res.mhalf[:], -0.5)
                pool.memset(res.ones[:], 1.0)

        mems = [(a["mem_prompt"] if t < 2 else a["mem_sample"])[0, (t % 2) * P:(t % 2 + 1) * P, :] for t in range(TILES)]

        def layers(l):
            def of(name):
                return a[name][l]

            with ExitStack() as mix:
                SG = mix.enter_context(nc.sbuf_tensor("gate_rows", [P, 2, HEADS, TOK], F32))
                raw = mix.enter_context(nc.sbuf_tensor("delta_rows", [P, 3, HEADS, TOK], F32))
                small = mix.enter_context(nc.sbuf_tensor("small", [P, TILES, 16], F32))
                gates = mix.enter_context(nc.sbuf_tensor("delta_gates", [P, 2, TILES, 8], F32))
                O = mix.enter_context(nc.sbuf_tensor("mixer_out", [P, TILES, HEADS, P], F32))
                w_in = of("w_in")
                with ExitStack() as rt:
                    tok = rt.enter_context(nc.sbuf_tensor("ret_rows", [P, 3, TILES, CHUNK], F32))
                    with Stage(nc, "win") as st:
                        b = st.block()
                        norm_part(Part(st, "norm"), b, res, res.X, of("norm_mix"))
                        project_part(Part(st, "project"), b, res, w_in, [
                            (3, 0, True, lambda j, t: one(tok[:, bass.ds(j, 1), t, :])),
                            (1, 3 * CHUNK, False, lambda j, c: SG[:, 0, c, :]),
                            (3, 4 * CHUNK, False, lambda j, c: one(raw[:, bass.ds(j, 1), c, :])),
                            (1, 7 * CHUNK, False, lambda j, c: SG[:, 1, c, :]),
                        ], tail=(w_in, 8 * CHUNK, small[:]))
                    retention_stage(nc, res, tok, O)
                with Stage(nc, "mret") as st:
                    merge_part(Part(st, "merge"), st.block(), res, O, True, of("ret_norm"), True, SG, 0, 0)
                conv_stage(nc, res, of("gdn_conv"), raw, small, gates, of("gdn_a_log").rearrange("d h -> (d h)"),
                           of("gdn_dt_bias").rearrange("d h -> (d h)"))
                with ExitStack() as dl:
                    tokm = dl.enter_context(nc.sbuf_tensor("delta_tokens", [P, TILES, 3, CHUNK], F32))
                    unit_stage(nc, res, raw, tokm)
                    delta_stage(nc, res, raw, tokm, gates, O)
                with Stage(nc, "wout") as st:
                    b = st.block()
                    merge_part(Part(st, "merge"), b, res, O, False, of("gdn_norm"), False, SG, 1, HEADS)
                    project_part(Part(st, "project"), b, res, of("w_out"), [(2, 0, True, None)])
            if stop == "mix":
                return
            with ExitStack() as xa:
                kT = xa.enter_context(nc.sbuf_tensor("mem_keys", [P, KC, TOK], F32))
                v = xa.enter_context(nc.sbuf_tensor("mem_values", [P, TILES, D], F32))
                qT = xa.enter_context(nc.sbuf_tensor("xa_queries", [P, KC, TOK], F32))
                with Stage(nc, "wkv") as st:
                    b = st.block()
                    norm_part(Part(st, "norm"), b, res, None, of("norm_mem"), mems)
                    project_part(Part(st, "project"), b, res, of("w_xkv"), [
                        (2, 0, False, lambda j, c: one(kT[:, bass.ds(j * 4 + c, 1), :])),
                        (2, 2 * CHUNK, True, lambda j, t: v[:, t, bass.ds(j * CHUNK, CHUNK)]),
                    ])
                with Stage(nc, "wxq") as st:
                    b = st.block()
                    norm_part(Part(st, "norm"), b, res, res.X, of("norm_xa"))
                    project_part(Part(st, "project"), b, res, of("w_xq"),
                                 [(2, 0, False, lambda j, c: one(qT[:, bass.ds(j * 4 + c, 1), :]))])
                with Stage(nc, "wxo") as st:
                    b = st.block()
                    attention_part(Part(st, "attend"), b, res, qT, kT, v)
                    project_part(Part(st, "project"), b, res, of("w_xo"), [(2, 0, True, None)])
            if stop == "xa":
                return
            with ExitStack() as pf:
                SL = Slots()
                SL.idx = pf.enter_context(nc.sbuf_tensor("slot_keys", [P, 2, TOK], F32))
                SL.g = pf.enter_context(nc.sbuf_tensor("slot_gates", [P, TOK], F32))
                with ExitStack() as pq:
                    qT = pq.enter_context(nc.sbuf_tensor("peer_queries", [P, 2 * PH, TOK], F32))
                    with Stage(nc, "wpq") as st:
                        b = st.block()
                        norm_part(Part(st, "norm"), b, res, res.X, of("norm_ffn"))
                        project_part(Part(st, "project"), b, res, of("peer_wq"),
                                     [(4, 0, False, lambda j, c: one(qT[:, bass.ds(j * 4 + c, 1), :]))])
                    select_stage(nc, res, qT, of("peer_keys"), SL)
                gate_stage(nc, res, SL)
            expert_stage(nc, res, of("peer_u"), of("peer_v"))

        with nc.Fori(0, depth) as l:
            layers(l)
            with Stage(nc, "turn") as st:
                st.block()
        final_stage(nc, res, a["norm_final"], outs)
        with Stage(nc, "end") as st:
            st.block()


def one(ap):
    return ap.squeeze(1) if len(ap.shape) == 3 else ap


def tables():
    f = np.float32
    inv = (np.float32(10000.0) ** (-np.arange(0, P, 2, dtype=f) / f(P))).astype(f)
    ang = (np.arange(SEQ, dtype=f)[:, None] * inv[None, :]).astype(f).astype(np.float64)
    rot = np.stack([np.cos(ang), np.sin(ang)], 1).astype(f).reshape(2, P, 2, 64).transpose(1, 0, 2, 3)
    i = np.arange(SEQ)
    diff = (i[None, :] - i[:, None]).astype(np.float64)
    dec = np.zeros((HEADS, SEQ, SEQ))
    for h in range(HEADS):
        fwd, bwd = np.log1p(-2.0 ** (-5.0 - h)), np.log1p(-2.0 ** (-5.5 - h))
        dec[h] = np.where(diff >= 0, np.exp(fwd * np.abs(diff)), np.exp(bwd * np.abs(diff))) * P ** -0.5
    dec = dec.reshape(HEADS, 2, P, SEQ).transpose(2, 0, 1, 3).astype(f)
    j, k = np.arange(P)[:, None], np.arange(P)[None, :]
    tri = np.stack([j <= k, j >= k], 1).astype(f)
    lm = np.zeros((P, DIRS, LEVELS, P), f)
    for lev in range(LEVELS):
        s = 1 << lev
        pair = (j // (2 * s)) == (k // (2 * s))
        lm[:, 0, lev] = pair & (j // s % 2 == 0) & (k // s % 2 == 1)
        lm[:, 1, lev] = pair & (j // s % 2 == 1) & (k // s % 2 == 0)
    return {"c_rot": np.ascontiguousarray(rot), "c_dec": np.ascontiguousarray(dec), "c_tri": tri, "c_lm": lm,
            "c_ident": np.eye(P, dtype=f), "c_iota": np.arange(P, dtype=f)}


_INS = ["x_prompt", "x_sample", "mem_prompt", "mem_sample", "norm_mix", "w_in", "ret_norm", "gdn_conv", "gdn_a_log",
        "gdn_dt_bias", "gdn_norm", "w_out", "norm_xa", "norm_mem", "w_xq", "w_xkv", "w_xo", "norm_ffn", "peer_wq",
        "peer_keys", "peer_u", "peer_v", "norm_final"]


def kernel(**inputs):
    import concourse.bacc as _bacc
    from concourse.bass_utils import run_bass_kernel_spmd as _run

    nc = _bacc.Bacc("TRN2", target_bir_lowering=False, num_devices=1)
    arrays, args = {}, {}
    for name, x in [(n, np.ascontiguousarray(inputs[n])) for n in _INS] + list(tables().items()):
        arrays[f"in_{name}"] = x
        args[name] = nc.dram_tensor(f"in_{name}", x.shape, F32, kind="ExternalInput").ap()
    outs = [nc.dram_tensor(f"out_{i}", [1, SEQ, D], F32, kind="ExternalOutput").ap() for i in range(N_SEQ)]
    build(nc, args, outs)
    r = _run(nc, [arrays], core_ids=[0])
    return tuple(r.results[0][f"out_{i}"] for i in range(N_SEQ))
```

```python
from contextlib import ExitStack

import numpy as np

import concourse.bass as bass
from concourse import mybir

ALU = mybir.AluOpType
ACT = mybir.ActivationFunctionType
AX = mybir.AxisListType
F32 = mybir.dt.float32
F32R = mybir.dt.float32r
U32 = mybir.dt.uint32

P = 128
EPS = 1e-6
SEQ = 256
N_SEQ = 2
TILES = N_SEQ * SEQ // P
TOK = N_SEQ * SEQ
D = 1024
KC = D // P
DEPTH = 2
HEADS = 4
LEVELS = 7
XA_DH = 256
PH = 8
TOPK = 16
SLOTS = PH * TOPK
NKEYS = 128
GROUP = 4
CHUNK = 512
NEG = -3.0e38
DIRS = 2


class Stage:

    before = []

    def __init__(self, nc, name):
        self.nc, self.name, self.ctx, self.sems = nc, name, ExitStack(), []

    def __enter__(self):
        return self

    def sb(self, name, shape, dtype=F32):
        return self.ctx.enter_context(self.nc.sbuf_tensor(f"{self.name}_{name}", shape, dtype))

    def sem(self, name):
        s = self.nc.alloc_semaphore(f"{self.name}_{name}")
        self.sems.append(s)
        return s

    def block(self):
        done, Stage.before = Stage.before, self.sems
        self.block_ctx = self.nc.Block()
        b = self.block_ctx.__enter__()

        @b.gpsimd
        def _(pool):
            for s in done:
                pool.sem_clear(s)

        self.done = done
        return b

    def __exit__(self, *e):
        self.block_ctx.__exit__(*e)
        for s in self.done:
            self.nc.release_semaphore(s)
        self.ctx.__exit__(*e)
        return False


class Part:

    def __init__(self, stage, name):
        self.stage, self.name = stage, name

    def sb(self, name, shape, dtype=F32):
        return self.stage.sb(f"{self.name}_{name}", shape, dtype)

    def sem(self, name):
        return self.stage.sem(f"{self.name}_{name}")


class Inner(Stage):

    def __init__(self, nc, outer, name):
        super().__init__(nc, name)
        outer.block_ctx.__exit__(None, None, None)
        for s in outer.done:
            nc.release_semaphore(s)
        self.outer = outer

    def close(self):
        self.outer.block_ctx, self.outer.done = self.block_ctx, self.done
        self.outer.ctx.push(self.ctx.pop_all())


def mm3(pe, out, lhs, rhs, first, last):
    pe.matmul(out, lhs[0], rhs[0], start=first, stop=False)
    pe.matmul(out, lhs[1], rhs[0], start=False, stop=False)
    return pe.matmul(out, lhs[0], rhs[1], start=False, stop=last)


def load_part(st, b, *loads):
    loaded = st.sem("loaded")

    @b.sync
    def _(sp):
        for buffer, source in loads:
            sp.dma_start(buffer, source).then_inc(loaded, 16)
        sp.wait_ge(loaded, 16 * len(loads))


class Weights:

    def __init__(self, part):
        self.raw = part.sb("raw", [P, 2, KC // 2, CHUNK])
        self.hi = part.sb("hi", [P, 2, KC // 2, CHUNK], F32R)
        self.lo = part.sb("lo", [P, 2, KC // 2, CHUNK], F32R)
        self.loaded = [part.sem(f"half{i}_loaded") for i in range(2)]
        self.h_ok = part.sem("hi_written")
        self.l_ok = part.sem("lo_written")
        self.acts = None
        self.between = None

    def first_hi(self, act):
        for kh in range(2):
            act.wait_ge(self.loaded[kh], 16)
            act.copy(self.hi[:, kh], self.raw[:, kh]).then_inc(self.h_ok, 1)

    def first_lo(self, eng, halves=(0, 1)):
        for kh in halves:
            eng.wait_ge(self.h_ok, kh + 1)
            if kh == 1 and len(halves) == 1:
                eng.wait_ge(self.l_ok, 1)
            eng.tensor_tensor(self.lo[:, kh], self.raw[:, kh], self.hi[:, kh].bitcast(F32),
                              ALU.subtract).then_inc(self.l_ok, 1)


def norm_part(st, b, res, src, weight, ahead, src_dram=None):
    AH, AL, ident, PS = res.AH, res.AL, res.ident, res.PS
    if src is None:
        src = st.sb("src", [P, TILES, D])
    sq = st.sb("sq", [P, D])
    ms = st.sb("ms", [P, TILES])
    mse = st.sb("mse", [P, TILES])
    rs = st.sb("rs", [P, TILES])
    wcol = st.sb("wcol", [P, KC])
    xn = st.sb("xn", [P, TILES, D])
    LAST = TILES - 1
    w_in_ = st.sem("weight_loaded")
    x_in = st.sem("rows_loaded")
    ssq = st.sem("squares_summed")
    last = st.sem("last_tile_step")
    m_ok = st.sem("mean_ready")
    r_ok = st.sem("rsqrt_ready")
    n_ok = st.sem("rows_scaled")
    t_ok = st.sem("chunk_transposed")
    h_ok = st.sem("hi_written")
    l_ok = st.sem("lo_written")

    @b.sync
    def _(sp):
        sp.dma_start(wcol[:], weight.rearrange("(k p) -> p k", p=P)).then_inc(w_in_, 16)
        if src_dram is not None:
            for t in range(TILES):
                sp.dma_start(src[:, t, :], src_dram[t]).then_inc(x_in, 16)

    @b.scalar
    def _(act):
        if src_dram is not None:
            act.wait_ge(x_in, 16 * TILES)
        for t in range(LAST):
            act.activation(sq[:], src[:, t, :], ACT.Square, accum_out=ms[:, t:t + 1]).then_inc(ssq, 1)
            act.wait_ge(ssq, t + 1)
        act.wait_ge(r_ok, 1)
        act.activation(xn[:, LAST, :], src[:, LAST, :], ACT.Copy, scale=rs[:, LAST:TILES]).then_inc(n_ok, 1)
        ahead.first_hi(act)
        act.wait_ge(w_in_, 16)
        for k in range(KC):
            act.wait_ge(t_ok, k + 1)
            act.activation(AH[:, k, :], PS[:, 4 + k % 4, :], ACT.Copy, scale=wcol[:, k:k + 1]).then_inc(h_ok, 1)

    @b.gpsimd
    def _(pool):
        pool.wait_ge(m_ok, 1)
        pool.tensor_tensor(rs[:], mse[:], res.mhalf[:, 0:TILES], ALU.pow).then_inc(r_ok, 1)
        ahead.first_lo(pool)

    @b.vector
    def _(dve):
        if src_dram is not None:
            dve.wait_ge(x_in, 16 * TILES)
        dve.tensor_tensor(xn[:, LAST, :], src[:, LAST, :], src[:, LAST, :], ALU.mult).then_inc(last, 1)
        dve.wait_ge(last, 1)
        dve.tensor_reduce(ms[:, LAST:TILES], xn[:, LAST, :], AX.X, ALU.add).then_inc(last, 1)
        dve.wait_ge(last, 2)
        dve.wait_ge(ssq, LAST)
        dve.tensor_scalar(mse[:], ms[:], 1.0 / D, EPS, ALU.mult, ALU.add).then_inc(m_ok, 1)
        dve.wait_ge(r_ok, 1)
        for t in range(LAST):
            dve.tensor_scalar(xn[:, t, :], src[:, t, :], rs[:, t:t + 1], None, ALU.mult).then_inc(n_ok, 1)
        dve.wait_ge(w_in_, 16)
        for k in range(KC):
            dve.wait_ge(h_ok, k + 1)
            dve.scalar_tensor_tensor(out=AL[:, k, :], in0=PS[:, 4 + k % 4, :], scalar=wcol[:, k:k + 1],
                                     in1=AH[:, k, :].bitcast(F32), op0=ALU.mult,
                                     op1=ALU.subtract).then_inc(l_ok, 1)

    @b.tensor
    def _(pe):
        pe.wait_ge(n_ok, TILES)
        for k in range(KC):
            if k >= 4:
                pe.wait_ge(l_ok, k - 3)
            for t in range(TILES):
                i = pe.transpose(PS[:, 4 + k % 4, t * P:(t + 1) * P], xn[:, t, k * P:(k + 1) * P], ident[:])
            i.then_inc(t_ok, 1)

    ahead.acts = [(l_ok, KC // 2), (l_ok, KC)]


def project_part(st, b, res, weights, w, parts, tail=None):
    AH, AL, PS, X = res.AH, res.AL, res.PS, res.X
    KH = KC // 2
    raw, hi, lo = weights.raw, weights.hi, weights.lo
    w_in_, h_ok, l_ok = weights.loaded, weights.h_ok, weights.l_ok
    mm = st.sem("bank_accumulated")
    ev = st.sem("bank_evacuated")
    if tail is not None:
        tw, tcol, tout = tail
        NT = tout.shape[2]
        traw = st.sb("traw", [P, KC, NT])
        thi = st.sb("thi", [P, KC, NT], F32R)
        tlo = st.sb("tlo", [P, KC, NT], F32R)
        t_in = st.sem("tail_loaded")
        th_ok = st.sem("tail_hi")
        tl_ok = st.sem("tail_lo")
        tT = st.sb("tail_feature_major", [NT, TOK])
        t_mm = st.sem("tail_accumulated")
        t_cp = st.sem("tail_copied")
        t_tr = st.sem("tail_turned")
    base = [sum(p[0] for p in parts[:i]) for i in range(len(parts))]
    total = sum(p[0] for p in parts)

    def w_half(job, col0, kh):
        return w.rearrange("(k p) n -> p k n", p=P)[:, kh * KH:(kh + 1) * KH, bass.ds(job * CHUNK + col0, CHUNK)]

    @b.sync
    def _(sp):
        if tail is not None:
            sp.dma_start(traw[:], tw.rearrange("(k p) n -> p k n", p=P)[:, :, tcol:tcol + NT]).then_inc(t_in, 16)
        for (jobs, col0, _, _), j0 in zip(parts, base):
            def load(job, n):
                for kh in range(2):
                    if n is not None:
                        sp.wait_ge(l_ok, 2 * n + kh - 1)
                    sp.dma_start(raw[:, kh], w_half(job, col0, kh)).then_inc(w_in_[kh], 16)
            first = 0
            if j0 == 0:
                load(0, None)
                first = 1
            if jobs > first:
                with sp.Fori(first, jobs) as job:
                    load(job, job + j0)

    @b.scalar
    def _(act):
        if tail is not None:
            act.wait_ge(t_in, 16)
            act.copy(thi[:], traw[:]).then_inc(th_ok, 1)

        with act.Fori(1, total) as n:
            for kh in range(2):
                act.wait_ge(w_in_[kh], 16 * (n + 1))
                act.wait_ge(mm, 8 * n - 4 + 4 * kh)
                act.copy(hi[:, kh], raw[:, kh]).then_inc(h_ok, 1)

    @b.vector
    def _(dve):
        if tail is not None:
            dve.wait_ge(th_ok, 1)
            dve.tensor_tensor(tlo[:], traw[:], thi[:].bitcast(F32), ALU.subtract).then_inc(tl_ok, 1)

        def split(c, kh):
            dve.wait_ge(h_ok, c + 1)
            dve.tensor_tensor(lo[:, kh], raw[:, kh], hi[:, kh].bitcast(F32), ALU.subtract).then_inc(l_ok, 1)

        def evacuate(n, job, out):
            for k in range(4):
                dve.wait_ge(mm, 8 * n + 5 + k)
                if out is None:
                    dst = X[:, k, bass.ds(job * CHUNK, CHUNK)]
                    dve.tensor_tensor(dst, PS[:, k, :], dst, ALU.add).then_inc(ev, 1)
                else:
                    dve.tensor_copy(out(job, k), PS[:, k, :]).then_inc(ev, 1)

        dve.wait_ge(l_ok, 2)
        for i, ((jobs, _, _, out), j0) in enumerate(zip(parts, base)):
            inner = jobs if i < len(parts) - 1 else jobs - 1
            if inner:
                with dve.Fori(0, inner) as job:
                    n = job + j0
                    split(2 * n + 2, 0)
                    evacuate(n, job, out)
                    split(2 * n + 3, 1)
            if inner < jobs:
                evacuate(total - 1, jobs - 1, out)
        if tail is not None:
            dve.wait_ge(t_mm, 1)
            dve.tensor_copy(tT[:], PS[0:NT, 4, :]).then_inc(t_cp, 1)
            dve.wait_ge(t_tr, 1)
            dve.tensor_copy(tout, PS[:, 5, 0:TILES * NT].rearrange("p (t n) -> p t n", n=NT)).then_inc(ev, 1)

    @b.tensor
    def _(pe):
        def product(n, token_major, again):
            for kh in range(2):
                pe.wait_ge(l_ok, 2 * n + kh + 1)
                if not again and weights.acts[kh]:
                    pe.wait_ge(*weights.acts[kh])
                for k in range(4):
                    if not again and kh == 0 and k == 2 and weights.between:
                        weights.between(pe)
                    if again and kh == 0:
                        pe.wait_ge(ev, 4 * n - 3 + k)
                    for i in range(KH):
                        kk = kh * KH + i
                        wide = slice(0, TOK)
                        tile = slice(k * P, (k + 1) * P)
                        if token_major:
                            lhs, rhs = (AH[:, kk, tile], AL[:, kk, tile]), (hi[:, kh, i, :], lo[:, kh, i, :])
                        else:
                            lhs, rhs = (hi[:, kh, i, tile], lo[:, kh, i, tile]), (AH[:, kk, wide], AL[:, kk, wide])
                        ins = mm3(pe, PS[:, k, :], lhs, rhs, kk == 0, kk == KC - 1)
                    ins.then_inc(mm, 1)

        for (jobs, _, token_major, _), j0 in zip(parts, base):
            first = 0
            if j0 == 0:
                product(0, token_major, False)
                first = 1
            if jobs > first:
                with pe.Fori(first, jobs) as job:
                    product(job + j0, token_major, True)
        if tail is not None:
            pe.wait_ge(tl_ok, 1)
            for k in range(KC):
                ins = mm3(pe, PS[0:NT, 4, :], (thi[:, k, :], tlo[:, k, :]), (AH[:, k, :], AL[:, k, :]),
                          k == 0, k == KC - 1)
            ins.then_inc(t_mm, 1)
            pe.wait_ge(t_cp, 1)
            for t in range(TILES):
                ins = pe.transpose(PS[:, 5, t * NT:(t + 1) * NT], tT[:, t * P:(t + 1) * P], res.ident[0:NT, 0:NT])
            ins.then_inc(t_tr, 1)


def merge_part(st, b, res, O, gain, gate, ahead):
    AH, AL, ident, PS = res.AH, res.AL, res.ident, res.PS
    R = TILES * HEADS
    tmp = st.sb("tmp", [P, R, P])
    s2 = st.sb("s2", [P, R])
    rs = st.sb("rs", [P, R])
    gcol = st.sb("gcol", [P, 1])
    prod = st.sb("prod", [P, 2, TOK])
    g_in = st.sem("gain_loaded")
    step = st.sem("vector_step")
    sqd = st.sem("squared")
    sgd = st.sem("gate_ready")
    r_ok = st.sem("rsqrt_ready")
    t_ok = st.sem("head_transposed")
    p_ok = st.sem("product_ready")
    h_ok = st.sem("hi_written")
    l_ok = st.sem("lo_written")
    o = O[:].rearrange("p t h e -> p (t h) e")

    @b.sync
    def _(sp):
        sp.dma_start(gcol[:], gain.rearrange("(p o) -> p o", o=1)).then_inc(g_in, 16)

    @b.scalar
    def _(act):
        act.activation(tmp[:], o, ACT.Square).then_inc(sqd, 1)
        ahead.first_hi(act)
        act.activation(gate, gate, ACT.Silu).then_inc(sgd, 1)
        for h in range(HEADS):
            act.wait_ge(p_ok, h + 1)
            act.copy(AH[:, HEADS + h, :], prod[:, h % 2, :]).then_inc(h_ok, 1)

    @b.gpsimd
    def _(pool):
        pool.wait_ge(step, 2)
        pool.tensor_tensor(rs[:], s2[:], res.mhalf[:, 0:R], ALU.pow).then_inc(r_ok, 1)
        ahead.first_lo(pool, (1,))

    @b.vector
    def _(dve):
        def lo(h):
            dve.wait_ge(h_ok, h + 1)
            dve.tensor_tensor(AL[:, HEADS + h, :], prod[:, h % 2, :], AH[:, HEADS + h, :].bitcast(F32),
                              ALU.subtract).then_inc(l_ok, 1)

        dve.wait_ge(sqd, 1)
        dve.tensor_reduce(s2[:], tmp[:], AX.X, ALU.add).then_inc(step, 1)
        dve.wait_ge(step, 1)
        dve.tensor_scalar(s2[:], s2[:], 1.0 / P, EPS, ALU.mult, ALU.add).then_inc(step, 1)
        ahead.first_lo(dve, (0,))
        dve.wait_ge(r_ok, 1)
        dve.tensor_tensor(tmp[:], o, rs[:, :, None].broadcast_to([P, R, P]), ALU.mult).then_inc(step, 1)
        dve.wait_ge(g_in, 16)
        dve.wait_ge(sgd, 1)
        for h in range(HEADS):
            dve.wait_ge(t_ok, h + 1)
            if h >= 2:
                dve.wait_ge(h_ok, h - 1)
                dve.wait_ge(l_ok, h - 1)
            dve.scalar_tensor_tensor(out=prod[:, h % 2, :], in0=PS[:, 4 + h, :], scalar=gcol[:, 0:1],
                                     in1=gate[:, h, :], op0=ALU.mult, op1=ALU.mult).then_inc(p_ok, 1)
            if h >= 1:
                lo(h - 1)
        lo(HEADS - 1)

    def turn_heads(pe):
        pe.wait_ge(step, 3)
        for h in range(HEADS):
            for t in range(TILES):
                ins = pe.transpose(PS[:, 4 + h, t * P:(t + 1) * P], tmp[:, t * HEADS + h, :], ident[:])
            ins.then_inc(t_ok, 1)

    ahead.acts, ahead.between = [None, (l_ok, HEADS)], turn_heads


def retention_conv_stage(nc, res, cs, dec, tok, Oret, conv_w, raw, small, gates, a_log, dt_bias):
    ident, PS = res.ident, res.PS
    UNITS = [(s, h) for s in range(N_SEQ) for h in range(HEADS)]
    NU = len(UNITS)
    ROWS = 3 * HEADS
    G = HEADS * DIRS
    with Stage(nc, "retc") as st:
        rot = st.sb("rotated", [P, 2, TILES, HEADS, 64, 2])
        ta = st.sb("ta", [P, 2, HEADS, 64])
        tb = st.sb("tb", [P, 2, HEADS, 64])
        tc = st.sb("tc", [P, 2, HEADS, 64])
        td = st.sb("td", [P, 2, HEADS, 64])
        qk = st.sb("qk_T", [P, 2, 2, SEQ])
        sc = st.sb("scores", [P, 2, 2, SEQ])
        mul = st.sem("rotary_products_vector")
        pmul = st.sem("rotary_products_pool")
        rt = st.sem("tile_rotated_vector")
        rp = st.sem("tile_rotated_pool")
        qt = st.sem("qk_transposed")
        qc = st.sem("qk_copied")
        sm = st.sem("scores_done")
        sd = st.sem("scores_decayed")
        om = st.sem("output_done")
        oc = st.sem("output_copied")
        wc = st.sb("taps", [P, 3, ROWS])
        y = st.sb("y", [P, 3, TOK])
        al = st.sb("a_log", [P, G])
        dtb = st.sb("dt_bias", [P, G])
        ea = st.sb("ea", [P, G])
        x = st.sb("x", [P, TILES, G])
        ax = st.sb("ax", [P, TILES, G])
        e = st.sb("e", [P, TILES, G])
        u1 = st.sb("u", [P, TILES, G])
        ln = st.sb("ln", [P, TILES, G])
        c = st.sb("c", [P, TILES, G])
        eb = st.sb("eb", [P, TILES, G])
        w_in_ = st.sem("taps_loaded")
        a_in = st.sem("gate_weights_loaded")
        mid = st.sem("middle_tap")
        side = st.sem("side_taps")
        done = st.sem("silu_done")
        gs = st.sem("gate_vector_step")
        ga = st.sem("gate_scalar_step")
        b = st.block()

        @b.sync
        def _(sp):
            sp.dma_start(al[:], a_log.partition_broadcast(P)).then_inc(a_in, 16)
            sp.dma_start(dtb[:], dt_bias.partition_broadcast(P)).then_inc(a_in, 16)
            for j in range(3):
                sp.dma_start(wc[:, j, :], conv_w[j].rearrange("(n p) -> p n", p=P)).then_inc(w_in_, 16)

        def rotate(eng, t, half, swapped, a, bb, op, products, done):
            v = tok[:, 0:2, t, :].rearrange("p j (h d two) -> p j h d two", h=HEADS, two=2)
            shape = [P, 2, HEADS, 64]
            cos = cs[:, t % 2, 0, :][:, None, None, :].broadcast_to(shape)
            sin = cs[:, t % 2, 1, :][:, None, None, :].broadcast_to(shape)
            if t:
                eng.wait_ge(done, t)
            eng.tensor_tensor(a[:], v[:, :, :, :, 0], sin if swapped else cos, ALU.mult).then_inc(products, 1)
            eng.tensor_tensor(bb[:], v[:, :, :, :, 1], cos if swapped else sin, ALU.mult).then_inc(products, 1)
            eng.wait_ge(products, 2 * t + 2)
            eng.tensor_tensor(rot[:, :, t, :, :, half], a[:], bb[:], op).then_inc(done, 1)

        @b.gpsimd
        def _(pool):
            for t in range(TILES):
                rotate(pool, t, 1, True, tc, td, ALU.add, pmul, rp)

        @b.vector
        def _(dve):
            def decay(u):
                s, h = UNITS[u]
                dve.wait_ge(sm, u + 1)
                if u >= 2:
                    dve.wait_ge(om, u - 1)
                dve.tensor_tensor(sc[:, u % 2], PS[:, 2 + u % 2, :].rearrange("p (a i) -> p a i", a=2), dec[:, h],
                                  ALU.mult).then_inc(sd, 1)

            def side_taps(n):
                dve.wait_ge(mid, n + 1)
                yy = y[:, n % 3, :].rearrange("p (s t) -> p s t", s=N_SEQ)
                xx = raw[:, n // HEADS, n % HEADS, :].rearrange("p (s t) -> p s t", s=N_SEQ)
                dve.scalar_tensor_tensor(out=yy[:, :, 1:], in0=xx[:, :, :-1], scalar=wc[:, 0, n:n + 1],
                                         in1=yy[:, :, 1:], op0=ALU.mult, op1=ALU.add).then_inc(side, 1)
                dve.wait_ge(side, 2 * n + 1)
                dve.scalar_tensor_tensor(out=yy[:, :, :-1], in0=xx[:, :, 1:], scalar=wc[:, 2, n:n + 1],
                                         in1=yy[:, :, :-1], op0=ALU.mult, op1=ALU.add).then_inc(side, 1)

            step = 0

            def link(ins):
                nonlocal step
                step += 1
                ins.then_inc(gs, 1)
                dve.wait_ge(gs, step)

            def delta_gates():
                dve.wait_ge(a_in, 32)
                link(dve.tensor_tensor(x[:], small[:, :, G:2 * G], dtb[:, None, :].broadcast_to([P, TILES, G]), ALU.add))
                link(dve.scalar_tensor_tensor(out=ax[:], in0=x[:], scalar=-1.0, in1=x[:], op0=ALU.mult, op1=ALU.max))
                dve.wait_ge(ga, 3)
                link(dve.tensor_scalar(x[:], x[:], 0.0, None, ALU.max))
                link(dve.tensor_scalar(u1[:], e[:], 1.0, None, ALU.add))
                link(dve.tensor_scalar(c[:], u1[:], -1.0, None, ALU.add))
                link(dve.tensor_tensor(c[:], e[:], c[:], ALU.subtract))
                dve.wait_ge(ga, 4)
                link(dve.reciprocal(u1[:], u1[:]))
                link(dve.tensor_tensor(c[:], c[:], u1[:], ALU.mult))
                link(dve.tensor_tensor(c[:], c[:], ln[:], ALU.add))
                link(dve.tensor_tensor(c[:], c[:], x[:], ALU.add))
                link(dve.tensor_tensor(c[:], c[:], ea[:, None, :].broadcast_to([P, TILES, G]), ALU.mult))
                link(dve.tensor_scalar(gates[:, 1], c[:], -1.0, None, ALU.mult))
                link(dve.tensor_scalar(eb[:], eb[:], 1.0, None, ALU.add))
                link(dve.reciprocal(gates[:, 0], eb[:]))

            rotate(dve, 0, 0, False, ta, tb, ALU.subtract, mul, rt)
            delta_gates()
            for t in range(1, TILES):
                rotate(dve, t, 0, False, ta, tb, ALU.subtract, mul, rt)
            dve.wait_ge(w_in_, 48)
            for n in range(ROWS):
                side_taps(n)
                if n < NU:
                    decay(n)

        @b.scalar
        def _(act):
            def delta_gates():
                act.wait_ge(a_in, 32)
                act.activation(ea[:], al[:], ACT.Exp).then_inc(ga, 1)
                act.activation(eb[:], small[:, :, 0:G], ACT.Exp, scale=-1.0).then_inc(ga, 1)
                act.wait_ge(gs, 2)
                act.activation(e[:], ax[:], ACT.Exp, scale=-1.0).then_inc(ga, 1)
                act.wait_ge(gs, 4)
                act.activation(ln[:], u1[:], ACT.Ln).then_inc(ga, 1)

            def middle_tap(n):
                if n >= 3:
                    act.wait_ge(done, n - 2)
                act.activation(y[:, n % 3, :], raw[:, n // HEADS, n % HEADS, :], ACT.Copy,
                               scale=wc[:, 1, n:n + 1]).then_inc(mid, 1)

            def silu(n):
                act.wait_ge(side, 2 * n + 2)
                act.activation(raw[:, n // HEADS, n % HEADS, :], y[:, n % 3, :], ACT.Silu).then_inc(done, 1)

            def take_qk(u):
                act.wait_ge(qt, u + 1)
                if u >= 2:
                    act.wait_ge(sm, u - 1)
                act.copy(qk[:, u % 2], PS[:, u % 2, :].rearrange("p (a i) -> p a i", a=2)).then_inc(qc, 1)

            def take_output(u):
                s, h = UNITS[u]
                act.wait_ge(om, u + 1)
                act.copy(Oret[:, 2 * s:2 * s + 2, h, :],
                         PS[:, 4 + u % 4, 0:2 * P].rearrange("p (c e) -> p c e", c=2)).then_inc(oc, 1)

            delta_gates()
            act.wait_ge(w_in_, 48)
            for n in range(ROWS):
                middle_tap(n)
                if n < NU:
                    take_qk(n)
                if n >= 1:
                    silu(n - 1)
                if 2 <= n < NU + 2:
                    take_output(n - 2)
            silu(ROWS - 1)

        @b.tensor
        def _(pe):
            def turn(u):
                s, h = UNITS[u]
                pe.wait_ge(rt, 2 * s + 2)
                pe.wait_ge(rp, 2 * s + 2)
                if u >= 2:
                    pe.wait_ge(qc, u - 1)
                for j in range(2):
                    for k in range(2):
                        src = rot[:, j, 2 * s + k, h].rearrange("p d two -> p (d two)")
                        i = pe.transpose(PS[:, u % 2, (2 * j + k) * P:(2 * j + k + 1) * P], src, ident[:])
                i.then_inc(qt, 1)

            def scores(u):
                pe.wait_ge(qc, u + 1)
                if u >= 2:
                    pe.wait_ge(sd, u - 1)
                for jc in range(2):
                    i = pe.matmul(PS[:, 2 + u % 2, jc * SEQ:(jc + 1) * SEQ], qk[:, u % 2, 1, jc * P:(jc + 1) * P],
                                  qk[:, u % 2, 0, :], start=True, stop=True)
                i.then_inc(sm, 1)

            def output(u):
                s, h = UNITS[u]
                pe.wait_ge(sd, u + 1)
                if u >= 4:
                    pe.wait_ge(oc, u - 3)
                for ic in range(2):
                    for jc in range(2):
                        i = pe.matmul(PS[:, 4 + u % 4, ic * P:(ic + 1) * P], sc[:, u % 2, jc, ic * P:(ic + 1) * P],
                                      tok[:, 2, 2 * s + jc, h * P:(h + 1) * P], start=jc == 0, stop=jc == 1)
                i.then_inc(om, 1)

            for u in range(NU + 2):
                if u < NU:
                    turn(u)
                if 1 <= u <= NU:
                    scores(u - 1)
                if u >= 2:
                    output(u - 2)


def merge_unit_stage(nc, res, raw, tokm, O, gain, SG, *tables_ahead):
    AH, AL, ident, PS = res.AH, res.AL, res.ident, res.PS
    N = 2 * HEADS
    R = TILES * HEADS
    with Stage(nc, "merunit") as st:
        tmp = st.sb("tmp", [P, R, P])
        cen = st.sb("centred", [P, R, P])
        s1 = st.sb("s1", [P, R])
        s2 = st.sb("s2", [P, R])
        rm = st.sb("merge_rsqrt", [P, R])
        gcol = st.sb("gcol", [P, HEADS])
        prod = st.sb("prod", [P, 2, TOK])
        g_in = st.sem("gain_loaded")
        ms = st.sem("merge_step")
        msq = st.sem("merge_squared")
        sgd = st.sem("gate_ready")
        mr = st.sem("merge_rsqrt_ready")
        mt = st.sem("head_transposed")
        mp = st.sem("product_ready")
        mh = st.sem("hi_written")
        ml = st.sem("lo_written")
        sq = st.sb("sq", [P, TILES, N, P])
        ss = st.sb("ss", [P, TILES, N])
        rs = st.sb("rs", [P, TILES, N])
        t_ok = st.sem("tile_transposed")
        c_ok = st.sem("tile_copied")
        sqd = st.sem("squared")
        summed = st.sem("squares_summed")
        eps = st.sem("eps_added")
        r_ok = st.sem("rsqrt_ready")
        rq = st.sem("q_factor_applied")
        un = st.sem("tile_scaled")
        b_ok = st.sem("head_transposed_back")
        bc = st.sem("head_copied")
        b = st.block()
        o = O[:].rearrange("p t h e -> p (t h) e")

        @b.sync
        def _(sp):
            sp.dma_start(gcol[:], gain.rearrange("(h p) -> p h", p=P)).then_inc(g_in, 16)

        load_part(Part(st, "tables"), b, *tables_ahead)

        @b.tensor
        def _(pe):
            for t in range(TILES):
                for j in range(3):
                    n = 3 * t + j
                    if n >= 4:
                        pe.wait_ge(c_ok, n - 3)
                    for h in range(HEADS):
                        i = pe.transpose(PS[:, n % 4, h * P:(h + 1) * P], raw[:, j, h, t * P:(t + 1) * P], ident[:])
                    i.then_inc(t_ok, 1)
            pe.wait_ge(ms, 6)
            for h in range(HEADS):
                for t in range(TILES):
                    i = pe.transpose(PS[:, 4 + h, t * P:(t + 1) * P], tmp[:, t * HEADS + h, :], ident[:])
                i.then_inc(mt, 1)
            pe.wait_ge(un, TILES)
            for n in range(N):
                if n < 4:
                    pe.wait_ge(c_ok, 3 * TILES)
                else:
                    pe.wait_ge(bc, n - 3)
                for t in range(TILES):
                    i = pe.transpose(PS[:, n % 4, t * P:(t + 1) * P],
                                     tokm[:, t, n // HEADS, (n % HEADS) * P:(n % HEADS + 1) * P], ident[:])
                i.then_inc(b_ok, 1)

        @b.scalar
        def _(act):
            act.activation(SG[:, 0], SG[:, 0], ACT.Silu).then_inc(sgd, 1)
            for t in range(TILES):
                for n in range(3 * t, 3 * t + 3):
                    act.wait_ge(t_ok, n + 1)
                    act.copy(tokm[:, n // 3, n % 3, :], PS[:, n % 4, :]).then_inc(c_ok, 1)
                if t == 1:
                    act.wait_ge(ms, 3)
                    act.activation(tmp[:], cen[:], ACT.Square).then_inc(msq, 1)
                act.wait_ge(c_ok, 3 * t + 3)
                act.activation(sq[:, t], tokm[:, t, 0:2].rearrange("p j (h e) -> p (j h) e", e=P),
                               ACT.Square).then_inc(sqd, 1)
            for h in range(HEADS):
                act.wait_ge(mp, h + 1)
                act.copy(AH[:, h, :], prod[:, h % 2, :]).then_inc(mh, 1)
            for n in range(N):
                act.wait_ge(b_ok, n + 1)
                act.copy(raw[:, n // HEADS, n % HEADS, :], PS[:, n % 4, :]).then_inc(bc, 1)

        @b.gpsimd
        def _(pool):
            pool.wait_ge(ms, 5)
            pool.tensor_tensor(rm[:], s2[:], res.mhalf[:, 0:R], ALU.pow).then_inc(mr, 1)
            for t in range(TILES):
                pool.wait_ge(eps, t + 1)
                pool.tensor_tensor(rs[:, t], ss[:, t], res.mhalf[:, 0:N], ALU.pow).then_inc(r_ok, 1)

        @b.vector
        def _(dve):
            def lo(h):
                dve.wait_ge(mh, h + 1)
                dve.tensor_tensor(AL[:, h, :], prod[:, h % 2, :], AH[:, h, :].bitcast(F32), ALU.subtract).then_inc(ml, 1)

            def tile_sums(t):
                dve.wait_ge(sqd, t + 1)
                dve.tensor_reduce(ss[:, t], sq[:, t], AX.X, ALU.add).then_inc(summed, 1)
                dve.wait_ge(summed, t + 1)
                dve.tensor_scalar(ss[:, t], ss[:, t], EPS, None, ALU.add).then_inc(eps, 1)

            def scale_tile(t):
                dve.wait_ge(r_ok, t + 1)
                dve.tensor_scalar(rs[:, t, 0:HEADS], rs[:, t, 0:HEADS], P ** -0.5, None, ALU.mult).then_inc(rq, 1)
                dve.wait_ge(rq, t + 1)
                v = tokm[:, t, 0:2, :].rearrange("p j (h e) -> p (j h) e", e=P)
                dve.tensor_tensor(v, v, rs[:, t, :, None].broadcast_to([P, N, P]), ALU.mult).then_inc(un, 1)

            dve.tensor_reduce(s1[:], o, AX.X, ALU.add).then_inc(ms, 1)
            dve.wait_ge(ms, 1)
            dve.tensor_scalar(s1[:], s1[:], 1.0 / P, None, ALU.mult).then_inc(ms, 1)
            dve.wait_ge(ms, 2)
            dve.tensor_tensor(cen[:], o, s1[:, :, None].broadcast_to([P, R, P]), ALU.subtract).then_inc(ms, 1)
            tile_sums(0)
            dve.wait_ge(msq, 1)
            dve.tensor_reduce(s2[:], tmp[:], AX.X, ALU.add).then_inc(ms, 1)
            dve.wait_ge(ms, 4)
            dve.tensor_scalar(s2[:], s2[:], 1.0 / P, EPS, ALU.mult, ALU.add).then_inc(ms, 1)
            for t in range(1, TILES):
                tile_sums(t)
            dve.wait_ge(mr, 1)
            dve.tensor_tensor(tmp[:], cen[:], rm[:, :, None].broadcast_to([P, R, P]), ALU.mult).then_inc(ms, 1)
            dve.wait_ge(g_in, 16)
            dve.wait_ge(sgd, 1)
            for t in range(TILES):
                scale_tile(t)
            for h in range(HEADS):
                dve.wait_ge(mt, h + 1)
                if h >= 2:
                    dve.wait_ge(mh, h - 1)
                    dve.wait_ge(ml, h - 1)
                dve.scalar_tensor_tensor(out=prod[:, h % 2, :], in0=PS[:, 4 + h, :], scalar=gcol[:, h:h + 1],
                                         in1=SG[:, 0, h, :], op0=ALU.mult, op1=ALU.mult).then_inc(mp, 1)
                if h >= 1:
                    lo(h - 1)
            lo(HEADS - 1)


def first_tile(s, d):
    return 2 * s + d


def second_tile(s, d):
    return 2 * s + 1 - d


def delta_stage(nc, res, tri, lm, raw, tokm, gates, Ogdn):
    ident, PS = res.ident, res.PS
    NB = TILES * DIRS
    H4 = [P, HEADS, P]
    qn, kn = raw[:, 0], raw[:, 1]

    def heads(ap):
        return ap.rearrange("p (h i) -> p h i", h=HEADS)

    def bank(n):
        return heads(PS[:, n, :])

    with Stage(nc, "dlta") as st:
        lmc = st.sb("level_mask", [P, DIRS, P])
        T = st.sb("T", [P, NB] + H4[1:])
        TT = st.sb("TT", [P, NB] + H4[1:])
        MT = st.sb("MT", [P, NB] + H4[1:])
        QK = st.sb("QK", [P, NB] + H4[1:])
        qd = st.sb("q_decayed", [P, 4] + H4[1:])
        ring = st.sb("ring", [P, 2] + H4[1:])
        gcc = st.sb("g_cumulative", [P, DIRS, TILES, HEADS])
        glast = st.sb("g_last", [P, TILES, DIRS, HEADS])
        kt = st.sb("tail_factor", [P, DIRS, TILES, HEADS])
        kg = st.sb("key_factor", [P, DIRS, TILES, HEADS])
        eg = st.sb("exp_g", [P, DIRS, TILES, HEADS])
        gm = st.sem("gate_sums_done")
        gcp = st.sem("gate_sums_copied")
        gst = st.sem("gate_factor_step")
        rows = st.sem("rows_ready")
        kk = st.sem("products_ready")
        df = st.sem("differences_ready")
        ex = st.sem("decay_ready")
        xg = st.sem("row_exponential_ready")
        br = st.sem("beta_row_copied")
        em = st.sem("decay_masked")
        ebm = st.sem("decay_times_beta")
        qu = st.sem("q_decayed_ready")
        fin = st.sem("batch_matrices_ready")
        m0 = st.sem("first_level_masked")
        t0 = st.sem("first_inverse_ready")
        b = st.block()

        def second(n):
            t, d = n // DIRS, n % DIRS
            return t == second_tile(t // 2, d)

        seconds = [n for n in range(NB) if second(n)]

        def banks(n):
            return (1, 2, 3, 4) if n % 2 == 0 else (5, 6, 7, 0)

        @b.tensor
        def _(pe):
            for d in range(DIRS):
                pe.matmul(PS[:, 0, d * 16:(d + 1) * 16], tri[:, d, :],
                          gates[:, 1].rearrange("p t (d h) -> p t d h", d=DIRS)[:, :, d, :], start=True, stop=True)
            pe.matmul(PS[:, 0, 32:64], res.ones[:], gates[:, 1], start=True, stop=True).then_inc(gm, 1)
            for n in range(NB):
                t, d = n // DIRS, n % DIRS
                b1, b2, b3, b4 = banks(n)
                if n == 1:
                    pe.wait_ge(gcp, 2)
                if n >= 2:
                    pe.wait_ge(fin, n - 1)
                for h in range(HEADS):
                    g = gates[:, 1, t, d * HEADS + h:d * HEADS + h + 1].broadcast_to([P, P])
                    be = gates[:, 0, t, d * HEADS + h:d * HEADS + h + 1].broadcast_to([P, P])
                    pe.matmul(PS[:, b1, h * P:(h + 1) * P], g, tri[:, d, :], start=True, stop=True)
                    i = pe.matmul(PS[:, b2, h * P:(h + 1) * P], be, ident[:], start=True, stop=True)
                i.then_inc(rows, 1)
                for h in range(HEADS):
                    s = slice(t * P, (t + 1) * P)
                    pe.matmul(PS[:, b3, h * P:(h + 1) * P], kn[:, h, s], kn[:, h, s], start=True, stop=True)
                    i = pe.matmul(PS[:, b4, h * P:(h + 1) * P], kn[:, h, s], qn[:, h, s], start=True, stop=True)
                i.then_inc(kk, 1)

        @b.scalar
        def _(act):
            act.wait_ge(gcp, 2)
            act.activation(eg[:], gcc[:], ACT.Exp).then_inc(gst, 1)
            act.wait_ge(gst, 2)
            act.activation(kt[:], kt[:], ACT.Exp).then_inc(gst, 1)
            for n in range(NB):
                act.wait_ge(rows, n + 1)
                if second(n):
                    if n > seconds[0]:
                        act.wait_ge(qu, seconds.index(n))
                    act.wait_ge(df, 2 * n + 1)
                    act.activation(ring[:, 0], bank(banks(n)[0]), ACT.Exp).then_inc(xg, 1)
                act.copy(TT[:, n], bank(banks(n)[1])).then_inc(br, 1)
                act.wait_ge(df, 2 * n + 2)
                act.activation(T[:, n], T[:, n], ACT.Exp).then_inc(ex, 1)

        @b.gpsimd
        def _(pool):
            def first_level(n):
                pool.wait_ge(fin, n + 1)
                pool.tensor_tensor(T[:, n], MT[:, n], lm[:, n % DIRS, 0, None, :].broadcast_to(H4), ALU.mult).then_inc(m0, 1)

            for n in range(NB):
                d = n % DIRS
                pool.wait_ge(ex, n + 1)
                pool.tensor_tensor(T[:, n], T[:, n], tri[:, d, None, :].broadcast_to(H4), ALU.mult).then_inc(em, 1)
                pool.wait_ge(br, n + 1)
                pool.wait_ge(em, n + 1)
                pool.tensor_tensor(TT[:, n], TT[:, n], T[:, n], ALU.mult).then_inc(ebm, 1)
                if n:
                    first_level(n - 1)
            first_level(NB - 1)

        @b.vector
        def _(dve):
            dve.wait_ge(gm, 1)
            dve.tensor_copy(gcc[:].rearrange("p d t h -> p (d t h)"), PS[:, 0, 0:32]).then_inc(gcp, 1)
            dve.tensor_copy(glast[:].rearrange("p t d h -> p (t d h)"), PS[:, 0, 32:64]).then_inc(gcp, 1)
            dve.wait_ge(gcp, 2)
            dve.wait_ge(gst, 1)
            dve.tensor_tensor(kt[:], glast[:].rearrange("p t d h -> p d t h"), gcc[:], ALU.subtract).then_inc(gst, 1)
            dve.tensor_tensor(kg[:], gates[:, 0].rearrange("p t (d h) -> p d t h", d=DIRS), eg[:],
                              ALU.mult).then_inc(gcp, 1)

            def first_inverse(n):
                dve.wait_ge(m0, n + 1)
                dve.tensor_tensor(TT[:, n], ident[:, None, :].broadcast_to(H4), T[:, n], ALU.subtract).then_inc(t0, 1)

            def differences(n):
                t, d = n // DIRS, n % DIRS
                dve.wait_ge(rows, n + 1)
                dve.tensor_tensor(T[:, n], bank(banks(n)[0]), gcc[:, d, t, :, None].broadcast_to(H4),
                                  ALU.subtract).then_inc(df, 1)
                dve.wait_ge(df, 2 * n + 1)
                dve.tensor_scalar(T[:, n], T[:, n], 0.0, None, ALU.min).then_inc(df, 1)
                if second(n):
                    i = seconds.index(n)
                    dve.wait_ge(xg, i + 1)
                    dve.tensor_tensor(qd[:, i], qn[:, :, t * P:(t + 1) * P], ring[:, 0], ALU.mult).then_inc(qu, 1)

            def matrices(n):
                _, _, b3, b4 = banks(n)
                dve.wait_ge(kk, n + 1)
                dve.wait_ge(em, n + 1)
                dve.tensor_tensor(QK[:, n], bank(b4), T[:, n], ALU.mult)
                dve.wait_ge(ebm, n + 1)
                dve.tensor_tensor(MT[:, n], bank(b3), TT[:, n], ALU.mult).then_inc(fin, 1)

            differences(0)
            for n in range(NB):
                if n + 1 < NB:
                    differences(n + 1)
                matrices(n)
                if n:
                    first_inverse(n - 1)
            dve.wait_ge(fin, NB)
            first_inverse(NB - 1)

        inv = Inner(nc, st, "inv")
        RINGS = 2
        mk = inv.sem("level_masked")
        xm = inv.sem("x_done")
        xc = inv.sem("x_copied")
        ym = inv.sem("y_done")
        up = inv.sem("inverse_updated")
        lc = inv.sem("level_mask_copied")
        tt = inv.sem("first_inverse_turned")
        tc = inv.sem("first_inverse_copied")
        b = inv.block()
        LAST = LEVELS - 2

        def each_level(eng, level):
            with eng.Fori(0, LAST) as r:
                level(r, False)
            level(LAST, True)

        @b.gpsimd
        def _(pool):
            pool.sem_inc(mk, 1)

            def level(r, last):
                pool.wait_ge(mk, r * NB + 1)
                mask = lm[:, :, LAST + 1, :] if last else lm[:, :, bass.ds(r + 1, 1), :].squeeze(2)
                pool.tensor_copy(lmc[:], mask).then_inc(lc, 1)
                pool.wait_ge(lc, r + 1)
                for n in range(NB):
                    pool.wait_ge(xm, r * NB + n + 1)
                    pool.tensor_tensor(ring[:, n % RINGS], MT[:, n],
                                       lmc[:, n % DIRS, None, :].broadcast_to(H4), ALU.mult).then_inc(mk, 1)

            each_level(pool, level)

        xs = Ogdn[:, 0:2]

        @b.tensor
        def _(pe):
            pe.sem_inc(xm, RINGS)
            pe.sem_inc(ym, RINGS)
            for n in range(NB):
                for h in range(HEADS):
                    i = pe.transpose(PS[:, n, h * P:(h + 1) * P], TT[:, n, h, :], ident[:])
                i.then_inc(tt, 1)

            def level(r, last):
                def x(n):
                    pe.wait_ge(mk, r * NB + n + 2)
                    pe.wait_ge(xc, r * NB + n + 1)
                    pe.wait_ge(tc, NB)
                    pe.wait_ge(up, 2 * NB * r + 2 * n + 1)
                    for h in range(HEADS):
                        i = pe.matmul(PS[:, n % 2, h * P:(h + 1) * P], ring[:, n % RINGS, h, :], T[:, n, h, :],
                                      start=True, stop=True)
                    i.then_inc(xm, 1)

                def y(n):
                    pe.wait_ge(xc, r * NB + n + RINGS + 1)
                    if n < 3:
                        pe.wait_ge(up, 2 * NB * r + 2 * (NB - 1 - (NB - 1 - n) % 3) + 2)
                    else:
                        pe.wait_ge(up, 2 * NB * (r + 1) + (n - 2) * (1 if last else 2))
                    bk = 2 + 2 * (n % 3)
                    for h in range(HEADS):
                        if not last:
                            pe.matmul(PS[:, bk, h * P:(h + 1) * P], TT[:, n, h, :], xs[:, n % RINGS, h, :],
                                      start=True, stop=True)
                        i = pe.matmul(PS[:, bk + 1, h * P:(h + 1) * P], xs[:, n % RINGS, h, :], TT[:, n, h, :],
                                      start=True, stop=True)
                    i.then_inc(ym, 1)

                x(0)
                for n in range(1, NB):
                    x(n)
                    y(n - 1)
                y(NB - 1)

            each_level(pe, level)

        @b.scalar
        def _(act):
            act.sem_inc(xc, RINGS)
            for n in range(NB):
                act.wait_ge(tt, n + 1)
                act.copy(T[:, n], bank(n)).then_inc(tc, 1)

            def level(r, last):
                for n in range(NB):
                    act.wait_ge(xm, r * NB + n + RINGS + 1)
                    act.wait_ge(ym, r * NB + n + 1)
                    act.copy(xs[:, n % RINGS], bank(n % 2)).then_inc(xc, 1)

            each_level(act, level)

        @b.vector
        def _(dve):
            dve.sem_inc(up, 2 * NB)

            def level(r, last):
                for n in range(NB):
                    dve.wait_ge(ym, r * NB + n + RINGS + 1)
                    bk = 2 + 2 * (n % 3)
                    if not last:
                        dve.tensor_tensor(T[:, n], T[:, n], bank(bk), ALU.subtract).then_inc(up, 1)
                    dve.tensor_tensor(TT[:, n], TT[:, n], bank(bk + 1), ALU.subtract).then_inc(up, 1)

            each_level(dve, level)
        inv.close()

        out = Inner(nc, st, "dout")
        vb = MT
        kb = T
        NW = ring
        S = raw[:, 2].rearrange("p q (h e) -> p q h e", h=HEADS)
        SEQS = [(s, d) for s in range(N_SEQ) for d in range(DIRS)]
        scl = out.sem("operands_scaled")
        um = out.sem("first_values_done")
        uc = out.sem("first_values_copied")
        wm = out.sem("readers_done")
        wc = out.sem("readers_copied")
        sm = out.sem("state_done")
        scp = out.sem("state_copied")
        vm = out.sem("second_values_done")
        vc = out.sem("second_values_copied")
        om = out.sem("output_done")
        oc = out.sem("output_copied")
        b = out.block()

        def batch(t, d):
            return t * DIRS + d

        def tok(t, j):
            return heads(tokm[:, t, j, :])

        NQ = len(SEQS)

        def half(q):
            return 4 * (q % 2)

        @b.vector
        def _(dve):
            def scale(q):
                s, d = SEQS[q]
                f, g = first_tile(s, d), second_tile(s, d)
                bf = gates[:, 0, f, d * HEADS:(d + 1) * HEADS, None].broadcast_to(H4)
                bg = gates[:, 0, g, d * HEADS:(d + 1) * HEADS, None].broadcast_to(H4)
                dve.tensor_tensor(vb[:, batch(f, d)], tok(f, 2), bf, ALU.mult).then_inc(scl, 1)
                dve.tensor_tensor(kb[:, q], tok(g, 1), kg[:, d, g, :, None].broadcast_to(H4), ALU.mult).then_inc(scl, 1)
                dve.tensor_tensor(kb[:, 4 + q], tok(f, 1), kt[:, d, f, :, None].broadcast_to(H4), ALU.mult).then_inc(scl, 1)
                dve.tensor_tensor(vb[:, batch(g, d)], tok(g, 2), bg, ALU.mult).then_inc(scl, 1)

            def readers(q):
                dve.wait_ge(wm, q + 1)
                if q >= 2:
                    dve.wait_ge(vm, q - 1)
                dve.tensor_scalar(NW[:, q % 2], bank(half(q) + 1), -1.0, None, ALU.mult).then_inc(wc, 1)

            def second_values(q):
                s, d = SEQS[q]
                dve.wait_ge(vm, q + 1)
                dve.tensor_copy(vb[:, batch(second_tile(s, d), d)], bank(half(q) + 3)).then_inc(vc, 1)

            scale(0)
            scale(1)
            readers(0)
            for q in range(NQ):
                if q + 1 < NQ:
                    readers(q + 1)
                if q + 2 < NQ:
                    scale(q + 2)
                second_values(q)

        @b.scalar
        def _(act):
            def first_values(q):
                s, d = SEQS[q]
                act.wait_ge(um, q + 1)
                act.copy(vb[:, batch(first_tile(s, d), d)], bank(half(q))).then_inc(uc, 1)

            first_values(0)
            for q in range(NQ):
                if q + 1 < NQ:
                    first_values(q + 1)
                act.wait_ge(sm, q + 1)
                act.copy(S[:, q], bank(half(q) + 2)).then_inc(scp, 1)
            for t in range(TILES):
                act.wait_ge(om, t + 1)
                act.copy(Ogdn[:, t], bank(4 + t)).then_inc(oc, 1)

        @b.tensor
        def _(pe):
            def begin(q):
                s, d = SEQS[q]
                f, g = first_tile(s, d), second_tile(s, d)
                pe.wait_ge(scl, 4 * q + 1)
                if q >= 2:
                    pe.wait_ge(vc, q - 1)
                for h in range(HEADS):
                    i = pe.matmul(PS[:, half(q), h * P:(h + 1) * P], TT[:, batch(f, d), h, :],
                                  vb[:, batch(f, d), h, :], start=True, stop=True)
                i.then_inc(um, 1)
                pe.wait_ge(scl, 4 * q + 2)
                for h in range(HEADS):
                    i = pe.matmul(PS[:, half(q) + 1, h * P:(h + 1) * P], kb[:, q, h, :],
                                  TT[:, batch(g, d), h, :], start=True, stop=True)
                i.then_inc(wm, 1)

            def end(q):
                s, d = SEQS[q]
                f, g = first_tile(s, d), second_tile(s, d)
                pe.wait_ge(uc, q + 1)
                pe.wait_ge(scl, 4 * q + 4)
                for h in range(HEADS):
                    i = pe.matmul(PS[:, half(q) + 2, h * P:(h + 1) * P], kb[:, 4 + q, h, :],
                                  vb[:, batch(f, d), h, :], start=True, stop=True)
                i.then_inc(sm, 1)
                if q + 1 < NQ:
                    begin(q + 1)
                pe.wait_ge(wc, q + 1)
                pe.wait_ge(scp, q + 1)
                for h in range(HEADS):
                    o = PS[:, half(q) + 3, h * P:(h + 1) * P]
                    pe.matmul(o, TT[:, batch(g, d), h, :], vb[:, batch(g, d), h, :], start=True, stop=False)
                    i = pe.matmul(o, NW[:, q % 2, h, :], S[:, q, h, :], start=False, stop=True)
                i.then_inc(vm, 1)

            begin(0)
            for q in range(NQ):
                end(q)
            pe.wait_ge(vc, NQ)
            for t in range(TILES):
                s = t // 2
                d2 = [d for d in range(DIRS) if second_tile(s, d) == t][0]
                for h in range(HEADS):
                    o = PS[:, 4 + t, h * P:(h + 1) * P]
                    for d in range(DIRS):
                        pe.matmul(o, QK[:, batch(t, d), h, :], vb[:, batch(t, d), h, :], start=d == 0, stop=False)
                    i = pe.matmul(o, qd[:, seconds.index(batch(t, d2)), h, :], S[:, SEQS.index((s, d2)), h, :],
                                  start=False, stop=True)
                i.then_inc(om, 1)
        out.close()


def attention_part(st, b, res, qT, kT, v, ahead):
    AH, AL, ident, PS = res.AH, res.AL, res.ident, res.PS
    UNITS = [(s, h) for s in range(N_SEQ) for h in range(HEADS)]
    NU = len(UNITS)
    RING = 3
    scale = XA_DH ** -0.5
    p = st.sb("probs", [P, RING, 2, SEQ])
    pT = st.sb("probs_T", [P, 2, 2, SEQ])
    mx = st.sb("max", [P, RING, 2])
    nm = st.sb("neg_max", [P, RING, 2])
    su = st.sb("sum", [P, RING, 2])
    ri = st.sb("inverse", [P, RING, 2])
    sm = st.sem("scores_done")
    ms = st.sem("max_step")
    ex = st.sem("exp_done")
    rs = st.sem("sum_inverted")
    nz = st.sem("probs_normalised")
    tm = st.sem("probs_turned")
    tcp = st.sem("probs_T_copied")
    om = st.sem("output_done")
    h_ok = st.sem("hi_written")
    l_ok = st.sem("lo_written")

    def dst(a, u):
        s, h = UNITS[u]
        return a[:, 2 * h:2 * h + 2, s * SEQ:(s + 1) * SEQ]

    def two(n):
        return PS[:, n, :].rearrange("p (a i) -> p a i", a=2)

    def steps(*stages):
        for i in range(NU + max(lag for _, lag in stages)):
            for f, lag in stages:
                if 0 <= i - lag < NU:
                    f(i - lag)

    @b.tensor
    def _(pe):
        def scores(u):
            s, h = UNITS[u]
            if u >= 2:
                pe.wait_ge(ex, 2 * (u - 1))
            for t in range(2):
                for k in range(2):
                    i = pe.matmul(PS[:, u % 2, t * SEQ:(t + 1) * SEQ],
                                  qT[:, 2 * h + k, s * SEQ + t * P:s * SEQ + (t + 1) * P],
                                  kT[:, 2 * h + k, s * SEQ:(s + 1) * SEQ], start=k == 0, stop=k == 1)
            i.then_inc(sm, 1)

        def turn(u):
            pe.wait_ge(nz, 2 * u + 2)
            if u >= 2:
                pe.wait_ge(tcp, u - 1)
            for m in range(2):
                for t in range(2):
                    i = pe.transpose(PS[:, 2 + u % 2, m * SEQ + t * P:m * SEQ + (t + 1) * P],
                                     p[:, u % RING, t, m * P:(m + 1) * P], ident[:])
            i.then_inc(tm, 1)

        def output(u):
            s, h = UNITS[u]
            pe.wait_ge(tcp, u + 1)
            if u >= 2:
                pe.wait_ge(l_ok, u - 1)
            for e in range(2):
                for m in range(2):
                    i = pe.matmul(PS[:, 4 + u % 2, e * SEQ:(e + 1) * SEQ],
                                  v[:, 2 * s + m, h * XA_DH + e * P:h * XA_DH + (e + 1) * P],
                                  pT[:, u % 2, m, :], start=m == 0, stop=m == 1)
            i.then_inc(om, 1)

        steps((scores, 0), (turn, 2), (output, 3))

    @b.vector
    def _(dve):
        def maximum(u):
            dve.wait_ge(sm, u + 1)
            if u >= RING:
                dve.wait_ge(ex, 2 * (u - RING + 1))
            dve.tensor_reduce(mx[:, u % RING], two(u % 2), AX.X, ALU.max).then_inc(ms, 1)
            dve.wait_ge(ms, 2 * u + 1)
            dve.tensor_scalar(nm[:, u % RING], mx[:, u % RING], -scale, None, ALU.mult).then_inc(ms, 1)

        def normalise(u):
            r = u % RING
            dve.wait_ge(ex, 2 * u + 2)
            if u >= RING:
                dve.wait_ge(nz, 2 * (u - RING + 1))
            dve.reciprocal(ri[:, r], su[:, r]).then_inc(rs, 1)
            dve.wait_ge(rs, u + 1)
            for t in range(2):
                dve.tensor_scalar(p[:, r, t], p[:, r, t], ri[:, r, t:t + 1], None, ALU.mult).then_inc(nz, 1)

        def take_turned(u):
            dve.wait_ge(tm, u + 1)
            if u >= 2:
                dve.wait_ge(om, u - 1)
            dve.tensor_copy(pT[:, u % 2], two(2 + u % 2)).then_inc(tcp, 1)

        def low(u):
            dve.wait_ge(h_ok, u + 1)
            dve.tensor_tensor(dst(AL, u), two(4 + u % 2), dst(AH, u).bitcast(F32), ALU.subtract).then_inc(l_ok, 1)

        steps((maximum, 0), (normalise, 1), (take_turned, 2), (low, 4))

    @b.scalar
    def _(act):
        def exponentials(u):
            r = u % RING
            act.wait_ge(ms, 2 * u + 2)
            if u >= RING:
                act.wait_ge(tm, u - RING + 1)
            for t in range(2):
                act.activation(p[:, r, t], PS[:, u % 2, t * SEQ:(t + 1) * SEQ], ACT.Exp,
                               bias=nm[:, r, t:t + 1], scale=scale, accum_out=su[:, r, t:t + 1]).then_inc(ex, 1)
            if u == 1:
                ahead.first_hi(act)

        def high(u):
            act.wait_ge(om, u + 1)
            act.copy(dst(AH, u), two(4 + u % 2)).then_inc(h_ok, 1)

        steps((exponentials, 0), (high, 3))

    @b.gpsimd
    def _(pool):
        ahead.first_lo(pool)

    ahead.acts = [(l_ok, len(UNITS)), (l_ok, len(UNITS))]


def select_stage(nc, res, qT, kraw, SL):
    ident, PS = res.ident, res.PS
    HC = 2 * PH
    BLOCKS = [(a, max(a, 1), TOPK // (a + 1)) for a in (0, 1, 2, 4, 8)]
    ROW = [nb for _, na, nb in BLOCKS for _ in range(na)]
    START = [sum(ROW[:a]) for a in range(TOPK + 1)]
    NCAND = START[TOPK]
    SINGLE = BLOCKS[-1][0]
    with Stage(nc, "sel") as st:
        kTs = st.sb("keys_T", [P, HC, P])
        sc = st.sb("scores", [P, 2, HC, NKEYS])
        v1 = st.sb("top_values", [P, HC, TOPK])
        i1 = st.sb("top_indices", [P, HC, TOPK], U32)
        i1f = st.sb("top_indices_f", [P, 2, HC, TOPK])
        ca = st.sb("candidates", [P, PH, NCAND])
        tv = st.sb("best_values", [P, PH, TOPK])
        tp = st.sb("best_positions", [P, PH, TOPK], U32)
        pf = st.sb("best_positions_f", [P, SLOTS])
        past = st.sb("past_row_start", [P, 2, SINGLE, SLOTS])
        tail = st.sb("past_last_start", [P, SLOTS])
        abf = st.sb("position_ranks", [P, 2, SLOTS])
        eq = st.sb("eq", [P, 2, SLOTS, TOPK])
        out = st.sb("slot_gates", [P, SLOTS])
        ez = st.sb("gate_exp", [P, PH, TOPK])
        zs = st.sb("gate_sum", [P, PH])
        zi = st.sb("gate_inverse", [P, PH])
        kt_ = st.sem("keys_turned")
        kc = st.sem("keys_copied")
        sm = st.sem("scores_done")
        scp = st.sem("scores_copied")
        used = st.sem("scores_used")
        step = st.sem("vector_step")
        pos = st.sem("positions_ready")
        zr = st.sem("gate_exponents_ready")
        ge = st.sem("gate_exp_done")
        dec = st.sem("pool_step")
        rk = st.sem("ranks_ready")
        ma = st.sem("matches_ready")
        px = st.sem("matches_times_index")
        pd = st.sem("last_matches_times_index")
        so = st.sem("slot_gates_ready")
        tr = st.sem("slots_turned")
        tcp = st.sem("slots_copied")
        b = st.block()
        LAST = TILES - 1

        @b.tensor
        def _(pe):
            for n in range(4):
                for m in range(4):
                    i = pe.transpose(PS[:, n, m * P:(m + 1) * P], kraw[:, 4 * n + m, :], ident[:])
                i.then_inc(kt_, 1)

            def scores(t):
                for n in range(4):
                    if t == 0:
                        pe.wait_ge(kc, n + 1)
                    else:
                        pe.wait_ge(scp, 4 * (t - 1) + n + 1)
                    for m in range(4):
                        i = pe.matmul(PS[:, n, m * P:(m + 1) * P], qT[:, 4 * n + m, t * P:(t + 1) * P],
                                      kTs[:, 4 * n + m, :], start=True, stop=True)
                    i.then_inc(sm, 1)

            scores(0)
            scores(1)
            for t in range(TILES):
                if t + 2 < TILES:
                    scores(t + 2)
                if t >= 1:
                    pe.wait_ge(tcp, 2 * t)
                for c in range(2):
                    if t == LAST and c == 1:
                        pe.wait_ge(pd, 1)
                    else:
                        pe.wait_ge(px, 2 * t + c + 1)
                    for k in range(TOPK):
                        pe.matmul(PS[:, 4, c * P:(c + 1) * P], eq[:, c, :, k], ident[:], start=k == 0, stop=k == TOPK - 1)
                pe.wait_ge(so, t + 1)
                pe.transpose(PS[:, 4, 2 * P:3 * P], out[:], ident[:]).then_inc(tr, 1)

        @b.scalar
        def _(act):
            for n in range(4):
                act.wait_ge(kt_, n + 1)
                act.copy(kTs[:, 4 * n:4 * n + 4, :].rearrange("p a n -> p (a n)"), PS[:, n, :]).then_inc(kc, 1)

            def scores(t):
                if t >= 2:
                    act.wait_ge(used, t - 1)
                for n in range(4):
                    act.wait_ge(sm, 4 * t + n + 1)
                    act.copy(sc[:, t % 2, 4 * n:4 * n + 4, :].rearrange("p a n -> p (a n)"), PS[:, n, :]).then_inc(scp, 1)

            scores(0)
            scores(1)
            for t in range(TILES):
                act.wait_ge(zr, t + 1)
                act.activation(ez[:], ez[:], ACT.Exp).then_inc(ge, 1)
                if t + 2 < TILES:
                    scores(t + 2)
                act.wait_ge(tr, t + 1)
                ts = slice(t * P, (t + 1) * P)
                act.copy(SL.idx[:, :, ts], PS[:, 4, 0:2 * P].rearrange("p (a t) -> p a t", a=2)).then_inc(tcp, 1)
                act.copy(SL.g[:, ts], PS[:, 4, 2 * P:3 * P]).then_inc(tcp, 1)

        def ranks(eng, mark, t):
            for r in range(SINGLE):
                eng.tensor_scalar(past[:, 0, r, :], pf[:], float(START[r + 1]), None, ALU.is_ge)
                eng.tensor_scalar(past[:, 1, r, :], pf[:], float(START[r + 1]), float(ROW[r]), ALU.is_ge, ALU.mult)
            mark(eng.tensor_scalar(tail[:], pf[:], -float(START[SINGLE]), 0.0, ALU.add, ALU.max))
            half = SINGLE // 2
            while half:
                mark(eng.tensor_tensor(past[:, :, 0:half], past[:, :, 0:half], past[:, :, half:2 * half], ALU.add))
                half //= 2
            if t >= 1:
                eng.wait_ge(ma, 2 * t)
            mark(eng.tensor_tensor(past[:, :, 0], past[:, :, 0], tail[:, None, :].broadcast_to([P, 2, SLOTS]), ALU.add))
            eng.tensor_copy(abf[:, 0], past[:, 0, 0]).then_inc(rk, 1)
            eng.tensor_tensor(abf[:, 1], pf[:], past[:, 1, 0], ALU.subtract).then_inc(rk, 1)

        def indices(eng, t, c):
            eng.wait_ge(ma, 2 * t + c + 1)
            e4 = eq[:, c].rearrange("p (h k) a -> p h k a", h=PH)
            ix = i1f[:, t % 2].rearrange("p (h c) k -> p h c k", c=2)[:, :, c, None, :]
            return eng.tensor_tensor(e4, e4, ix.broadcast_to([P, PH, TOPK, TOPK]), ALU.mult)

        @b.gpsimd
        def _(pool):
            n = 0

            def mark(ins):
                nonlocal n
                n += 1
                ins.then_inc(dec, 1)
                pool.wait_ge(dec, n)

            for t in range(LAST):
                pool.wait_ge(pos, t + 1)
                ranks(pool, mark, t)
                for c in range(2):
                    indices(pool, t, c).then_inc(px, 1)
            indices(pool, LAST, 0).then_inc(px, 1)

        @b.vector
        def _(dve):
            n = 0

            def mark(ins):
                nonlocal n
                n += 1
                ins.then_inc(step, 1)
                dve.wait_ge(step, n)

            def top16(values, count, top, index, arrived=None):
                for half in (slice(0, 8), slice(8, 16)):
                    for j in range(count):
                        if half.start == 0 and arrived is not None and j % 4 == 0:
                            dve.wait_ge(scp, arrived + j // 4 + 1)
                        i = dve.max(top[:, j, half], values[:, j, :])
                    mark(i)
                    for j in range(count):
                        i = dve.max_index(index[:, j, half], top[:, j, half], values[:, j, :])
                    mark(i)
                    if half.start == 0:
                        for j in range(count):
                            i = dve.match_replace(values[:, j, :], top[:, j, half], values[:, j, :], NEG)
                        mark(i)

            def rank_keys(t):
                top16(sc[:, t % 2], HC, v1, i1, 4 * t)
                if t >= 2:
                    dve.wait_ge(px, 2 * (t - 1))
                dve.tensor_copy(i1f[:, t % 2], i1[:]).then_inc(used, 1)

            def match(t):
                if t:
                    dve.wait_ge(tr, t)
                for c in range(2):
                    dve.wait_ge(rk, 2 * t + c + 1)
                    dve.tensor_tensor(eq[:, c], abf[:, c, :, None].broadcast_to([P, SLOTS, TOPK]),
                                      res.iota[:, None, 0:TOPK].broadcast_to([P, SLOTS, TOPK]), ALU.is_equal).then_inc(ma, 1)
                dve.wait_ge(ge, t + 1)
                mark(dve.tensor_reduce(zs[:], ez[:], AX.X, ALU.add))
                mark(dve.reciprocal(zi[:], zs[:]))
                dve.tensor_tensor(out[:].rearrange("p (h k) -> p h k", h=PH), ez[:],
                                  zi[:, :, None].broadcast_to([P, PH, TOPK]), ALU.mult).then_inc(so, 1)
                dve.wait_ge(so, t + 1)

            def rank_sums(t):
                vv = v1[:].rearrange("p (h c) k -> p h c k", c=2)
                for a0, na, nb in BLOCKS:
                    shape = [P, PH, na, nb]
                    i = dve.tensor_tensor(ca[:, :, START[a0]:START[a0 + na]].rearrange("p h (a b) -> p h a b", a=na),
                                          vv[:, :, 0, a0:a0 + na, None].broadcast_to(shape),
                                          vv[:, :, 1, None, 0:nb].broadcast_to(shape), ALU.add)
                mark(i)
                top16(ca, PH, tv, tp)
                dve.tensor_copy(pf[:], tp[:].rearrange("p h k -> p (h k)")).then_inc(pos, 1)
                dve.tensor_tensor(ez[:], tv[:], tv[:, :, 0:1].broadcast_to([P, PH, TOPK]), ALU.subtract).then_inc(zr, 1)

            rank_keys(0)
            rank_sums(0)
            for t in range(1, TILES):
                rank_keys(t)
                match(t - 1)
                rank_sums(t)
            dve.wait_ge(pos, TILES)
            ranks(dve, mark, LAST)
            match(LAST)
            indices(dve, LAST, 1).then_inc(pd, 1)


BLK = 128


def gate_stage(nc, res, SL, last_block):
    PS = res.PS
    SUB = 4
    NR = 4
    BATCH = SUB * NR
    NBLK = TOK // BLK
    with Stage(nc, "gate") as st:
        oh = st.sb("one_hots", [P, NR, 2, SUB, P])
        gh = st.sb("gated_one_hots", [P, NR, SUB, P])
        gb = [st.sb("block", [P, P, BLK]), last_block]
        ok = st.sem("one_hots_ready")
        gp = st.sem("gated_by_pool")
        ga = st.sem("gated_by_scalar")
        mm = st.sem("four_tokens_done")
        cp = st.sem("bank_free")
        so = [st.sem(f"block{i}_stored") for i in range(2)]
        b = st.block()

        def first(it, q):
            return it * BATCH + q * SUB

        @b.vector
        def _(dve):
            with dve.Fori(0, TOK // BATCH) as it:
                for q in range(NR):
                    dve.wait_ge(mm, it * NR + q + 1)
                    shape = [P, 2, SUB, P]
                    dve.tensor_tensor(oh[:, q], SL.idx[:, :, bass.ds(first(it, q), SUB)][:, :, :, None].broadcast_to(shape),
                                      res.iota[:, None, None, :].broadcast_to(shape), ALU.is_equal).then_inc(ok, 1)

        @b.gpsimd
        def _(pool):
            with pool.Fori(0, TOK // BATCH) as it:
                for q in range(0, NR, 2):
                    g = SL.g[:, bass.ds(first(it, q), SUB)][:, :, None].broadcast_to([P, SUB, P])
                    pool.wait_ge(ok, it * NR + q + 1)
                    pool.tensor_tensor(gh[:, q], oh[:, q, 1], g, ALU.mult).then_inc(gp, 1)

        @b.tensor
        def _(pe):
            pe.sem_inc(mm, NR)
            with pe.Fori(0, TOK // BATCH) as it:
                for q in range(NR):
                    if q % 2 == 0:
                        pe.wait_ge(gp, it * (NR // 2) + q // 2 + 1)
                    else:
                        pe.wait_ge(ga, it * (NR // 2) + q // 2 + 1)
                    pe.wait_ge(cp, it * NR + q + 1)
                    for k in range(SUB):
                        i = pe.matmul(PS[:, q, k * P:(k + 1) * P], gh[:, q, k, :], oh[:, q, 0, k, :],
                                      start=True, stop=True)
                    i.then_inc(mm, 1)

        @b.scalar
        def _(act):
            act.sem_inc(cp, NR)
            PER = BLK // BATCH

            def gate(it, q):
                act.wait_ge(ok, it * NR + q + 1)
                for k in range(SUB):
                    i = act.activation(gh[:, q, k, :], oh[:, q, 1, k, :], ACT.Copy,
                                       scale=SL.g[:, bass.ds(first(it, q) + k, 1)])
                i.then_inc(ga, 1)

            def take_out(half, it, r, parts):
                for q in parts:
                    act.wait_ge(mm, it * NR + NR + q + 1)
                    act.copy(gb[half][:, :, bass.ds(r * BATCH + q * SUB, SUB)].rearrange("p i t -> p t i"),
                             PS[:, q, :].rearrange("p (t i) -> p t i", t=SUB)).then_inc(cp, 1)

            with act.Fori(0, NBLK // 2) as pair:
                for half in range(2):
                    first_it = (pair * 2 + half) * PER
                    gate(first_it, 1)
                    gate(first_it, 3)
                    act.wait_ge(so[half], 16 * pair + 16)
                    take_out(half, first_it, 0, (0, 1))
                    with act.Fori(1, PER) as r:
                        it = first_it + r
                        gate(it, 1)
                        take_out(half, it - 1, r - 1, (2, 3))
                        gate(it, 3)
                        take_out(half, it, r, (0, 1))
                    take_out(half, first_it + PER - 1, PER - 1, (2, 3))

        @b.sync
        def _(sp):
            for half in range(2):
                sp.sem_inc(so[half], 16)

            def store(pair, half):
                sp.wait_ge(cp, NR + (pair * 2 + half + 1) * (BLK // SUB))
                sp.dma_start(res.gates[:, :, bass.ds((pair * 2 + half) * BLK, BLK)].rearrange("a b t -> b a t"),
                             gb[half][:]).then_inc(so[half], 16)

            with sp.Fori(0, NBLK // 2 - 1) as pair:
                store(pair, 0)
                store(pair, 1)
            store(NBLK // 2 - 1, 0)
            sp.wait_ge(so[0], 16 * (NBLK // 2 + 1))
            sp.wait_ge(so[1], 16 * (NBLK // 2))


def expert_stage(nc, res, U, V, last_block):
    AH, AL, ident, PS, X = res.AH, res.AL, res.ident, res.PS, res.X
    NT = NKEYS
    NG = NT // GROUP
    with Stage(nc, "exp") as st:
        ur = st.sb("u_raw", [P, 2, D])
        uh = st.sb("uT_hi", [P, 2, KC, P], F32R)
        ul = st.sb("uT_lo", [P, 2, KC, P], F32R)
        vr = st.sb("v_raw", [P, 2, D])
        vh = st.sb("v_hi", [P, GROUP, D], F32R)
        vl = st.sb("v_lo", [P, GROUP, D], F32R)
        gt = st.sb("gates", [P, 2, TOK])
        w = st.sb("w", [P, 2, TOK])
        wh = st.sb("w_hi", [P, GROUP, TOK], F32R)
        wl = st.sb("w_lo", [P, GROUP, TOK], F32R)
        u_in = [st.sem(f"u{i}_loaded") for i in range(2)]
        v_in = [st.sem(f"v{i}_loaded") for i in range(2)]
        g_in = [st.sem(f"gates{i}_loaded") for i in range(2)]
        g_out = st.sem("last_gates_stored")
        ut = st.sem("u_turned")
        uho = st.sem("uT_hi_written")
        ulo = st.sem("uT_lo_written")
        vho = st.sem("v_hi_written")
        vlo = st.sem("v_lo_written")
        am = st.sem("a_done")
        ge = st.sem("gelu_done")
        wo = st.sem("w_ready")
        who = st.sem("w_hi_written")
        wlo = st.sem("w_lo_written")
        om = st.sem("output_bank_done")
        ad = st.sem("output_bank_added")
        b = st.block()

        @b.sync
        def _(sp):
            def load_u(n, slot):
                sp.dma_start(ur[:, slot], U[bass.ds(n * P, P), :]).then_inc(u_in[slot], 16)

            def load_v(n, slot):
                sp.dma_start(vr[:, slot], V[bass.ds(n * P, P), :]).then_inc(v_in[slot], 16)

            def load_g(n, slot):
                sp.dma_start(gt[:, slot], res.gates[bass.ds(n, 1), :, :].rearrange("a b t -> (a b) t")).then_inc(g_in[slot], 16)

            FIRST = 2 * GROUP
            PIECE = (NKEYS - FIRST) // FIRST
            edges = [0] + [FIRST + i * PIECE for i in range(FIRST + 1)]

            def store_gates(i):
                keys = slice(edges[i], edges[i + 1])
                sp.dma_start(res.gates[keys, :, TOK - BLK:TOK].rearrange("a b t -> b a t"),
                             last_block[:, keys, :]).then_inc(g_out, 16)

            for n in range(2):
                load_u(n, n)
                load_v(n, n)
            store_gates(0)
            sp.wait_ge(g_out, 16)
            for n in range(2):
                load_g(n, n)

            def ahead(g, e, last):
                n = g * GROUP + e
                sp.wait_ge(ut, n + 1)
                load_u(0 if last and e >= GROUP - 2 else n + 2, e % 2)
                if not (last and e >= GROUP - 2):
                    sp.wait_ge(vlo, n + 1)
                    load_v(n + 2, e % 2)
                    sp.wait_ge(wo, n + 3)
                    load_g(n + 2, e % 2)

            for n in range(FIRST):
                if n == GROUP:
                    sp.wait_ge(g_out, 32)
                ahead(n // GROUP, n % GROUP, False)
                store_gates(n + 1)
            sp.wait_ge(g_out, 16 * (FIRST + 1))
            with sp.Fori(FIRST // GROUP, NG - 1) as g:
                for e in range(GROUP):
                    ahead(g, e, False)
            for e in range(GROUP - 1):
                ahead(NG - 1, e, True)
            sp.wait_ge(u_in[0], 16 * (NT // 2 + 1))

        @b.tensor
        def _(pe):
            def turn(n, slot):
                pe.wait_ge(u_in[slot], (n - slot) * 8 + 16)
                for k in range(KC):
                    i = pe.transpose(PS[:, k // 4, (k % 4) * P:(k % 4 + 1) * P], ur[:, slot, k * P:(k + 1) * P], ident[:])
                i.then_inc(ut, 1)

            pe.sem_inc(am, 1)
            pe.sem_inc(om, 1)
            turn(0, 0)
            with pe.Fori(0, NG) as g:
                for e in range(GROUP):
                    n = g * GROUP + e
                    pe.wait_ge(ulo, n + 1)
                    turn(n + 1, (e + 1) % 2)
                    pe.wait_ge(ge, n + 1)
                    for k in range(KC):
                        i = mm3(pe, PS[:, 2 + e % 2, :], (uh[:, e % 2, k, :], ul[:, e % 2, k, :]),
                                (AH[:, k, :], AL[:, k, :]), k == 0, k == KC - 1)
                    i.then_inc(am, 1)
                for half in range(2):
                    cols = slice(half * CHUNK, (half + 1) * CHUNK)
                    for e in range(GROUP):
                        if half == 0:
                            pe.wait_ge(wlo, g * GROUP + e + 3)
                            pe.wait_ge(vlo, g * GROUP + e + 1)
                        for t in range(TILES):
                            if e == 0:
                                pe.wait_ge(ad, g * 8 + 4 * half + t + 1)
                            s = slice(t * P, (t + 1) * P)
                            i = mm3(pe, PS[:, 4 + t, :], (wh[:, e, s], wl[:, e, s]),
                                    (vh[:, e, cols], vl[:, e, cols]), e == 0, e == GROUP - 1)
                            if e == GROUP - 1:
                                i.then_inc(om, 1)

        def turned(n=None):
            return PS[:, 0:2, :].rearrange("p b (k e) -> p (b k) e", k=4)

        @b.scalar
        def _(act):
            act.sem_inc(ge, 2)

            def u_hi(n, slot):
                act.wait_ge(ut, n + 1)
                act.copy(uh[:, slot], turned()).then_inc(uho, 1)

            u_hi(0, 0)
            with act.Fori(0, NG) as g:
                for e in range(GROUP):
                    n = g * GROUP + e
                    act.wait_ge(v_in[e % 2], g * 32 + (e // 2) * 16 + 16)
                    if e == 0:
                        act.wait_ge(om, g * 8 + 1)
                    act.copy(vh[:, e], vr[:, e % 2]).then_inc(vho, 1)
                    act.wait_ge(am, n + 1)
                    u_hi(n + 1, (e + 1) % 2)
                    act.wait_ge(am, n + 2)
                    act.wait_ge(wlo, n + 1)
                    act.activation(w[:, e % 2], PS[:, 2 + e % 2, :], ACT.Gelu_apprx_tanh).then_inc(ge, 1)
                    act.wait_ge(wo, n + 3)
                    act.copy(wh[:, e], w[:, e % 2]).then_inc(who, 1)

        @b.vector
        def _(dve):
            dve.sem_inc(wo, 2)
            dve.sem_inc(wlo, 2)
            dve.sem_inc(ad, 4)

            def u_lo(n, slot):
                dve.wait_ge(uho, n + 1)
                dve.tensor_tensor(ul[:, slot], turned(), uh[:, slot].bitcast(F32), ALU.subtract).then_inc(ulo, 1)

            u_lo(0, 0)
            with dve.Fori(0, NG) as g:
                for e in range(GROUP):
                    n = g * GROUP + e
                    dve.wait_ge(vho, n + 1)
                    dve.tensor_tensor(vl[:, e], vr[:, e % 2], vh[:, e].bitcast(F32), ALU.subtract).then_inc(vlo, 1)
                    u_lo(n + 1, (e + 1) % 2)
                    dve.wait_ge(ge, n + 3)
                    dve.wait_ge(g_in[e % 2], g * 32 + (e // 2) * 16 + 16)
                    dve.tensor_tensor(w[:, e % 2], w[:, e % 2], gt[:, e % 2], ALU.mult).then_inc(wo, 1)
                    dve.wait_ge(who, n + 1)
                    dve.tensor_tensor(wl[:, e], w[:, e % 2], wh[:, e].bitcast(F32), ALU.subtract).then_inc(wlo, 1)
                for half in range(2):
                    for t in range(TILES):
                        dve.wait_ge(om, g * 8 + 4 * half + t + 2)
                        x = X[:, t, half * CHUNK:(half + 1) * CHUNK]
                        dve.tensor_tensor(x, PS[:, 4 + t, :], x, ALU.add).then_inc(ad, 1)


def final_stage(nc, res, weight, outs):
    X = res.X
    with Stage(nc, "final") as st:
        wb = st.sb("weight", [P, D])
        sq = st.sb("sq", [P, D])
        y = st.sb("y", [P, TILES, D])
        ms = st.sb("ms", [P, TILES])
        mse = st.sb("mse", [P, TILES])
        rs = st.sb("rs", [P, TILES])
        w_in_ = st.sem("weight_loaded")
        ssq = st.sem("squares_summed")
        m_ok = st.sem("mean_ready")
        r_ok = st.sem("rsqrt_ready")
        y_ok = st.sem("row_ready")
        stored = st.sem("stored")
        b = st.block()

        @b.sync
        def _(sp):
            sp.dma_start(wb[:], weight.partition_broadcast(P)).then_inc(w_in_, 16)
            for t in range(TILES):
                sp.wait_ge(y_ok, t + 1)
                sp.dma_start(outs[t // 2][0, (t % 2) * P:(t % 2 + 1) * P, :], y[:, t, :]).then_inc(stored, 16)
            sp.wait_ge(stored, 16 * TILES)

        @b.scalar
        def _(act):
            for t in range(TILES):
                act.activation(sq[:], X[:, t, :], ACT.Square, accum_out=ms[:, t:t + 1]).then_inc(ssq, 1)
                act.wait_ge(ssq, t + 1)

        @b.gpsimd
        def _(pool):
            pool.wait_ge(m_ok, 1)
            pool.tensor_tensor(rs[:], mse[:], res.mhalf[:, 0:TILES], ALU.pow).then_inc(r_ok, 1)

        @b.vector
        def _(dve):
            dve.wait_ge(ssq, TILES)
            dve.tensor_scalar(mse[:], ms[:], 1.0 / D, EPS, ALU.mult, ALU.add).then_inc(m_ok, 1)
            dve.wait_ge(r_ok, 1)
            dve.wait_ge(w_in_, 16)
            for t in range(TILES):
                dve.scalar_tensor_tensor(out=y[:, t, :], in0=X[:, t, :], scalar=rs[:, t:t + 1], in1=wb[:],
                                         op0=ALU.mult, op1=ALU.mult).then_inc(y_ok, 1)


class Resident:
    pass


class Slots:
    pass


def build(nc, a, outs):
    Stage.before = []
    res = Resident()
    with ExitStack() as ctx:
        ctx.enter_context(nc.allow_non_contiguous_dma(reason="per-partition vectors of a few values"))

        def sb(name, shape, dtype=F32):
            return ctx.enter_context(nc.sbuf_tensor(name, shape, dtype))

        res.X = sb("residual", [P, TILES, D])
        res.AH = sb("act_hi", [P, KC, TOK], F32R)
        res.AL = sb("act_lo", [P, KC, TOK], F32R)
        res.ident = sb("identity", [P, P])
        res.ones = sb("ones", [P, P])
        res.iota = sb("iota", [P, P])
        res.mhalf = sb("minus_half", [P, 32])
        res.PS = ctx.enter_context(nc.psum_tensor("banks", [P, 8, 512], F32))
        res.c_rot, res.c_dec, res.c_tri, res.c_lm = a["c_rot"], a["c_dec"], a["c_tri"], a["c_lm"]
        res.gates = nc.dram_tensor("dense_gates", [NKEYS, NKEYS, TOK], F32, kind="Internal").ap()

        with Stage(nc, "load") as st:
            x_in = st.sem("loaded")
            b = st.block()

            @b.sync
            def _(sp):
                for t in range(TILES):
                    src = a["x_prompt"] if t < 2 else a["x_sample"]
                    sp.dma_start(res.X[:, t, :], src[0, (t % 2) * P:(t % 2 + 1) * P, :]).then_inc(x_in, 16)
                sp.dma_start(res.ident[:], a["c_ident"]).then_inc(x_in, 16)
                sp.dma_start(res.iota[:], a["c_iota"].partition_broadcast(P)).then_inc(x_in, 16)
                sp.wait_ge(x_in, 16 * (TILES + 2))

            @b.gpsimd
            def _(pool):
                pool.memset(res.mhalf[:], -0.5)
                pool.memset(res.ones[:], 1.0)

        mems = [(a["mem_prompt"] if t < 2 else a["mem_sample"])[0, (t % 2) * P:(t % 2 + 1) * P, :] for t in range(TILES)]

        def layers(l):
            def of(name):
                return a[name][l]

            with ExitStack() as mix:
                SG = mix.enter_context(nc.sbuf_tensor("gate_rows", [P, 2, HEADS, TOK], F32))
                raw = mix.enter_context(nc.sbuf_tensor("delta_rows", [P, 3, HEADS, TOK], F32))
                small = mix.enter_context(nc.sbuf_tensor("small", [P, TILES, 16], F32))
                gates = mix.enter_context(nc.sbuf_tensor("delta_gates", [P, 2, TILES, 8], F32))
                O = mix.enter_context(nc.sbuf_tensor("mixer_out", [P, TILES, HEADS, P], F32))
                w_in = of("w_in")
                with ExitStack() as rt:
                    tok = rt.enter_context(nc.sbuf_tensor("ret_rows", [P, 3, TILES, CHUNK], F32))
                    cos_sin = rt.enter_context(nc.sbuf_tensor("cos_sin", [P, 2, 2, 64], F32))
                    decay = rt.enter_context(nc.sbuf_tensor("decay", [P, HEADS, 2, SEQ], F32))
                    with Stage(nc, "win") as st:
                        b = st.block()
                        p = Part(st, "project")
                        ws = Weights(p)
                        norm_part(Part(st, "norm"), b, res, res.X, of("norm_mix"), ws)
                        project_part(p, b, res, ws, w_in, [
                            (3, 0, True, lambda j, t: one(tok[:, bass.ds(j, 1), t, :])),
                            (1, 3 * CHUNK, False, lambda j, c: SG[:, 0, c, :]),
                            (3, 4 * CHUNK, False, lambda j, c: one(raw[:, bass.ds(j, 1), c, :])),
                            (1, 7 * CHUNK, False, lambda j, c: SG[:, 1, c, :]),
                        ], tail=(w_in, 8 * CHUNK, small[:]))
                        load_part(Part(st, "tables"), b, (cos_sin[:], res.c_rot), (decay[:], res.c_dec))
                    retention_conv_stage(nc, res, cos_sin, decay, tok, O, of("gdn_conv"), raw, small, gates,
                                         of("gdn_a_log").rearrange("d h -> (d h)"),
                                         of("gdn_dt_bias").rearrange("d h -> (d h)"))
                with ExitStack() as dl:
                    tokm = dl.enter_context(nc.sbuf_tensor("delta_tokens", [P, TILES, 3, CHUNK], F32))
                    tri = dl.enter_context(nc.sbuf_tensor("tri", [P, DIRS, P], F32))
                    level_masks = dl.enter_context(nc.sbuf_tensor("level_masks", [P, DIRS, LEVELS, P], F32))
                    merge_unit_stage(nc, res, raw, tokm, O, of("ret_norm"), SG, (tri[:], res.c_tri), (level_masks[:], res.c_lm))
                    delta_stage(nc, res, tri, level_masks, raw, tokm, gates, O)
                with Stage(nc, "wout") as st:
                    b = st.block()
                    p = Part(st, "project")
                    ws = Weights(p)
                    merge_part(Part(st, "merge"), b, res, O, of("gdn_norm"), SG[:, 1], ws)
                    project_part(p, b, res, ws, of("w_out"), [(2, 0, True, None)])
            with ExitStack() as xa:
                kT = xa.enter_context(nc.sbuf_tensor("mem_keys", [P, KC, TOK], F32))
                v = xa.enter_context(nc.sbuf_tensor("mem_values", [P, TILES, D], F32))
                qT = xa.enter_context(nc.sbuf_tensor("xa_queries", [P, KC, TOK], F32))
                with Stage(nc, "wkv") as st:
                    b = st.block()
                    p = Part(st, "project")
                    ws = Weights(p)
                    norm_part(Part(st, "norm"), b, res, None, of("norm_mem"), ws, mems)
                    project_part(p, b, res, ws, of("w_xkv"), [
                        (2, 0, False, lambda j, c: one(kT[:, bass.ds(j * 4 + c, 1), :])),
                        (2, 2 * CHUNK, True, lambda j, t: v[:, t, bass.ds(j * CHUNK, CHUNK)]),
                    ])
                with Stage(nc, "wxq") as st:
                    b = st.block()
                    p = Part(st, "project")
                    ws = Weights(p)
                    norm_part(Part(st, "norm"), b, res, res.X, of("norm_xa"), ws)
                    project_part(p, b, res, ws, of("w_xq"),
                                 [(2, 0, False, lambda j, c: one(qT[:, bass.ds(j * 4 + c, 1), :]))])
                with Stage(nc, "wxo") as st:
                    b = st.block()
                    p = Part(st, "project")
                    ws = Weights(p)
                    attention_part(Part(st, "attend"), b, res, qT, kT, v, ws)
                    project_part(p, b, res, ws, of("w_xo"), [(2, 0, True, None)])
            with ExitStack() as pf:
                SL = Slots()
                SL.idx = pf.enter_context(nc.sbuf_tensor("slot_keys", [P, 2, TOK], F32))
                SL.g = pf.enter_context(nc.sbuf_tensor("slot_gates", [P, TOK], F32))
                with ExitStack() as pq:
                    qT = pq.enter_context(nc.sbuf_tensor("peer_queries", [P, 2 * PH, TOK], F32))
                    kraw = pq.enter_context(nc.sbuf_tensor("sub_keys", [P, 2 * PH, P], F32))
                    with Stage(nc, "wpq") as st:
                        b = st.block()
                        p = Part(st, "project")
                        ws = Weights(p)
                        norm_part(Part(st, "norm"), b, res, res.X, of("norm_ffn"), ws)
                        project_part(p, b, res, ws, of("peer_wq"),
                                     [(4, 0, False, lambda j, c: one(qT[:, bass.ds(j * 4 + c, 1), :]))])
                        load_part(Part(st, "keys"), b, *[
                            (kraw[:, 4 * i:4 * i + 4, :],
                             of("peer_keys")[2 * i:2 * i + 2].rearrange("h c n d -> n (h c) d")) for i in range(PH // 2)])
                    select_stage(nc, res, qT, kraw, SL)
                last_block = pf.enter_context(nc.sbuf_tensor("last_gates", [P, P, BLK], F32))
                gate_stage(nc, res, SL, last_block)
                expert_stage(nc, res, of("peer_u"), of("peer_v"), last_block)

        with nc.Fori(0, DEPTH) as l:
            layers(l)
            with Stage(nc, "turn") as st:
                st.block()
        final_stage(nc, res, a["norm_final"], outs)
        with Stage(nc, "end") as st:
            st.block()


def one(ap):
    return ap.squeeze(1) if len(ap.shape) == 3 else ap


def tables():
    f = np.float32
    inv = (np.float32(10000.0) ** (-np.arange(0, P, 2, dtype=f) / f(P))).astype(f)
    ang = (np.arange(SEQ, dtype=f)[:, None] * inv[None, :]).astype(f).astype(np.float64)
    rot = np.stack([np.cos(ang), np.sin(ang)], 1).astype(f).reshape(2, P, 2, 64).transpose(1, 0, 2, 3)
    i = np.arange(SEQ)
    diff = (i[None, :] - i[:, None]).astype(np.float64)
    dec = np.zeros((HEADS, SEQ, SEQ))
    for h in range(HEADS):
        fwd, bwd = np.log1p(-2.0 ** (-5.0 - h)), np.log1p(-2.0 ** (-5.5 - h))
        dec[h] = np.where(diff >= 0, np.exp(fwd * np.abs(diff)), np.exp(bwd * np.abs(diff))) * P ** -0.5
    dec = dec.reshape(HEADS, 2, P, SEQ).transpose(2, 0, 1, 3).astype(f)
    j, k = np.arange(P)[:, None], np.arange(P)[None, :]
    tri = np.stack([j <= k, j >= k], 1).astype(f)
    lm = np.zeros((P, DIRS, LEVELS, P), f)
    for lev in range(LEVELS):
        s = 1 << lev
        pair = (j // (2 * s)) == (k // (2 * s))
        lm[:, 0, lev] = pair & (j // s % 2 == 0) & (k // s % 2 == 1)
        lm[:, 1, lev] = pair & (j // s % 2 == 1) & (k // s % 2 == 0)
    return {"c_rot": np.ascontiguousarray(rot), "c_dec": np.ascontiguousarray(dec), "c_tri": tri, "c_lm": lm,
            "c_ident": np.eye(P, dtype=f), "c_iota": np.arange(P, dtype=f)}


_INS = ["x_prompt", "x_sample", "mem_prompt", "mem_sample", "norm_mix", "w_in", "ret_norm", "gdn_conv", "gdn_a_log",
        "gdn_dt_bias", "gdn_norm", "w_out", "norm_xa", "norm_mem", "w_xq", "w_xkv", "w_xo", "norm_ffn", "peer_wq",
        "peer_keys", "peer_u", "peer_v", "norm_final"]


def kernel(**inputs):
    import concourse.bacc as _bacc
    from concourse.bass_utils import run_bass_kernel_spmd as _run

    nc = _bacc.Bacc("TRN2", target_bir_lowering=False, num_devices=1)
    arrays, args = {}, {}
    for name, x in [(n, np.ascontiguousarray(inputs[n])) for n in _INS] + list(tables().items()):
        arrays[f"in_{name}"] = x
        args[name] = nc.dram_tensor(f"in_{name}", x.shape, F32, kind="ExternalInput").ap()
    outs = [nc.dram_tensor(f"out_{i}", [1, SEQ, D], F32, kind="ExternalOutput").ap() for i in range(N_SEQ)]
    build(nc, args, outs)
    r = _run(nc, [arrays], core_ids=[0])
    return tuple(r.results[0][f"out_{i}"] for i in range(N_SEQ))
```
